# Optimizing a Trainium2 kernel written in Bass

```python
import jax, jax.numpy as jnp
from jax import lax
import numpy as np

D_MODEL = 2048
BATCH = 1
SEQ = 256
DEPTH = 1
DEC_BATCH = 1
DEC_SEQ = 1024
PAST_LEN = 512

GRID_W = 64
N_HEADS = 8
N_KV_HEADS = 2
HEAD_DIM = 128
Q_PER_KV = N_HEADS // N_KV_HEADS
ATTN_WIDTH = N_HEADS * HEAD_DIM
KV_WIDTH = N_KV_HEADS * HEAD_DIM
POOL_WIDTH = D_MODEL - ATTN_WIDTH
POOL_SIZES = (2, 4, 8, 16)
POOL_GROUP = POOL_WIDTH // len(POOL_SIZES)
IN_WIDTH = ATTN_WIDTH + 2 * KV_WIDTH + POOL_WIDTH
WINDOW = 128
BLOCK = 128
ROPE_THETA = 10000.0
ROPE_FREQS = HEAD_DIM // 4
N_EXPERTS = 16
EC_FACTOR = 2
D_EXPERT = 1024
N_MOD = 6
EPS = 1e-6
NEG = -1e30

kernel_name = 'hymba_pool_ec_diffusion_step'

def rmsnorm(x, g):
    xf = x.astype(jnp.float32)
    y = xf * lax.rsqrt(jnp.mean(xf * xf, axis=-1, keepdims=True) + EPS)
    return (y * g.astype(jnp.float32)).astype(x.dtype)

def modulation(cond, w_ada, b_ada):
    m = jax.nn.silu(cond) @ w_ada + b_ada
    return jnp.split(m[:, None, :], N_MOD, axis=-1)

def modulate(h, shift, scale):
    return h * (1 + scale) + shift

def split_projection(h, w_in):
    u = h @ w_in
    b, n = h.shape[0], h.shape[1]
    q = u[..., :ATTN_WIDTH].reshape(b, n, N_HEADS, HEAD_DIM)
    k = u[..., ATTN_WIDTH:ATTN_WIDTH + KV_WIDTH].reshape(b, n, N_KV_HEADS, HEAD_DIM)
    v = u[..., ATTN_WIDTH + KV_WIDTH:ATTN_WIDTH + 2 * KV_WIDTH].reshape(b, n, N_KV_HEADS, HEAD_DIM)
    p = u[..., ATTN_WIDTH + 2 * KV_WIDTH:]
    return q, k, v, p

def axial_cos_sin(n):
    rows = n // GRID_W
    row = jnp.repeat(jnp.arange(rows, dtype=jnp.float32), GRID_W)
    col = jnp.tile(jnp.arange(GRID_W, dtype=jnp.float32), rows)
    inv = ROPE_THETA ** (-jnp.arange(ROPE_FREQS, dtype=jnp.float32) / ROPE_FREQS)
    ang = jnp.stack([row[:, None] * inv, col[:, None] * inv], axis=1)
    return jnp.cos(ang), jnp.sin(ang)

def apply_axial_rope(x, cos, sin):
    b, n, h, _ = x.shape
    xr = x.astype(jnp.float32).reshape(b, n, h, 2, 2, ROPE_FREQS)
    x1, x2 = xr[..., 0, :], xr[..., 1, :]
    c = cos[None, :, None, :, :]
    s = sin[None, :, None, :, :]
    out = jnp.stack([x1 * c - x2 * s, x1 * s + x2 * c], axis=-2)
    return out.reshape(b, n, h, HEAD_DIM).astype(x.dtype)

def sink_column(sink, lead_shape):
    return jnp.broadcast_to(sink.astype(jnp.float32).reshape(N_KV_HEADS, Q_PER_KV)[:, :, None, None], lead_shape + (1,)) if False else None

def context_attention(q, k, v, sink):
    b, l = q.shape[0], q.shape[1]
    qg = q.reshape(b, l, N_KV_HEADS, Q_PER_KV, HEAD_DIM)
    s = jnp.einsum('blkgd,bmkd->bkglm', qg, k).astype(jnp.float32) * (HEAD_DIM ** -0.5)
    sk = jnp.broadcast_to(sink.astype(jnp.float32).reshape(1, N_KV_HEADS, Q_PER_KV, 1, 1), s.shape[:-1] + (1,))
    p = jax.nn.softmax(jnp.concatenate([s, sk], axis=-1), axis=-1)
    out = jnp.einsum('bkglm,bmkd->blkgd', p[..., :l].astype(v.dtype), v)
    return out.reshape(b, l, ATTN_WIDTH)

def latent_attention(q, k, v, k_ctx, v_ctx, sink):
    b, n = q.shape[0], q.shape[1]
    l = k_ctx.shape[1]
    nb = n // BLOCK
    qb = q.reshape(b, nb, BLOCK, N_KV_HEADS, Q_PER_KV, HEAD_DIM)
    pad = ((0, 0), (BLOCK, BLOCK), (0, 0), (0, 0))
    kp = jnp.pad(k, pad).reshape(b, nb + 2, BLOCK, N_KV_HEADS, HEAD_DIM)
    vp = jnp.pad(v, pad).reshape(b, nb + 2, BLOCK, N_KV_HEADS, HEAD_DIM)
    kband = jnp.concatenate([kp[:, :-2], kp[:, 1:-1], kp[:, 2:]], axis=2)
    vband = jnp.concatenate([vp[:, :-2], vp[:, 1:-1], vp[:, 2:]], axis=2)
    scale = HEAD_DIM ** -0.5
    s_loc = jnp.einsum('bnqkgd,bnskd->bnkgqs', qb, kband).astype(jnp.float32) * scale
    blk = jnp.arange(nb)[:, None, None]
    qpos = blk * BLOCK + jnp.arange(BLOCK)[None, :, None]
    kpos = (blk - 1) * BLOCK + jnp.arange(3 * BLOCK)[None, None, :]
    mask = (jnp.abs(kpos - qpos) <= WINDOW) & (kpos >= 0) & (kpos < n)
    s_loc = jnp.where(mask[None, :, None, None, :, :], s_loc, NEG)
    s_ctx = jnp.einsum('bnqkgd,blkd->bnkgql', qb, k_ctx).astype(jnp.float32) * scale
    sk = jnp.broadcast_to(sink.astype(jnp.float32).reshape(1, 1, N_KV_HEADS, Q_PER_KV, 1, 1), s_loc.shape[:-1] + (1,))
    p = jax.nn.softmax(jnp.concatenate([s_loc, s_ctx, sk], axis=-1), axis=-1)
    p_loc = p[..., :3 * BLOCK].astype(v.dtype)
    p_ctx = p[..., 3 * BLOCK:3 * BLOCK + l].astype(v.dtype)
    out = (jnp.einsum('bnkgqs,bnskd->bnqkgd', p_loc, vband)
           + jnp.einsum('bnkgql,blkd->bnqkgd', p_ctx, v_ctx))
    return out.reshape(b, n, ATTN_WIDTH)

def pool_mixer(p, pool_w, pool_scale):
    b, n, _ = p.shape
    t = jnp.arange(n)
    outs = []
    for g, w in enumerate(POOL_SIZES):
        pg = p[..., g * POOL_GROUP:(g + 1) * POOL_GROUP]
        cs = jnp.concatenate([jnp.zeros((b, 1, POOL_GROUP), jnp.float32),
                              jnp.cumsum(pg.astype(jnp.float32), axis=1)], axis=1)
        lo = jnp.clip(t - w // 2, 0, n)
        hi = jnp.clip(t + w - w // 2, 0, n)
        cnt = (hi - lo).astype(jnp.float32)
        mean = (jnp.take(cs, hi, axis=1) - jnp.take(cs, lo, axis=1)) / cnt[None, :, None]
        mixed = (mean - pg.astype(jnp.float32)).astype(p.dtype)
        outs.append(mixed @ pool_w[g])
    return jnp.concatenate(outs, axis=-1) * pool_scale

def expert_choice_ffn(h, w_router, w_gate, w_up, w_down):
    shp = h.shape
    xt = h.reshape(-1, shp[-1])
    cap = EC_FACTOR * xt.shape[0] // N_EXPERTS
    affin = jax.nn.softmax((xt @ w_router).astype(jnp.float32), axis=-1)
    gates, idx = lax.top_k(affin.T, cap)
    xs = xt[idx]
    hid = jax.nn.silu(jnp.einsum('ecd,edf->ecf', xs, w_gate)) * jnp.einsum('ecd,edf->ecf', xs, w_up)
    y = jnp.einsum('ecf,efd->ecd', hid, w_down) * gates[..., None].astype(xt.dtype)
    out = jnp.zeros_like(xt).at[idx.reshape(-1)].add(y.reshape(-1, shp[-1]))
    return out.reshape(shp)

def setup_inputs(seed: int = 0) -> dict:
    key = jax.random.key(seed)
    ks = jax.random.split(key, 20)
    f32 = jnp.float32
    D, E, F = D_MODEL, N_EXPERTS, D_EXPERT
    nrm = lambda k, s, sc: jax.random.normal(k, s, f32) * sc
    return {
        'x_prompt': nrm(ks[0], (BATCH, SEQ, D), 1.0),
        'x_sample': nrm(ks[1], (DEC_BATCH, DEC_SEQ, D), 1.0),
        'c': nrm(ks[2], (DEC_BATCH, D), 1.0),
        'cache_k': nrm(ks[3], (DEC_BATCH, DEPTH, PAST_LEN, N_KV_HEADS, HEAD_DIM), 1.0),
        'cache_v': nrm(ks[4], (DEC_BATCH, DEPTH, PAST_LEN, N_KV_HEADS, HEAD_DIM), 1.0),
        'c_ctx': nrm(ks[5], (D,), 1.0),
        'w_ada': nrm(ks[6], (DEPTH, D, N_MOD * D), D ** -0.5),
        'b_ada': nrm(ks[7], (DEPTH, N_MOD * D), 0.01),
        'norm_mix': 1.0 + nrm(ks[8], (DEPTH, D), 0.01),
        'w_in': nrm(ks[9], (DEPTH, D, IN_WIDTH), D ** -0.5),
        'sink_logits': nrm(ks[10], (DEPTH, N_HEADS), 1.0),
        'pool_w': nrm(ks[11], (DEPTH, len(POOL_SIZES), POOL_GROUP, POOL_GROUP), POOL_GROUP ** -0.5),
        'pool_scale': 1.0 + nrm(ks[12], (DEPTH, POOL_WIDTH), 0.02),
        'w_out': nrm(ks[13], (DEPTH, D, D), D ** -0.5),
        'norm_ffn': 1.0 + nrm(ks[14], (DEPTH, D), 0.01),
        'w_router': nrm(ks[15], (DEPTH, D, E), D ** -0.5),
        'w_gate': nrm(ks[16], (DEPTH, E, D, F), D ** -0.5),
        'w_up': nrm(ks[17], (DEPTH, E, D, F), D ** -0.5),
        'w_down': nrm(ks[18], (DEPTH, E, F, D), F ** -0.5),
        'norm_final': 1.0 + nrm(ks[19], (D,), 0.01),
    }

def reference(x_prompt, x_sample, c, cache_k, cache_v, c_ctx, w_ada, b_ada, norm_mix, w_in,
              sink_logits, pool_w, pool_scale, w_out, norm_ffn, w_router, w_gate, w_up,
              w_down, norm_final):
    xp = x_prompt
    xs = x_sample
    n_lat = xs.shape[1]
    cos, sin = axial_cos_sin(n_lat)
    new_k = []
    new_v = []
    for l in range(DEPTH):
        sh1, sc1, g1, sh2, sc2, g2 = modulation(c_ctx[None, :], w_ada[l], b_ada[l])
        h = modulate(rmsnorm(xp, norm_mix[l]), sh1, sc1)
        q, k, v, p = split_projection(h, w_in[l])
        new_k.append(k)
        new_v.append(v)
        mix = jnp.concatenate([context_attention(q, k, v, sink_logits[l]),
                               pool_mixer(p, pool_w[l], pool_scale[l])], axis=-1) @ w_out[l]
        xp = xp + g1 * mix
        h = modulate(rmsnorm(xp, norm_ffn[l]), sh2, sc2)
        xp = xp + g2 * expert_choice_ffn(h, w_router[l], w_gate[l], w_up[l], w_down[l])

        sh1, sc1, g1, sh2, sc2, g2 = modulation(c, w_ada[l], b_ada[l])
        h = modulate(rmsnorm(xs, norm_mix[l]), sh1, sc1)
        q, k, v, p = split_projection(h, w_in[l])
        q = apply_axial_rope(q, cos, sin)
        k = apply_axial_rope(k, cos, sin)
        attn = latent_attention(q, k, v, cache_k[:, l], cache_v[:, l], sink_logits[l])
        mix = jnp.concatenate([attn, pool_mixer(p, pool_w[l], pool_scale[l])], axis=-1) @ w_out[l]
        xs = xs + g1 * mix
        h = modulate(rmsnorm(xs, norm_ffn[l]), sh2, sc2)
        xs = xs + g2 * expert_choice_ffn(h, w_router[l], w_gate[l], w_up[l], w_down[l])

    y_prompt = rmsnorm(xp, norm_final)
    y_sample = rmsnorm(xs, norm_final)
    state_k = jnp.stack(new_k, axis=1)
    state_v = jnp.stack(new_v, axis=1)
    return (y_prompt, y_sample, state_k, state_v)


_drawn_inputs = setup_inputs


def setup_inputs(seed=0):
    import zlib

    import numpy as np

    out = dict(_drawn_inputs(seed))
    spreads = {}
    factors = {'b_ada': 3.163,
     'norm_mix': 6.42,
     'sink_logits': 8.0,
     'pool_scale': 3.598,
     'norm_ffn': 4.623,
     'norm_final': 5.817}
    for name, (base, spread) in spreads.items():
        noise = np.random.default_rng([zlib.crc32(name.encode()), seed]).standard_normal(out[name].shape)
        drawn = base * np.exp(spread * noise) if base else spread * noise
        out[name] = __import__('jax').numpy.asarray(drawn.astype(out[name].dtype))
    for name, factor in factors.items():
        out[name] = (out[name] * factor).astype(out[name].dtype)
    return out
```

```python
from contextlib import ExitStack

import numpy as np

import concourse.bass as bass
from concourse import mybir

F32 = mybir.dt.float32
F32R = mybir.dt.float32r
BF16 = mybir.dt.bfloat16
U32 = mybir.dt.uint32
ACT = mybir.ActivationFunctionType
ALU = mybir.AluOpType
AXX = mybir.AxisListType.X

P = 128
D = 2048
KT = D // P
NS = 1024
NP_ = 256
ST = NS // P
TT = (NS + NP_) // P
CH = [(0, 4, 0), (4, 4, 0), (8, 2, 1)]
PAST = 512
NH, NKV, HD = 8, 2, 128
AW = NH * HD
KW = NKV * HD
PW = D - AW
INW = AW + 2 * KW + PW
POOLS = (2, 4, 8, 16)
PG = PW // 4
HALO = 8
NE = 16
FE = 1024
CAP_S, CAP_P = 2 * NS // NE, 2 * NP_ // NE
CAP = CAP_S + CAP_P
EPS = 1e-6
NEG = -1e30
SCALE = HD ** -0.5
CC = 512
KG = 4
NRAW = 3
NSPLIT = 3
NRING = 12
NADA = 6 * D // CC
ADA_A = 2 * D // CC
PIECES_E = 2 * (D // P // KG) * (FE // CC) + (FE // P // KG) * (D // CC)


def build_units():
    units = []
    for tc, (t0, nt, cond) in enumerate(CH):
        nk = 9 if cond == 0 else 2
        nu = (2 * nk + 7) // 8
        for u in range(nu):
            units.append((tc, "K", 0, u))
        per = 4 // nt
        for b in range(nt):
            units.append((tc, "Q", b, 0))
            for h in range(NH):
                units.append((tc, "H", b, h))
            for g in range(b * per, b * per + per):
                units.append((tc, "M", b, g))
    heads, copies, nh, ncp = [], [], 0, 0
    for u in units:
        heads.append(nh)
        copies.append(ncp)
        if u[1] == "H":
            nh += 1
        else:
            ncp += 1
    return units, heads, copies


UNITS, HEADS_BEFORE, COPIES_BEFORE = build_units()


def local_blocks(tc, b):
    t0, nt, cond = CH[tc]
    if cond:
        return [0, 1], False, False
    q = t0 + b
    first = max(0, t0 - 1)
    ks = [k for k in (q - 1, q, q + 1) if 0 <= k < ST]
    return [k - first for k in ks], q - 1 >= 0, q + 1 < ST


def hybrid_backbone_step(nc, t, o):
    ctx = ExitStack()
    with ctx:
        def sem(name):
            return ctx.enter_context(nc.semaphore(name))

        def dram(name, shape):
            return nc.dram_tensor(name, shape, F32, kind="Internal").ap()

        mod_d = dram("mod_rows", [2, 6 * D])
        qkv_d = dram("qkv_rows", [NS + NP_, AW + 2 * KW])
        pool_d = dram("pool_cols", [PW, NS + NP_])
        res_s, res_p = dram("resid_s", [NS, D]), dram("resid_p", [NP_, D])
        h2_s, h2_p = dram("h2_s", [NS, D]), dram("h2_p", [NP_, D])

        xs = t["x_sample"].rearrange("b n d -> (b n) d")
        xp = t["x_prompt"].rearrange("b n d -> (b n) d")
        ys = o["y_sample"].rearrange("b n d -> (b n) d")
        yp = o["y_prompt"].rearrange("b n d -> (b n) d")
        st_k = o["state_k"].rearrange("b l n h d -> (b l n) (h d)")
        st_v = o["state_v"].rearrange("b l n h d -> (b l n) (h d)")
        ck = t["cache_k"].rearrange("b l n h d -> (b l n) (h d)")
        cv = t["cache_v"].rearrange("b l n h d -> (b l n) (h d)")
        w_ada = t["w_ada"].rearrange("l k n -> (l k) n")
        w_in = t["w_in"].rearrange("l k n -> (l k) n")
        w_out = t["w_out"].rearrange("l k n -> (l k) n")
        w_gate = t["w_gate"].rearrange("l e k n -> (l e) k n")
        w_up = t["w_up"].rearrange("l e k n -> (l e) k n")
        w_down = t["w_down"].rearrange("l e k n -> (l e) k n")

        def rows(a_s, a_p, i):
            return a_s[i * P:(i + 1) * P, :] if i < ST else a_p[(i - ST) * P:(i - ST + 1) * P, :]

        def piece(w, kg, c0):
            return w[kg * KG * P:(kg + 1) * KG * P, c0:c0 + CC].rearrange("(r p) n -> p r n", p=P)

        pieces = [piece(w_ada, kg, a * CC) for a in range(ADA_A) for kg in range(4)]
        n_ada = ADA_A
        for tc in range(3):
            for cc in range(5):
                pieces += [piece(w_in, kg, cc * CC) for kg in range(4)]
                pieces += [piece(w_ada, kg, n_ada * CC) for kg in range(4)]
                n_ada += 1
        pieces += [piece(w_ada, kg, n_ada * CC) for kg in range(4)]
        D0 = len(pieces)
        for tc in range(3):
            for cc in range(4):
                pieces += [piece(w_out, kg, cc * CC) for kg in range(4)]

        PS = ctx.enter_context(nc.psum_tensor("PS", [P, 8, 512], F32))

        def keep(name, shape, dt=F32):
            return ctx.enter_context(nc.sbuf_tensor(name, shape, dt))

        ident = keep("ident", [P, P])
        maskL = keep("maskL", [P, P])
        maskR = keep("maskR", [P, P])
        sel = keep("sel", [5, 2])
        sinks = keep("sinks", [P, 2, NH])
        pscale = keep("pscale", [P, PW // P])
        wr = keep("wr", [P, KT, NE])
        ss = keep("ss", [P, 3 * TT])
        st = keep("st", [P, 8])
        sm = keep("sm", [P, 2, 8])
        aff = keep("aff", [P, TT, NE])

        mix = ExitStack()

        def mixt(name, shape, dt):
            return mix.enter_context(nc.sbuf_tensor(name, shape, dt))

        raw = mixt("raw", [P, NRAW, KG, CC], F32)
        whi = mixt("whi", [P, NSPLIT, KG, CC], F32R)
        wlo = mixt("wlo", [P, NSPLIT, KG, CC], F32R)
        ahi = mixt("ahi", [P, KT, 512], F32R)
        alo = mixt("alo", [P, KT, 512], F32R)
        off = [0]
        arena = [None]

        def carve(*shape):
            n = int(np.prod(shape))
            v = arena[0][:, off[0]:off[0] + n]
            off[0] += n
            assert off[0] <= arena[0].shape[1], off[0]
            if len(shape) == 2:
                v = v.rearrange("p (a b) -> p a b", a=shape[0])
            if len(shape) == 3:
                v = v.rearrange("p (a b c) -> p a b c", a=shape[0], b=shape[1])
            return v

        early = ExitStack()
        arena[0] = early.enter_context(nc.sbuf_tensor("arena_ab", [P, 58 * 256], F32))
        cond_s = early.enter_context(nc.sbuf_tensor("cond_s", [P, KT, P], F32R))
        xb = carve(2, D)
        tabA, tabS = carve(D), carve(D)
        stg = carve(4, 512)
        rt = carve(4, 256)
        rtab = carve(2, 256)
        junk = carve(D // 2).bitcast(BF16)
        arow = carve(2, 512)
        mrow = carve(2, 512)
        cond_r = junk.bitcast(F32)[:, 0:P]
        cond_f = junk.bitcast(F32)[:, P:P + 32]
        early.close()
        arena[0] = mixt("arena_cd", [P, 66 * 256], F32)
        off[0] = 0
        kT = carve(2 * 9 * P)
        vv = carve(9, KW)
        qq = carve(AW)
        qT = carve(NH, P)
        pt0 = off[0]
        pp = carve(2, 7 * P)
        pT = carve(2, 7, P)
        ktm = arena[0][:, pt0:pt0 + 9 * KW].rearrange("p (a b) -> p a b", a=9)
        pin = carve(2, 512 + 2 * HALO)
        pa = carve(2, 512 + 2 * HALO)
        pb = carve(2, 512 + 2 * HALO)
        mixT = carve(2, 512)
        rcnt = carve(512)
        pw = carve(2, PG)
        off[0] = 0
        tabG, tabA2, tabS2 = carve(D), carve(D), carve(D)
        x1 = carve(4, D)
        h2T = carve(4, P)
        h2b = carve(D)
        mix.close()

        ring = keep("ring", [P, NRING, KG, CC])
        xT = keep("xT", [P, KT, CAP])
        hid = keep("hid", [P, FE // P, CAP])
        hg = keep("hg", [P, 2, KG * CAP])
        yT = keep("yT", [P, 2, KG * CAP])
        g_s, g_p = keep("g_s", [P, D]), keep("g_p", [CAP_P, D])
        y_s, y_p = keep("y_s", [P, D]), keep("y_p", [CAP_P, D])
        g2_s, g2_p = keep("g2_s", [P, D]), keep("g2_p", [CAP_P, D])
        affT = keep("affT", [NE, NS + NP_])
        top = keep("top", [NE, CAP])
        topi = keep("topi", [NE, CAP], U32)
        topf = keep("topf", [NE, CAP])
        gate_s, gate_p = keep("gate_s", [P, NE]), keep("gate_p", [CAP_P, NE])
        idx_s, idx_p = keep("idx_s", [P, NE + 1], U32), keep("idx_p", [CAP_P, NE + 1], U32)
        ig_s, ig_p = keep("ig_s", [P, 1], U32), keep("ig_p", [CAP_P, 1], U32)
        ic_s, ic_p = keep("ic_s", [P, 1], U32), keep("ic_p", [CAP_P, 1], U32)

        raw_in = [sem(f"raw_in{i}") for i in range(NRAW)]
        hi_ok, lo_ok, used = sem("hi_ok"), sem("lo_ok"), sem("used")
        consts_in, cond_in, zero_ok = sem("consts_in"), sem("cond_in"), sem("zero_ok")
        cond_tr, cond_f_ok, cond_hi, cond_lo = sem("cond_tr"), sem("cond_f_ok"), sem("cond_hi"), sem("cond_lo")
        arow_ok, sel_ok, mrow_ok = sem("arow_ok"), sem("sel_ok"), sem("mrow_ok")
        brow_in = [sem(f"brow_in{i}") for i in range(2)]
        mod_out = [sem(f"mod_out{i}") for i in range(2)]
        tab_in, tab_ok = sem("tab_in"), sem("tab_ok")
        x_in = [sem(f"x_in{i}") for i in range(2)]
        sq_ok, root_ok, h_ok = sem("sq_ok"), sem("root_ok"), sem("h_ok")
        ms_ok = sem("ms_ok")
        h_tr, h_hi, h_lo = sem("h_tr"), sem("h_hi"), sem("h_lo")
        stg_ok, stg_out = sem("stg_ok"), sem("stg_out")
        rtab_in = sem("rtab_in")
        dve_step, pool_step = sem("dve_step"), sem("pool_step")
        kv_in, q_in, unit_pe = sem("kv_in"), sem("q_in"), sem("unit_pe")
        copied, m_hi, masked, exped, sank = sem("copied"), sem("m_hi"), sem("masked"), sem("exped"), sem("sank")
        p_ok, p_tr, pt_a, pt_v, pv_ok, o_hi, o_lo = (sem(n) for n in ("p_ok", "p_tr", "pt_a", "pt_v", "pv_ok", "o_hi", "o_lo"))
        pin_in, mixed = sem("pin_in"), sem("mixed")
        dtab_in, x1_in, dtab_ok = sem("dtab_in"), sem("x1_in"), sem("dtab_ok")
        x1_ok, x1_out, h2_ok, h2_out = (sem(n) for n in ("x1_ok", "x1_out", "h2_ok", "h2_out"))
        h2_tr, h2T_ok, lmax_ok, lexp_ok, aff_ok = (
            sem(n) for n in ("h2_tr", "h2T_ok", "lmax_ok", "lexp_ok", "aff_ok"))
        h2T_used = sem("h2T_used")
        aff_tr, affT_ok, top_ok, top_tr, gate_ok = (sem(n) for n in ("aff_tr", "affT_ok", "top_ok", "top_tr", "gate_ok"))
        ring_in = [sem(f"ring_in{i}") for i in range(NRING)]
        ring_free, silu_ok, hid_ok = sem("ring_free"), sem("silu_ok"), sem("hid_ok")
        yT_ok, x_tr, xs_ok, xp_ok, y_tr, ys_ok, yp_ok = (
            sem(n) for n in ("yT_ok", "x_tr", "xs_ok", "xp_ok", "y_tr", "ys_ok", "yp_ok"))
        gs_in, gp_in, ig_ok, ic_ok, y_free, s_out, p_out = (
            sem(n) for n in ("gs_in", "gp_in", "ig_ok", "ic_ok", "y_free", "s_out", "p_out"))
        g2_in, turn = sem("g2_in"), sem("turn")
        NF = 4
        f_in = [sem(f"f_in{i}") for i in range(NF)]
        f_out = [sem(f"f_out{i}") for i in range(NF)]
        nf_in, f_sq, f_ms, f_root, f_ok = sem("nf_in"), sem("f_sq"), sem("f_ms"), sem("f_root"), sem("f_ok")

        N_CONST = 11
        n_units = len(UNITS)
        n_heads = HEADS_BEFORE[-1] + (UNITS[-1][1] == "H")
        n_copies = COPIES_BEFORE[-1] + (UNITS[-1][1] != "H")
        unit_end = [max(k for k in range(n_units) if UNITS[k][0] == tc) + 1 for tc in range(3)]
        unit_start = [0, unit_end[0], unit_end[1]]

        def heads_by(k):
            return HEADS_BEFORE[k] if k < n_units else n_heads

        def copies_by(k):
            return COPIES_BEFORE[k] if k < n_units else n_copies

        def m_by(k):
            return sum(1 for u in UNITS[:k] if u[1] == "M")

        def kind(k):
            return UNITS[k][1] if 0 <= k < n_units else None

        def in_chunk(k, tc):
            return unit_start[tc] <= k < unit_end[tc]

        def keys(tc, b):
            loc, ml, mr = local_blocks(tc, b)
            ctx_n = 0 if CH[tc][2] else PAST // P
            return ctx_n, [ctx_n + k for k in loc], ml, mr

        def ada_pieces(a):
            return 4 * (a + 1) if a < ADA_A else (4 * ADA_A + 8 * (a - ADA_A + 1) if a < NADA - 1 else D0)

        def win_pieces(n):
            return 4 * ADA_A + 8 * n + 4

        def m_unit(n):
            return [k for k in range(n_units) if UNITS[k][1] == "M"][n]

        def staged_by(n):
            return sum((CH[c // 5][1] if c % 5 < 3 else 4) for c in range(n))

        def x1_by(tc, cc):
            return sum(4 * CH[c][1] for c in range(tc)) + (cc + 1) * CH[tc][1]

        def x_loads(i):
            n = i // 2 + 1
            if i % 2 == 0:
                n += 1 + (i >= 8)
            return n

        def p_place(cn, z):
            return z if cn else 4 * z

        kv_by = [64, 128, 160]

        stores_by = [0]
        for tc, (t0, nt, cond) in enumerate(CH):
            for cc in range(5):
                if cc < 3:
                    n = nt + (2 * nt if cond and cc == 2 else 0)
                else:
                    n = 4
                stores_by.append(stores_by[-1] + n)

        block = ctx.enter_context(nc.Block())

        @block.sync
        def _(sp):
            for g, src in enumerate(pieces):
                if g >= NRAW:
                    sp.wait_ge(lo_ok, g - NRAW + 1)
                sp.dma_start(raw[:, g % NRAW], src).then_inc(raw_in[g % NRAW], 16)
            with sp.Fori(0, NE) as e:
                n = 0
                for w, nkg, ncc in ((w_gate, 4, 1), (w_up, 4, 1), (w_gate, 4, 2), (w_up, 4, 2), (w_down, 2, 0)):
                    for c in (range(D // CC) if ncc == 0 else [ncc - 1]):
                        for kg in range(nkg):
                            sp.wait_ge(ring_free, e * PIECES_E + n + 1)
                            src = w[bass.ds(e, 1), kg * KG * P:(kg + 1) * KG * P, c * CC:(c + 1) * CC]
                            sp.dma_start(ring[:, n % NRING],
                                         src.rearrange("e (r p) n -> p (e r) n", p=P)).then_inc(ring_in[n % NRING], 16)
                            n += 1

        @block.tensor
        def _(pe):
            g = [0]

            def next_piece():
                n = g[0]
                g[0] += 1
                pe.wait_ge(lo_ok, n + 1)
                return whi[:, n % NSPLIT], wlo[:, n % NSPLIT]

            def ada(a):
                if a:
                    pe.wait_ge(arow_ok, a)
                for kg in range(4):
                    hi, lo = next_piece()
                    for r in range(KG):
                        kt = kg * KG + r
                        nc.tensor.matmul(PS[:, 7, :], cond_s[:, kt, :], hi[:, r, :], start=(kt == 0), stop=False)
                        last = nc.tensor.matmul(PS[:, 7, :], cond_s[:, kt, :], lo[:, r, :],
                                                start=False, stop=(kt == KT - 1))
                    last.then_inc(used, 1)

            def select(a):
                pe.wait_ge(arow_ok, a + 1)
                pe.wait_ge(brow_in[a % 2], 16 * (a // 2 + 1))
                if a:
                    pe.wait_ge(mrow_ok, a)
                nc.tensor.matmul(PS[0:2, 6, :], sel[0:5, :], arow[0:5, a % 2, :], start=True, stop=True).then_inc(sel_ok, 1)

            pe.wait_ge(consts_in, 16 * N_CONST)
            pe.wait_ge(cond_in, 32)
            nc.tensor.transpose(PS[:, 0, 0:32], cond_r[0:32, :], ident[0:32, 0:32]).then_inc(cond_tr, 1)
            pe.wait_ge(cond_lo, 1)
            for a in range(ADA_A):
                ada(a)
                if a:
                    select(a - 1)
            select(ADA_A - 1)

            n_ada = ADA_A
            for tc, (t0, nt, cond) in enumerate(CH):
                T = nt * P
                for j in range(nt):
                    i = t0 + j
                    pe.wait_ge(h_ok, i + 1)
                    for q in range(4):
                        n = 4 * i + q
                        if n >= 2:
                            pe.wait_ge(h_lo, n - 1)
                        for r in range(4):
                            kt = 4 * q + r
                            last = nc.tensor.transpose(PS[:, 4 + n % 2, r * P:(r + 1) * P],
                                                       xb[:, i % 2, kt * P:(kt + 1) * P], ident[:])
                        last.then_inc(h_tr, 1)
                for cc in range(5):
                    n = 5 * tc + cc
                    if n:
                        pe.wait_ge(stg_ok, staged_by(n))
                    if cc == 0:
                        pe.wait_ge(h_lo, 4 * (t0 + nt))
                    for kg in range(4):
                        hi, lo = next_piece()
                        for r in range(KG):
                            kt = kg * KG + r
                            for m in range(nt if cc < 3 else 4):
                                s = slice(m * P, (m + 1) * P)
                                if cc < 3:
                                    ops = ((ahi[:, kt, s], hi[:, r, :]), (alo[:, kt, s], hi[:, r, :]),
                                           (ahi[:, kt, s], lo[:, r, :]))
                                    out = PS[:, m, :]
                                else:
                                    ops = ((hi[:, r, s], ahi[:, kt, 0:T]), (hi[:, r, s], alo[:, kt, 0:T]),
                                           (lo[:, r, s], ahi[:, kt, 0:T]))
                                    out = PS[:, m, 0:T]
                                for z, (w, x) in enumerate(ops):
                                    last = nc.tensor.matmul(out, w, x, start=(kt == 0 and z == 0),
                                                            stop=(kt == KT - 1 and z == 2))
                        last.then_inc(used, 1)
                    if n:
                        select(n_ada - 1)
                    ada(n_ada)
                    n_ada += 1
            ada(n_ada)
            select(n_ada - 1)
            select(n_ada)

            for tc, (t0, nt, cond) in enumerate(CH):
                if tc == 0:
                    pe.wait_ge(stg_ok, staged_by(15))
                    pe.wait_ge(mrow_ok, NADA)
                else:
                    pe.wait_ge(aff_ok, t0)
                    pe.wait_ge(x1_ok, 16 * tc)
                nk = 9 if cond == 0 else 2
                for k in range(unit_start[tc], unit_end[tc] + 2):
                    if k < unit_end[tc]:
                        _, kd, b, h = UNITS[k]
                        pair = 2 * (k % 2)
                        if k - 2 >= unit_start[tc]:
                            if kind(k - 2) == "H":
                                pe.wait_ge(exped, heads_by(k - 1))
                            else:
                                pe.wait_ge(copied, copies_by(k - 1))
                        flat = PS[:, pair:pair + 2, :].rearrange("p a b -> p (a b)")
                        if kd == "K":
                            pe.wait_ge(kv_in, kv_by[tc])
                            for z in range(h * 8, min(h * 8 + 8, 2 * nk)):
                                kv, kb = z // nk, z % nk
                                last = nc.tensor.transpose(flat[:, (z % 8) * P:(z % 8 + 1) * P],
                                                           ktm[:, kb, kv * P:(kv + 1) * P], ident[:])
                        elif kd == "Q":
                            pe.wait_ge(q_in, 16 * (t0 + b + 1))
                            for z in range(NH):
                                last = nc.tensor.transpose(flat[:, z * P:(z + 1) * P], qq[:, z * P:(z + 1) * P], ident[:])
                        elif kd == "H":
                            if h == 0:
                                pe.wait_ge(copied, copies_by(k))
                            cn, loc, _, _ = keys(tc, b)
                            kv = h // (NH // NKV)
                            base = kv * nk * P
                            if cn:
                                nc.tensor.matmul(flat[:, 0:cn * P], qT[:, h, :], kT[:, base:base + cn * P],
                                                 start=True, stop=True)
                            l0 = base + loc[0] * P
                            last = nc.tensor.matmul(flat[:, cn * P:(cn + len(loc)) * P], qT[:, h, :],
                                                    kT[:, l0:l0 + len(loc) * P], start=True, stop=True)
                        else:
                            gi = 4 * tc + h
                            pe.wait_ge(mixed, gi + 1)
                            for m in range(2):
                                for z in range(2):
                                    last = nc.tensor.matmul(PS[:, pair + m, 0:nt * P], pw[:, z, m * P:(m + 1) * P],
                                                            mixT[:, z, 0:nt * P], start=(z == 0), stop=(z == 1))
                        last.then_inc(unit_pe, 1)
                    if in_chunk(k - 2, tc) and kind(k - 2) == "H":
                        _, _, b, h = UNITS[k - 2]
                        hc = heads_by(k - 2)
                        cn, loc, _, _ = keys(tc, b)
                        places = list(range(cn)) + loc
                        pe.wait_ge(pt_a, hc + 1)
                        pe.wait_ge(pt_v, hc + 1)
                        if h % 4 == 0 and hc >= 8:
                            pe.wait_ge(o_lo, hc // 4 - 1)
                        for z, kb in enumerate(places):
                            last = nc.tensor.matmul(PS[:, 6 + h // 4, (h % 4) * P:(h % 4 + 1) * P],
                                                    vv[:, kb, (h // 4) * P:(h // 4 + 1) * P], pT[:, hc % 2, z, :],
                                                    start=(z == 0), stop=(z == len(places) - 1))
                        last.then_inc(pv_ok, 1)
                    if in_chunk(k - 1, tc) and kind(k - 1) == "H":
                        _, _, b, h = UNITS[k - 1]
                        hc = heads_by(k - 1)
                        cn, loc, _, _ = keys(tc, b)
                        pe.wait_ge(p_ok, hc + 1)
                        if hc:
                            pe.wait_ge(pt_a, hc)
                            pe.wait_ge(pt_v, hc)
                        flat = PS[:, 4:6, :].rearrange("p a b -> p (a b)")
                        for z in range(cn + len(loc)):
                            c0 = p_place(cn, z) * P
                            last = nc.tensor.transpose(flat[:, c0:c0 + P], pp[:, hc % 2, z * P:(z + 1) * P], ident[:])
                        last.then_inc(p_tr, 1)

                pe.wait_ge(exped, heads_by(unit_end[tc]))
                pe.wait_ge(copied, copies_by(unit_end[tc]))
                pe.wait_ge(o_lo, heads_by(unit_end[tc]) // 4)
                pe.wait_ge(pt_a, heads_by(unit_end[tc]))
                pe.wait_ge(pt_v, heads_by(unit_end[tc]))
                for cc in range(4):
                    n = 4 * tc + cc
                    if cc >= 2:
                        pe.wait_ge(x1_ok, x1_by(tc, cc - 2))
                    for kg in range(4):
                        hi, lo = next_piece()
                        for r in range(KG):
                            kt = kg * KG + r
                            for m in range(nt):
                                s = slice(m * P, (m + 1) * P)
                                for z, (w, x) in enumerate(((ahi[:, kt, s], hi[:, r, :]), (alo[:, kt, s], hi[:, r, :]),
                                                            (ahi[:, kt, s], lo[:, r, :]))):
                                    last = nc.tensor.matmul(PS[:, 4 * (cc % 2) + m, :], w, x,
                                                            start=(kt == 0 and z == 0), stop=(kt == KT - 1 and z == 2))
                        last.then_inc(used, 1)
                pe.wait_ge(x1_ok, x1_by(tc, 3))
                for j in range(nt):
                    i = t0 + j
                    pe.wait_ge(h2_ok, i + 1)
                    for q in range(4):
                        n = 4 * i + q
                        if n:
                            pe.wait_ge(h2T_ok, n)
                        for r in range(4):
                            kt = 4 * q + r
                            last = nc.tensor.transpose(PS[:, n % 2, r * P:(r + 1) * P], h2b[:, kt * P:(kt + 1) * P], ident[:])
                        last.then_inc(h2_tr, 1)
                        pe.wait_ge(h2T_ok, n + 1)
                        if q == 0 and i:
                            pe.wait_ge(lexp_ok, i)
                        for r in range(4):
                            kt = 4 * q + r
                            last = nc.tensor.matmul(PS[:, 2, 0:NE], h2T[:, r, :], wr[:, kt, :],
                                                    start=(kt == 0), stop=(kt == KT - 1))
                        last.then_inc(h2T_used, 1)

            pe.wait_ge(aff_ok, TT)
            for i in range(TT):
                last = nc.tensor.transpose(PS[0:NE, 4 + i // 4, (i % 4) * P:(i % 4 + 1) * P], aff[:, i, :], ident[:])
            last.then_inc(aff_tr, 1)
            nc.tensor.nop().then_inc(ring_free, NRING)
            pe.wait_ge(top_ok, 1)
            nc.tensor.transpose(PS[:, 0, 0:NE], top[:, 0:CAP_S], ident[0:NE, 0:NE])
            nc.tensor.transpose(PS[:, 0, NE:2 * NE], topf[:, 0:CAP_S], ident[0:NE, 0:NE])
            nc.tensor.transpose(PS[0:CAP_P, 1, 0:NE], top[:, CAP_S:CAP], ident[0:NE, 0:NE])
            nc.tensor.transpose(PS[0:CAP_P, 1, NE:2 * NE], topf[:, CAP_S:CAP], ident[0:NE, 0:NE]).then_inc(top_tr, 1)
            pe.wait_ge(gate_ok, 1)

            def turn_tokens(j):
                for r in range(4):
                    kt = 4 * j + r
                    nc.tensor.transpose(PS[:, 4, r * P:(r + 1) * P], g_s[:, kt * P:(kt + 1) * P], ident[:])
                    last = nc.tensor.transpose(PS[:, 5, r * CAP_P:(r + 1) * CAP_P], g_p[:, kt * P:(kt + 1) * P],
                                               ident[0:CAP_P, 0:CAP_P])
                last.then_inc(x_tr, 1)

            pe.wait_ge(affT_ok, 1)
            pe.wait_ge(gs_in, 16)
            pe.wait_ge(gp_in, 16)
            for j in range(4):
                if j:
                    pe.wait_ge(xs_ok, j)
                    pe.wait_ge(xp_ok, j)
                turn_tokens(j)

            with pe.Fori(0, NE) as e:
                def banks(b, w, x, kt, last_kt):
                    for m in range(4):
                        out = PS[:, b + m // 2, (m % 2) * CAP:(m % 2 + 1) * CAP]
                        ins = nc.tensor.matmul(out, w[:, m * P:(m + 1) * P], x, start=(kt == 0 and m % 2 == 0),
                                               stop=(kt == last_kt), skip_group_check=True)
                    return ins

                n = 0

                def take(n):
                    pe.wait_ge(ring_in[n % NRING], e * (16 * PIECES_E // NRING) + 16 * (n // NRING + 1))
                    return ring[:, n % NRING]

                for half in range(2):
                    for up in range(2):
                        if half == 1 and up == 0:
                            pe.wait_ge(silu_ok, e * 2 + 1)
                        if half == 1 and up == 1:
                            pe.wait_ge(hid_ok, e * 2 + 1)
                        for kg in range(4):
                            if half == 0 and up == 0:
                                pe.wait_ge(xs_ok, e * 4 + kg + 1)
                                pe.wait_ge(xp_ok, e * 4 + kg + 1)
                            w = take(n)
                            for r in range(KG):
                                kt = kg * KG + r
                                last = banks(2 * up, w[:, r, :], xT[:, kt, :], kt, KT - 1)
                            last.then_inc(ring_free, 1)
                            n += 1
                for cc in range(4):
                    if cc == 0:
                        pe.wait_ge(silu_ok, e * 2 + 2)
                        pe.wait_ge(hid_ok, e * 2 + 1)
                    if cc == 1:
                        pe.wait_ge(hid_ok, e * 2 + 2)
                    if cc >= 2:
                        pe.wait_ge(yT_ok, e * 4 + cc - 1)
                    for kg in range(2):
                        if cc == 0 and kg == 1:
                            pe.wait_ge(hid_ok, e * 2 + 2)
                        w = take(n)
                        for r in range(KG):
                            kt = kg * KG + r
                            last = banks(2 * (cc % 2), w[:, r, :], hid[:, kt, :], kt, FE // P - 1)
                        last.then_inc(ring_free, 1)
                        n += 1
                    if cc == 0:
                        pe.wait_ge(gs_in, e * 16 + 32)
                        pe.wait_ge(gp_in, e * 16 + 32)
                    pe.wait_ge(xs_ok, e * 4 + 4 + cc)
                    pe.wait_ge(xp_ok, e * 4 + 4 + cc)
                    turn_tokens(cc)
                    for c in ([cc - 1] if cc < 3 else [2, 3]):
                        if c < 0:
                            continue
                        pe.wait_ge(yT_ok, e * 4 + c + 1)
                        if c:
                            pe.wait_ge(ys_ok, e * 4 + c)
                            pe.wait_ge(yp_ok, e * 4 + c)
                        for m in range(4):
                            y = yT[:, c % 2, m * CAP:(m + 1) * CAP]
                            nc.tensor.transpose(PS[:, 6, m * P:(m + 1) * P], y[:, 0:CAP_S], ident[:])
                            last = nc.tensor.transpose(PS[0:CAP_P, 7, m * P:(m + 1) * P], y[:, CAP_S:CAP], ident[:])
                        last.then_inc(y_tr, 1)

        @block.scalar
        def _(act):
            g = [0]
            steps = [0]

            def split_hi():
                n = g[0]
                g[0] += 1
                act.wait_ge(raw_in[n % NRAW], 16 * (n // NRAW + 1))
                if n >= NSPLIT:
                    act.wait_ge(used, n - NSPLIT + 1)
                nc.scalar.activation(whi[:, n % NSPLIT], raw[:, n % NRAW], ACT.Copy).then_inc(hi_ok, 1)

            def ada_rows(a):
                act.wait_ge(used, ada_pieces(a))
                if a >= 2:
                    act.wait_ge(sel_ok, a - 1)
                nc.scalar.activation(arow[0:4, a % 2, :], PS[0:4, 7, :], ACT.Copy).then_inc(arow_ok, 1)

            def mod_rows(a):
                act.wait_ge(sel_ok, a + 1)
                if a >= 2:
                    act.wait_ge(mod_out[a % 2], 16 * (a // 2))
                nc.scalar.activation(mrow[0:2, a % 2, :], PS[0:2, 6, :], ACT.Copy).then_inc(mrow_ok, 1)

            act.wait_ge(cond_tr, 1)
            nc.scalar.activation(cond_f, PS[:, 0, 0:32], ACT.Silu).then_inc(cond_f_ok, 1)
            act.wait_ge(cond_f_ok, 1)
            act.wait_ge(zero_ok, 1)
            cf = cond_f.rearrange("p (c t) -> p t c", c=2)
            nc.scalar.activation(cond_s[:, :, 0:2], cf, ACT.Copy).then_inc(cond_hi, 1)
            for a in range(ADA_A):
                for kg in range(4):
                    split_hi()
                    if kg == 1 and a:
                        ada_rows(a - 1)
                        if a > 1:
                            mod_rows(a - 2)
            ada_rows(ADA_A - 1)
            mod_rows(ADA_A - 2)
            mod_rows(ADA_A - 1)

            n_ada = ADA_A

            def stage(tc, cc):
                nt = CH[tc][1]
                act.wait_ge(used, win_pieces(5 * tc + cc))
                if tc or cc:
                    act.wait_ge(stg_out, 16 * stores_by[5 * tc + cc])
                for m in range(nt if cc < 3 else 4):
                    w = 512 if cc < 3 else nt * P
                    nc.scalar.activation(stg[:, m, 0:w], PS[:, m, 0:w], ACT.Copy).then_inc(stg_ok, 1)

            for tc, (t0, nt, cond) in enumerate(CH):
                for j in range(nt):
                    i = t0 + j
                    act.wait_ge(x_in[i % 2], 16 * x_loads(i))
                    if i:
                        act.wait_ge(sq_ok, i)
                    nc.scalar.activation(junk, xb[:, i % 2, :], ACT.Square, accum_out=ss[:, i:i + 1]).then_inc(sq_ok, 1)
                    act.wait_ge(ms_ok, i + 1)
                    nc.scalar.activation(st[:, 1:2], st[:, 0:1], ACT.Sqrt).then_inc(root_ok, 1)
                    for q in range(4):
                        n = 4 * i + q
                        act.wait_ge(h_tr, n + 1)
                        nc.scalar.activation(ahi[:, 4 * q:4 * q + 4, j * P:(j + 1) * P],
                                             PS[:, 4 + n % 2, :].rearrange("p (a b) -> p a b", a=4), ACT.Copy).then_inc(h_hi, 1)
                for cc in range(5):
                    for kg in range(4):
                        split_hi()
                        if kg == 1 and 5 * tc + cc:
                            if cc:
                                ada_rows(n_ada - 1)
                            if 5 * tc + cc > 1 and cc:
                                mod_rows(n_ada - 2)
                    for kg in range(4):
                        split_hi()
                        if kg == 1:
                            stage(tc, cc)
                    n_ada += 1
                if tc < 2:
                    ada_rows(n_ada - 1)
                    mod_rows(n_ada - 2)
            for kg in range(4):
                split_hi()
                if kg == 1:
                    ada_rows(n_ada - 1)
            ada_rows(n_ada)
            mod_rows(n_ada - 2)
            mod_rows(n_ada - 1)
            mod_rows(n_ada)

            for tc, (t0, nt, cond) in enumerate(CH):
                for k in range(unit_start[tc], unit_end[tc] + 2):
                    if k < unit_end[tc] and kind(k) == "H":
                        _, _, b, h = UNITS[k]
                        hc = heads_by(k)
                        cn, loc, _, _ = keys(tc, b)
                        w = (cn + len(loc)) * P
                        pair = 2 * (k % 2)
                        act.wait_ge(masked, hc + 1)
                        if hc >= 2:
                            act.wait_ge(p_tr, hc - 1)
                        nc.scalar.activation(pp[:, hc % 2, 0:w], PS[:, pair:pair + 2, :].rearrange("p a b -> p (a b)")[:, 0:w],
                                             ACT.Exp, bias=sm[:, hc % 2, 1:2], scale=SCALE,
                                             accum_out=sm[:, hc % 2, 2:3]).then_inc(exped, 1)
                        nc.scalar.activation(sm[:, hc % 2, 3:4], sinks[:, 0, h:h + 1], ACT.Exp,
                                             bias=sm[:, hc % 2, 1:2]).then_inc(sank, 1)
                    if k < unit_end[tc] and kind(k) == "M":
                        gi = UNITS[k][3]
                        pair = 2 * (k % 2)
                        act.wait_ge(unit_pe, k + 1)
                        for m in range(2):
                            ct = 2 * gi + m
                            nc.scalar.activation(ahi[:, NH + ct, 0:nt * P], PS[:, pair + m, 0:nt * P], ACT.Copy,
                                                 scale=pscale[:, ct:ct + 1]).then_inc(m_hi, 1)
                    if in_chunk(k - 1, tc) and kind(k - 1) == "H":
                        hc = heads_by(k - 1)
                        cn, loc, _, _ = keys(tc, UNITS[k - 1][2])
                        act.wait_ge(p_tr, hc + 1)
                        if hc >= 2:
                            act.wait_ge(pv_ok, hc - 1)
                        w = min(4, cn + len(loc))
                        if cn == 0:
                            w = 1
                        nc.scalar.activation(pT[:, hc % 2, 0:w, :], PS[:, 4, 0:w * P].rearrange("p (a b) -> p a b", a=w),
                                             ACT.Copy).then_inc(pt_a, 1)
                    if in_chunk(k - 2, tc) and kind(k - 2) == "H" and UNITS[k - 2][3] % 4 == 3:
                        _, _, b, h = UNITS[k - 2]
                        act.wait_ge(pv_ok, heads_by(k - 2) + 1)
                        nc.scalar.activation(ahi[:, h - 3:h + 1, b * P:(b + 1) * P],
                                             PS[:, 6 + h // 4, :].rearrange("p (a b) -> p a b", a=4), ACT.Copy).then_inc(o_hi, 1)
                for kg in range(16):
                    split_hi()
                for j in range(nt):
                    i = t0 + j
                    act.wait_ge(x1_ok, x1_by(tc, 3))
                    act.wait_ge(dtab_ok, tc + 1)
                    if i:
                        act.wait_ge(h2_out, 16 * i)
                        act.wait_ge(h2_tr, 4 * i)
                    nc.scalar.activation(h2b, x1[:, j, :], ACT.Square, accum_out=ss[:, TT + i:TT + i + 1]).then_inc(sq_ok, 1)
                    act.wait_ge(ms_ok, TT + i + 1)
                    nc.scalar.activation(st[:, 1:2], st[:, 0:1], ACT.Sqrt).then_inc(root_ok, 1)
                    for q in range(4):
                        n = 4 * i + q
                        act.wait_ge(h2_tr, n + 1)
                        if n:
                            act.wait_ge(h2T_used, n)
                        nc.scalar.activation(h2T, PS[:, n % 2, :].rearrange("p (a b) -> p a b", a=4), ACT.Copy).then_inc(h2T_ok, 1)
                    act.wait_ge(lmax_ok, i + 1)
                    nc.scalar.activation(aff[:, i, :], PS[:, 2, 0:NE], ACT.Exp, bias=st[:, 5:6],
                                         accum_out=st[:, 6:7]).then_inc(lexp_ok, 1)

            act.wait_ge(x1_out, 16 * TT)
            act.wait_ge(h2_out, 16 * TT)
            act.wait_ge(aff_tr, 1)
            nc.scalar.activation(affT[:], PS[0:NE, 4:7, :].rearrange("p a b -> p (a b)")[:, 0:NS + NP_], ACT.Copy).then_inc(affT_ok, 1)

            def take_tokens(j):
                nc.scalar.activation(xT[:, 4 * j:4 * j + 4, 0:CAP_S], PS[:, 4, :].rearrange("p (a b) -> p a b", a=4),
                                     ACT.Copy).then_inc(xs_ok, 1)

            for j in range(4):
                act.wait_ge(x_tr, j + 1)
                take_tokens(j)

            with act.Fori(0, NE) as e:
                for half in range(2):
                    act.wait_ge(ring_free, e * PIECES_E + NRING + 8 * half + 4)
                    nc.scalar.activation(hg[:, half, :].rearrange("p (a b) -> p a b", a=2), PS[:, 0:2, 0:2 * CAP],
                                         ACT.Silu).then_inc(silu_ok, 1)
                for cc in range(4):
                    b = 2 * (cc % 2)
                    act.wait_ge(ring_free, e * PIECES_E + NRING + 18 + 2 * cc)
                    nc.scalar.activation(yT[:, cc % 2, :].rearrange("p (a b) -> p a b", a=2), PS[:, b:b + 2, 0:2 * CAP],
                                         ACT.Copy).then_inc(yT_ok, 1)
                    act.wait_ge(x_tr, e * 4 + 5 + cc)
                    take_tokens(cc)

            for i in range(TT):
                act.wait_ge(f_in[i % NF], 16 * (i // NF + 1))
                if i >= NF:
                    act.wait_ge(f_out[i % NF], 16 * (i // NF))
                nc.scalar.activation(ring[:, NF + i % NF].rearrange("p a b -> p (a b)"),
                                     ring[:, i % NF].rearrange("p a b -> p (a b)"), ACT.Square,
                                     accum_out=ss[:, 2 * TT + i:2 * TT + i + 1]).then_inc(f_sq, 1)
                act.wait_ge(f_ms, i + 1)
                nc.scalar.activation(st[:, 1:2], st[:, 0:1], ACT.Sqrt).then_inc(f_root, 1)

        @block.vector
        def _(dve):
            g = [0]
            steps = [0]

            def link(ins):
                steps[0] += 1
                ins.then_inc(dve_step, 1)
                dve.wait_ge(dve_step, steps[0])

            def split_lo():
                n = g[0]
                g[0] += 1
                dve.wait_ge(hi_ok, n + 1)
                nc.vector.tensor_tensor(wlo[:, n % NSPLIT], raw[:, n % NRAW], whi[:, n % NSPLIT].bitcast(F32),
                                        ALU.subtract).then_inc(lo_ok, 1)

            def rstd(col, n, sq, ms, root):
                dve.wait_ge(sq, n)
                nc.vector.tensor_scalar(st[:, 0:1], ss[:, col:col + 1], 1.0 / D, EPS, ALU.mult, ALU.add).then_inc(ms, 1)
                dve.wait_ge(root, n)
                link(nc.vector.reciprocal(st[:, 2:3], st[:, 1:2]))
                link(nc.vector.scalar_tensor_tensor(out=st[:, 3:4], in0=st[:, 2:3], scalar=st[:, 2:3], in1=st[:, 0:1],
                                                    op0=ALU.mult, op1=ALU.mult))
                link(nc.vector.tensor_scalar(st[:, 3:4], st[:, 3:4], -0.5, 1.5, ALU.mult, ALU.add))
                link(nc.vector.tensor_tensor(st[:, 4:5], st[:, 2:3], st[:, 3:4], ALU.mult))

            nc.vector.memset(cond_s[:].bitcast(F32), 0.0).then_inc(zero_ok, 1)
            dve.wait_ge(cond_hi, 1)
            cf = cond_f.rearrange("p (c t) -> p t c", c=2)
            nc.vector.tensor_tensor(cond_s[:, :, 2:4], cf, cond_s[:, :, 0:2].bitcast(F32), ALU.subtract).then_inc(cond_lo, 1)
            for _ in range(4 * ADA_A):
                split_lo()

            for tc, (t0, nt, cond) in enumerate(CH):
                if tc != 1:
                    n = tc // 2
                    dve.wait_ge(tab_in, 16 * (2 * n + 2))
                    dve.wait_ge(x_in[0], 16 * (x_loads(t0) - 1))
                    nc.vector.scalar_tensor_tensor(out=tabA, in0=tabA, scalar=1.0, in1=xb[:, 0, :],
                                                   op0=ALU.add, op1=ALU.mult).then_inc(tab_ok, 1)
                    dve.wait_ge(tab_ok, n + 1)
                for j in range(nt):
                    i = t0 + j
                    rstd(i, i + 1, sq_ok, ms_ok, root_ok)
                    x = xb[:, i % 2, :]
                    link(nc.vector.scalar_tensor_tensor(out=x, in0=x, scalar=st[:, 4:5], in1=tabA,
                                                        op0=ALU.mult, op1=ALU.mult))
                    nc.vector.tensor_tensor(x, x, tabS, ALU.add).then_inc(h_ok, 1)
                    for q in range(4):
                        n = 4 * i + q
                        dve.wait_ge(h_hi, n + 1)
                        s = (slice(None), slice(4 * q, 4 * q + 4), slice(j * P, (j + 1) * P))
                        nc.vector.tensor_tensor(alo[s], PS[:, 4 + n % 2, :].rearrange("p (a b) -> p a b", a=4),
                                                ahi[s].bitcast(F32), ALU.subtract).then_inc(h_lo, 1)
                for _ in range(40):
                    split_lo()
            for _ in range(4):
                split_lo()

            for tc, (t0, nt, cond) in enumerate(CH):
                for k in range(unit_start[tc], unit_end[tc] + 2):
                    if in_chunk(k - 1, tc) and kind(k - 1) == "H":
                        hc = heads_by(k - 1)
                        cn, loc, _, _ = keys(tc, UNITS[k - 1][2])
                        w = (cn + len(loc)) * P
                        s = sm[:, hc % 2, :]
                        dve.wait_ge(sank, hc + 1)
                        link(nc.vector.tensor_tensor(s[:, 4:5], s[:, 2:3], s[:, 3:4], ALU.add))
                        link(nc.vector.reciprocal(s[:, 5:6], s[:, 4:5]))
                        nc.vector.tensor_scalar(pp[:, hc % 2, 0:w], pp[:, hc % 2, 0:w], s[:, 5:6], None,
                                                ALU.mult).then_inc(p_ok, 1)
                    if k < unit_end[tc]:
                        _, kd, b, h = UNITS[k]
                        pair = 2 * (k % 2)
                        flat = PS[:, pair:pair + 2, :].rearrange("p a b -> p (a b)")
                        dve.wait_ge(unit_pe, k + 1)
                        if kd == "H":
                            hc = heads_by(k)
                            cn, loc, ml, mr = keys(tc, b)
                            w = (cn + len(loc)) * P
                            s = sm[:, hc % 2, :]
                            if ml:
                                v = flat[:, cn * P:(cn + 1) * P]
                                link(nc.vector.tensor_tensor(v, v, maskL[:], ALU.add))
                            if mr:
                                v = flat[:, w - P:w]
                                link(nc.vector.tensor_tensor(v, v, maskR[:], ALU.add))
                            link(nc.vector.reduce_max(s[:, 0:1], flat[:, 0:w], AXX))
                            nc.vector.tensor_scalar(s[:, 1:2], s[:, 0:1], -SCALE, sinks[:, 1, h:h + 1],
                                                    ALU.mult, ALU.min).then_inc(masked, 1)
                        elif kd == "K":
                            nk = 9 if cond == 0 else 2
                            z0, z1 = h * 8, min(h * 8 + 8, 2 * nk)
                            nc.vector.tensor_copy(kT[:, z0 * P:z1 * P], flat[:, 0:(z1 - z0) * P]).then_inc(copied, 1)
                        elif kd == "Q":
                            nc.vector.tensor_copy(qT.rearrange("p a b -> p (a b)"), flat).then_inc(copied, 1)
                        else:
                            dve.wait_ge(m_hi, 2 * (m_by(k) + 1))
                            for m in range(2):
                                ct = 2 * h + m
                                ins = nc.vector.scalar_tensor_tensor(
                                    out=alo[:, NH + ct, 0:nt * P], in0=PS[:, pair + m, 0:nt * P],
                                    scalar=pscale[:, ct:ct + 1], in1=ahi[:, NH + ct, 0:nt * P].bitcast(F32),
                                    op0=ALU.mult, op1=ALU.subtract)
                            ins.then_inc(copied, 1)
                    if in_chunk(k - 1, tc) and kind(k - 1) == "H":
                        hc = heads_by(k - 1)
                        cn, loc, _, _ = keys(tc, UNITS[k - 1][2])
                        dve.wait_ge(p_tr, hc + 1)
                        if hc >= 2:
                            dve.wait_ge(pv_ok, hc - 1)
                        z0 = 4 if cn else 1
                        z1 = cn + len(loc)
                        flat = PS[:, 4:6, :].rearrange("p a b -> p (a b)")
                        c0 = p_place(cn, z0) * P
                        nc.vector.tensor_copy(pT[:, hc % 2, z0:z1, :],
                                              flat[:, c0:c0 + (z1 - z0) * P].rearrange("p (a b) -> p a b", b=P)).then_inc(pt_v, 1)
                    if in_chunk(k - 2, tc) and kind(k - 2) == "H" and UNITS[k - 2][3] % 4 == 3:
                        _, _, b, h = UNITS[k - 2]
                        dve.wait_ge(o_hi, (heads_by(k - 2) + 1) // 4)
                        s = (slice(None), slice(h - 3, h + 1), slice(b * P, (b + 1) * P))
                        nc.vector.tensor_tensor(alo[s], PS[:, 6 + h // 4, :].rearrange("p (a b) -> p a b", a=4),
                                                ahi[s].bitcast(F32), ALU.subtract).then_inc(o_lo, 1)

                def residual(cc):
                    dve.wait_ge(used, D0 + 4 * (4 * tc + cc + 1))
                    s = slice(cc * CC, (cc + 1) * CC)
                    for m in range(nt):
                        v = PS[:, 4 * (cc % 2) + m, :]
                        link(nc.vector.tensor_tensor(v, v, tabG[:, s], ALU.mult))
                        nc.vector.tensor_tensor(x1[:, m, s], x1[:, m, s], v, ALU.add).then_inc(x1_ok, 1)

                for cc in range(4):
                    for kg in range(4):
                        split_lo()
                        if kg == 1 and cc:
                            if cc == 1:
                                dve.wait_ge(dtab_in, 16 * (4 * tc + 4))
                                dve.wait_ge(x1_in, 16 * (t0 + nt))
                            residual(cc - 1)
                residual(3)
                nc.vector.scalar_tensor_tensor(out=tabA2, in0=tabA2, scalar=1.0, in1=h2b, op0=ALU.add,
                                               op1=ALU.mult).then_inc(dtab_ok, 1)
                dve.wait_ge(dtab_ok, tc + 1)
                for j in range(nt):
                    i = t0 + j
                    rstd(TT + i, TT + i + 1, sq_ok, ms_ok, root_ok)
                    link(nc.vector.scalar_tensor_tensor(out=h2b, in0=x1[:, j, :], scalar=st[:, 4:5], in1=tabA2,
                                                        op0=ALU.mult, op1=ALU.mult))
                    nc.vector.tensor_tensor(h2b, h2b, tabS2, ALU.add).then_inc(h2_ok, 1)
                    dve.wait_ge(h2T_used, 4 * i + 4)
                    nc.vector.tensor_reduce(st[:, 5:6], PS[:, 2, 0:NE], AXX, ALU.max, negate=True).then_inc(lmax_ok, 1)
                    dve.wait_ge(lexp_ok, i + 1)
                    link(nc.vector.reciprocal(st[:, 7:8], st[:, 6:7]))
                    nc.vector.tensor_scalar(aff[:, i, :], aff[:, i, :], st[:, 7:8], None, ALU.mult).then_inc(aff_ok, 1)

            dve.wait_ge(affT_ok, 1)
            link(nc.vector.memset(idx_s[:], 0))
            link(nc.vector.memset(idx_p[:], 0))
            for c0, c1, k0, cap in ((0, NS, 0, CAP_S), (NS, NS + NP_, CAP_S, CAP_P)):
                v = affT[:, c0:c1]
                for r in range(cap // 8):
                    s = slice(k0 + 8 * r, k0 + 8 * r + 8)
                    link(nc.vector.max(top[:, s], v))
                    link(nc.vector.max_index(topi[:, s], top[:, s], v))
                    link(nc.vector.match_replace(v, top[:, s], v, -1.0))
            nc.vector.tensor_copy(topf[:], topi[:]).then_inc(top_ok, 1)
            dve.wait_ge(top_tr, 1)
            link(nc.vector.tensor_copy(gate_s[:], PS[:, 0, 0:NE]))
            link(nc.vector.tensor_copy(gate_p[:], PS[0:CAP_P, 1, 0:NE]))
            link(nc.vector.tensor_copy(idx_s[:, 0:NE], PS[:, 0, NE:2 * NE]))
            link(nc.vector.tensor_copy(idx_p[:, 0:NE], PS[0:CAP_P, 1, NE:2 * NE]))
            nc.vector.tensor_copy(ig_s[:], idx_s[:, 0:1])
            nc.vector.tensor_copy(ig_p[:], idx_p[:, 0:1]).then_inc(gate_ok, 1)

            def take_prompt(j):
                nc.vector.tensor_copy(xT[:, 4 * j:4 * j + 4, CAP_S:CAP],
                                      PS[:, 5, 0:4 * CAP_P].rearrange("p (a b) -> p a b", a=4)).then_inc(xp_ok, 1)

            for j in range(4):
                dve.wait_ge(x_tr, j + 1)
                take_prompt(j)
            dve.wait_ge(g2_in, 32)

            with dve.Fori(0, NE) as e:
                dve.wait_ge(gs_in, e * 16 + 16)
                dve.wait_ge(gp_in, e * 16 + 16)
                nc.vector.tensor_copy(ig_s[:], idx_s[:, bass.ds(e + 1, 1)])
                nc.vector.tensor_copy(ig_p[:], idx_p[:, bass.ds(e + 1, 1)]).then_inc(ig_ok, 1)
                dve.wait_ge(y_free, e + 1)
                nc.vector.tensor_copy(ic_s[:], idx_s[:, bass.ds(e, 1)])
                nc.vector.tensor_copy(ic_p[:], idx_p[:, bass.ds(e, 1)]).then_inc(ic_ok, 1)
                for half in range(2):
                    dve.wait_ge(silu_ok, e * 2 + half + 1)
                    dve.wait_ge(ring_free, e * PIECES_E + NRING + 8 * half + 8)
                    h = hid[:, 4 * half:4 * half + 4, :].rearrange("p (a c) b -> p a (c b)", a=2)
                    nc.vector.tensor_tensor(h, hg[:, half, :].rearrange("p (a b) -> p a b", a=2), PS[:, 2:4, 0:2 * CAP],
                                            ALU.mult).then_inc(hid_ok, 1)

                def scale_rows(c):
                    s = slice(c * CC, (c + 1) * CC)
                    dve.wait_ge(y_tr, e * 4 + c + 1)
                    nc.vector.scalar_tensor_tensor(out=y_s[:, s], in0=PS[:, 6, :], scalar=gate_s[:, bass.ds(e, 1)],
                                                   in1=g2_s[:, s], op0=ALU.mult, op1=ALU.mult).then_inc(ys_ok, 1)
                    nc.vector.scalar_tensor_tensor(out=y_p[:, s], in0=PS[0:CAP_P, 7, :], scalar=gate_p[:, bass.ds(e, 1)],
                                                   in1=g2_p[:, s], op0=ALU.mult, op1=ALU.mult).then_inc(yp_ok, 1)

                for cc in range(4):
                    dve.wait_ge(x_tr, e * 4 + 5 + cc)
                    take_prompt(cc)
                    if cc:
                        scale_rows(cc - 1)
                scale_rows(3)

            dve.wait_ge(nf_in, 16)
            for i in range(TT):
                rstd(2 * TT + i, i + 1, f_sq, f_ms, f_root)
                nc.vector.scalar_tensor_tensor(out=ring[:, NF + i % NF].rearrange("p a b -> p (a b)"),
                                               in0=ring[:, i % NF].rearrange("p a b -> p (a b)"), scalar=st[:, 4:5],
                                               in1=ring[:, 2 * NF].rearrange("p a b -> p (a b)"),
                                               op0=ALU.mult, op1=ALU.mult).then_inc(f_ok, 1)

        @block.gpsimd
        def _(pool):
            steps = [0]
            dma = nc.gpsimd.dma_start

            def link(ins):
                steps[0] += 1
                ins.then_inc(pool_step, 1)
                pool.wait_ge(pool_step, steps[0])

            dma(cond_r[0:16, :], t["c"].rearrange("b (t p) -> (b t) p", p=P)).then_inc(cond_in, 16)
            dma(cond_r[16:32, :], t["c_ctx"].rearrange("(t p) -> t p", p=P)).then_inc(cond_in, 16)
            dma(ident[:], t["k_ident"]).then_inc(consts_in, 16)
            dma(sel[:], t["k_sel"]).then_inc(consts_in, 16)
            dma(maskL[:], t["k_mask"][0]).then_inc(consts_in, 16)
            dma(maskR[:], t["k_mask"][1]).then_inc(consts_in, 16)
            dma(sinks[:, 0, :], t["sink_logits"][0].partition_broadcast(P)).then_inc(consts_in, 16)
            dma(sinks[:, 1, :], t["sink_logits"][0].partition_broadcast(P)).then_inc(consts_in, 16)
            dma(pscale[:], t["pool_scale"]).then_inc(consts_in, 16)
            for z in range(4):
                dma(wr[:, 4 * z:4 * z + 4, :],
                    t["w_router"][0, z * 512:(z + 1) * 512].rearrange("(t p) e -> p t e", p=P)).then_inc(consts_in, 16)

            def bias_row(a):
                if a >= 2:
                    pool.wait_ge(sel_ok, a - 1)
                dma(arow[4:5, a % 2, :], t["b_ada"][:, a * CC:(a + 1) * CC]).then_inc(brow_in[a % 2], 16)

            def store_mod(a):
                pool.wait_ge(mrow_ok, a + 1)
                dma(mod_d[:, a * CC:(a + 1) * CC], mrow[0:2, a % 2, :]).then_inc(mod_out[a % 2], 16)

            def mods_stored(n):
                pool.wait_ge(mod_out[0], 16 * ((n + 1) // 2))
                pool.wait_ge(mod_out[1], 16 * (n // 2))

            def table(dst, cond, m, n=P):
                return dma(dst, mod_d[cond, m * D:(m + 1) * D].partition_broadcast(n))

            bias_row(0)
            bias_row(1)
            pool.wait_ge(consts_in, 16 * N_CONST)
            link(nc.gpsimd.tensor_scalar(sinks[:, 1, :], sinks[:, 1, :], -1.0, None, ALU.mult))
            for a in range(ADA_A):
                store_mod(a)
                bias_row(a + 2)
            mods_stored(ADA_A)

            n_ada = ADA_A
            for tc, (t0, nt, cond) in enumerate(CH):
                if tc != 1:
                    if tc:
                        pool.wait_ge(h_ok, t0)
                        pool.wait_ge(h_tr, 4 * t0)
                    table(tabA, cond, 1).then_inc(tab_in, 16)
                    table(tabS, cond, 0).then_inc(tab_in, 16)
                    dma(xb[:, 0, :], t["norm_mix"][0].partition_broadcast(P)).then_inc(x_in[0], 16)
                    pool.wait_ge(tab_ok, 1 + tc // 2)
                for j in range(nt):
                    i = t0 + j
                    if i >= 2:
                        pool.wait_ge(h_tr, 4 * (i - 1))
                    dma(xb[:, i % 2, :], rows(xs, xp, i)).then_inc(x_in[i % 2], 16)
                for cc in range(5):
                    n = 5 * tc + cc
                    done = staged_by(n)
                    for m in range(nt if cc < 3 else 4):
                        pool.wait_ge(stg_ok, done + m + 1)
                        i = t0 + m
                        if cc < 3:
                            nr = 8 if cc < 2 else 4
                            if cond == 0:
                                dma(rtab, t["k_rope"][i]).then_inc(rtab_in, 16)
                                s = stg[:, m, 0:nr * 64].rearrange("p (a h f) -> p a h f", h=2, f=32)
                                a1, a2 = s[:, :, 0, :], s[:, :, 1, :]
                                cs, sn = (rtab[:, z, 0:nr * 32].rearrange("p (a f) -> p a f", f=32) for z in range(2))
                                r = [rt[:, z, 0:nr * 32].rearrange("p (a f) -> p a f", f=32) for z in range(4)]
                                pool.wait_ge(rtab_in, 16 * (3 * 4 * tc + 4 * cc + m + 1))
                                nc.gpsimd.tensor_tensor(r[0], a1, cs, ALU.mult)
                                nc.gpsimd.tensor_tensor(r[1], a2, sn, ALU.mult)
                                nc.gpsimd.tensor_tensor(r[2], a1, sn, ALU.mult)
                                link(nc.gpsimd.tensor_tensor(r[3], a2, cs, ALU.mult))
                                nc.gpsimd.tensor_tensor(a1, r[0], r[1], ALU.subtract)
                                link(nc.gpsimd.tensor_tensor(a2, r[2], r[3], ALU.add))
                            dma(qkv_d[i * P:(i + 1) * P, cc * CC:(cc + 1) * CC], stg[:, m, :]).then_inc(stg_out, 16)
                            if cond and cc == 2:
                                dma(st_k[m * P:(m + 1) * P, :], stg[:, m, 0:KW]).then_inc(stg_out, 16)
                                dma(st_v[m * P:(m + 1) * P, :], stg[:, m, KW:2 * KW]).then_inc(stg_out, 16)
                        else:
                            ct = (cc - 3) * 4 + m
                            dma(pool_d[ct * P:(ct + 1) * P, t0 * P:(t0 + nt) * P], stg[:, m, 0:nt * P]).then_inc(stg_out, 16)
                    store_mod(n_ada - 1) if n else None
                    if n and n_ada + 1 < NADA:
                        bias_row(n_ada + 1)
                    n_ada += 1
            store_mod(n_ada - 1)
            store_mod(n_ada)
            mods_stored(NADA)
            pool.wait_ge(stg_out, 16 * stores_by[-1])
            pool.wait_ge(used, D0)
            pool.wait_ge(lo_ok, D0)

            def load_q(i):
                if i:
                    k = max(z for z in range(n_units) if UNITS[z][1] == "Q" and CH[UNITS[z][0]][0] + UNITS[z][2] == i - 1)
                    pool.wait_ge(unit_pe, k + 1)
                dma(qq, qkv_d[i * P:(i + 1) * P, 0:AW]).then_inc(q_in, 16)

            def mixer(tc, gi):
                t0, nt, cond = CH[tc]
                T = nt * P
                w, L = POOLS[gi], T + 2 * HALO
                n = 4 * tc + gi
                first = t0 in (0, ST)
                final = t0 + nt in (ST, TT)
                c0, c1 = (HALO if first else 0), T + 2 * HALO - (HALO if final else 0)
                if n:
                    pool.wait_ge(mixed, n)
                    pool.wait_ge(unit_pe, m_unit(n - 1) + 1)
                if first:
                    link(nc.gpsimd.memset(pin[:, :, 0:HALO], 0.0))
                if final:
                    link(nc.gpsimd.memset(pin[:, :, HALO + T:L], 0.0))
                dma(pw, t["pool_w"][0, gi].rearrange("(z p) n -> p z n", p=P)).then_inc(pin_in, 16)
                dma(rcnt[:, 0:T], t["k_rcnt"][gi, t0 * P:t0 * P + T].partition_broadcast(P)).then_inc(pin_in, 16)
                for z in range(2):
                    ct = 2 * gi + z
                    dma(pin[:, z, c0:c1], pool_d[ct * P:(ct + 1) * P, t0 * P - HALO + c0:t0 * P - HALO + c1]).then_inc(pin_in, 16)
                pool.wait_ge(pin_in, 64 * (n + 1))
                link(nc.gpsimd.tensor_tensor(pa[:, :, 1:L], pin[:, :, 0:L - 1], pin[:, :, 1:L], ALU.add))
                src, dst, lo, hi, half = pa, pb, 1, L, 1
                while 2 * half < w:
                    link(nc.gpsimd.tensor_tensor(dst[:, :, lo + half:hi - half], src[:, :, lo:hi - 2 * half],
                                                 src[:, :, lo + 2 * half:hi], ALU.add))
                    lo, hi = lo + half, hi - half
                    src, dst, half = dst, src, 2 * half
                for z in range(2):
                    link(nc.gpsimd.tensor_tensor(src[:, z, HALO:HALO + T], src[:, z, HALO:HALO + T], rcnt[:, 0:T], ALU.mult))
                nc.gpsimd.tensor_tensor(mixT[:, :, 0:T], src[:, :, HALO:HALO + T], pin[:, :, HALO:HALO + T],
                                        ALU.subtract).then_inc(mixed, 1)

            for tc, (t0, nt, cond) in enumerate(CH):
                if tc:
                    pool.wait_ge(aff_ok, t0)
                    pool.wait_ge(x1_out, 16 * t0)
                    pool.wait_ge(h2_out, 16 * t0)
                if cond == 0:
                    k0 = max(0, t0 - 1)
                    for dst, cache, col in ((ktm, ck, AW), (vv, cv, AW + KW)):
                        dma(dst[:, 0:4, :], cache.rearrange("(b p) d -> p b d", p=P)).then_inc(kv_in, 16)
                        dma(dst[:, 4:9, :], qkv_d[k0 * P:(k0 + 5) * P, col:col + KW].rearrange("(b p) d -> p b d", p=P)).then_inc(kv_in, 16)
                else:
                    for dst, col in ((ktm, AW), (vv, AW + KW)):
                        dma(dst[:, 0:2, :], qkv_d[NS:NS + NP_, col:col + KW].rearrange("(b p) d -> p b d", p=P)).then_inc(kv_in, 16)
                load_q(t0)
                per = 4 // nt
                for b in range(nt):
                    if b + 1 < nt:
                        pool_next = t0 + b + 1
                    for gi in range(b * per, b * per + per):
                        mixer(tc, gi)
                    if b + 1 < nt:
                        load_q(pool_next)

                pool.wait_ge(pv_ok, heads_by(unit_end[tc]))
                pool.wait_ge(unit_pe, unit_end[tc])
                pool.wait_ge(o_lo, heads_by(unit_end[tc]) // 4)
                pool.wait_ge(copied, copies_by(unit_end[tc]))
                pool.wait_ge(pt_a, heads_by(unit_end[tc]))
                table(tabG, cond, 2).then_inc(dtab_in, 16)
                table(tabA2, cond, 4).then_inc(dtab_in, 16)
                table(tabS2, cond, 3).then_inc(dtab_in, 16)
                if tc:
                    pool.wait_ge(h2_tr, 4 * t0)
                dma(h2b, t["norm_ffn"][0].partition_broadcast(P)).then_inc(dtab_in, 16)
                for j in range(nt):
                    dma(x1[:, j, :], rows(xs, xp, t0 + j)).then_inc(x1_in, 16)
                pool.wait_ge(x1_ok, x1_by(tc, 3))
                for j in range(nt):
                    dma(rows(res_s, res_p, t0 + j), x1[:, j, :]).then_inc(x1_out, 16)
                for j in range(nt):
                    pool.wait_ge(h2_ok, t0 + j + 1)
                    dma(rows(h2_s, h2_p, t0 + j), h2b).then_inc(h2_out, 16)
            pool.wait_ge(x1_out, 16 * TT)
            pool.wait_ge(h2_out, 16 * TT)
            pool.wait_ge(aff_tr, 1)

            table(g2_s[:], 0, 5).then_inc(g2_in, 16)
            table(g2_p[:], 1, 5, CAP_P).then_inc(g2_in, 16)

            def gather():
                nc.gpsimd.indirect_dma_start(out=g_s[:], out_offset=None, in_=h2_s,
                                             in_offset=bass.IndirectOffsetOnAxis(ap=ig_s[:, 0:1], axis=0)).then_inc(gs_in, 16)
                nc.gpsimd.indirect_dma_start(out=g_p[:], out_offset=None, in_=h2_p,
                                             in_offset=bass.IndirectOffsetOnAxis(ap=ig_p[:, 0:1], axis=0)).then_inc(gp_in, 16)

            pool.wait_ge(gate_ok, 1)
            gather()
            nc.gpsimd.nop().then_inc(y_free, 1)
            with pool.Fori(0, NE) as e:
                pool.wait_ge(ig_ok, e + 1)
                pool.wait_ge(x_tr, e * 4 + 4)
                nc.gpsimd.nop().then_inc(turn, 1)
                gather()
                pool.wait_ge(ic_ok, e + 1)
                pool.wait_ge(ys_ok, e * 4 + 4)
                pool.wait_ge(yp_ok, e * 4 + 4)
                nc.gpsimd.nop().then_inc(turn, 1)
                nc.gpsimd.indirect_dma_start(out=res_s, out_offset=bass.IndirectOffsetOnAxis(ap=ic_s[:, 0:1], axis=0),
                                             in_=y_s[:], in_offset=None, compute_op=ALU.add).then_inc(s_out, 16)
                nc.gpsimd.indirect_dma_start(out=res_p, out_offset=bass.IndirectOffsetOnAxis(ap=ic_p[:, 0:1], axis=0),
                                             in_=y_p[:], in_offset=None, compute_op=ALU.add).then_inc(p_out, 16)
                pool.wait_ge(s_out, e * 16 + 16)
                pool.wait_ge(p_out, e * 16 + 16)
                nc.gpsimd.nop().then_inc(y_free, 1)

            pool.wait_ge(ring_free, NRING + NE * PIECES_E)
            pool.wait_ge(gs_in, 16 * (NE + 1))
            pool.wait_ge(gp_in, 16 * (NE + 1))
            flat = [ring[:, z].rearrange("p a b -> p (a b)") for z in range(2 * NF + 1)]
            dma(flat[2 * NF], t["norm_final"].partition_broadcast(P)).then_inc(nf_in, 16)
            for i in range(NF):
                dma(flat[i], rows(res_s, res_p, i)).then_inc(f_in[i], 16)
            for i in range(TT):
                pool.wait_ge(f_ok, i + 1)
                dma(rows(ys, yp, i), flat[NF + i % NF]).then_inc(f_out[i % NF], 16)
                if i + NF < TT:
                    dma(flat[i % NF], rows(res_s, res_p, i + NF)).then_inc(f_in[i % NF], 16)
            for z in range(NF):
                pool.wait_ge(f_out[z], 16 * ((TT - z + NF - 1) // NF))


def shape_constants():
    i = np.arange(P)
    mask = np.zeros((2, P, P), np.float32)
    mask[0][i[None, :] < i[:, None]] = NEG
    mask[1][i[None, :] > i[:, None]] = NEG
    grid, nf = 64, HD // 4
    pos = np.arange(NS)
    inv = (np.float32(10000.0) ** (-np.arange(nf, dtype=np.float32) / np.float32(nf))).astype(np.float32)
    ang = np.stack([(pos // grid).astype(np.float32)[:, None] * inv,
                    (pos % grid).astype(np.float32)[:, None] * inv], axis=1).reshape(NS, 2 * nf)
    rope = np.stack([np.tile(np.cos(ang), (1, 4)), np.tile(np.sin(ang), (1, 4))], axis=1).astype(np.float32)
    rcnt = np.zeros((4, NS + NP_), np.float32)
    for gi, w in enumerate(POOLS):
        for base, n in ((0, NS), (NS, NP_)):
            tok = np.arange(n)
            cnt = np.clip(tok + w - w // 2, 0, n) - np.clip(tok - w // 2, 0, n)
            rcnt[gi, base:base + n] = 1.0 / cnt
    sel = np.zeros((5, 2), np.float32)
    sel[[0, 2], 0] = 1.0
    sel[[1, 3], 1] = 1.0
    sel[4] = 1.0
    return {"k_ident": np.eye(P, dtype=np.float32), "k_mask": mask,
            "k_rope": rope.reshape(ST, P, 2, 256), "k_rcnt": rcnt, "k_sel": sel}


_INS = ["x_prompt", "x_sample", "c", "cache_k", "cache_v", "c_ctx", "w_ada", "b_ada", "norm_mix", "w_in",
        "sink_logits", "pool_w", "pool_scale", "w_out", "norm_ffn", "w_router", "w_gate", "w_up", "w_down",
        "norm_final"]
_OUTS = [("y_prompt", (1, NP_, D)), ("y_sample", (1, NS, D)), ("state_k", (1, 1, NP_, NKV, HD)),
         ("state_v", (1, 1, NP_, NKV, HD))]


def kernel(**inputs):
    import concourse.bacc as _bacc
    from concourse.bass_utils import run_bass_kernel_spmd as _run

    nc = _bacc.Bacc("TRN2", target_bir_lowering=False, num_devices=1)
    arrays = {n: np.ascontiguousarray(inputs[n]) for n in _INS}
    arrays["pool_scale"] = np.ascontiguousarray(arrays["pool_scale"].reshape(PW // P, P).T)
    arrays.update(shape_constants())
    t = {n: nc.dram_tensor(n, a.shape, F32, kind="ExternalInput").ap() for n, a in arrays.items()}
    o = {n: nc.dram_tensor(n, s, F32, kind="ExternalOutput").ap() for n, s in _OUTS}
    hybrid_backbone_step(nc, t, o)
    r = _run(nc, [arrays], core_ids=[0])
    return tuple(r.results[0][n] for n, _ in _OUTS)
```

```python
from contextlib import ExitStack

import numpy as np

import concourse.bass as bass
from concourse import mybir

F32 = mybir.dt.float32
F32R = mybir.dt.float32r
BF16 = mybir.dt.bfloat16
U32 = mybir.dt.uint32
ACT = mybir.ActivationFunctionType
ALU = mybir.AluOpType
AXX = mybir.AxisListType.X

P = 128
D = 2048
KT = D // P
NS = 1024
NP_ = 256
ST = NS // P
TT = (NS + NP_) // P
CH = [(0, 4, 0), (4, 4, 0), (8, 2, 1)]
PAST = 512
NH, NKV, HD = 8, 2, 128
AW = NH * HD
KW = NKV * HD
PW = D - AW
INW = AW + 2 * KW + PW
POOLS = (2, 4, 8, 16)
PG = PW // 4
HALO = 8
NE = 16
FE = 1024
CAP_S, CAP_P = 2 * NS // NE, 2 * NP_ // NE
CAP = CAP_S + CAP_P
EPS = 1e-6
NEG = -1e30
SCALE = HD ** -0.5
CC = 512
KG = 4
NRAW = 3
NSPLIT = 3
NRING = 12
NADA = 6 * D // CC
ADA_A = 2 * D // CC
PIECES_E = 2 * (D // P // KG) * (FE // CC) + (FE // P // KG) * (D // CC)


def stream_units():
    units, a = [], ADA_A
    for tc, ada_after in enumerate(((2, 2, 2, 1, 1), (2, 2, 2, 1, 1), (0, 0, 0, 0, 0))):
        for cc in range(5):
            units.append(("w", tc, cc))
            for _ in range(ada_after[cc]):
                units.append(("a", a, 0))
                a += 1
    assert a == NADA
    return units


B_UNITS = stream_units()


def build_units():
    units = []
    for tc, (t0, nt, cond) in enumerate(CH):
        nk = 9 if cond == 0 else 2
        nu = (2 * nk + 7) // 8
        for u in range(nu):
            units.append((tc, "K", 0, u))
        per = 4 // nt
        for b in range(nt):
            units.append((tc, "Q", b, 0))
            for h in range(NH):
                units.append((tc, "H", b, h))
            for g in range(b * per, b * per + per):
                units.append((tc, "M", b, g))
    heads, copies, nh, ncp = [], [], 0, 0
    for u in units:
        heads.append(nh)
        copies.append(ncp)
        if u[1] == "H":
            nh += 1
        else:
            ncp += 1
    return units, heads, copies


UNITS, HEADS_BEFORE, COPIES_BEFORE = build_units()


def local_blocks(tc, b):
    t0, nt, cond = CH[tc]
    if cond:
        return [0, 1], False, False
    q = t0 + b
    first = max(0, t0 - 1)
    ks = [k for k in (q - 1, q, q + 1) if 0 <= k < ST]
    return [k - first for k in ks], q - 1 >= 0, q + 1 < ST


def hybrid_backbone_step(nc, t, o):
    ctx = ExitStack()
    with ctx:
        def sem(name):
            return ctx.enter_context(nc.semaphore(name))

        def dram(name, shape):
            return nc.dram_tensor(name, shape, F32, kind="Internal").ap()

        mod_d = dram("mod_rows", [2, 6 * D])
        qkv_d = dram("qkv_rows", [NS + NP_, AW + 2 * KW])
        pool_d = dram("pool_cols", [PW, NS + NP_])
        res_s, res_p = dram("resid_s", [NS, D]), dram("resid_p", [NP_, D])
        h2_s, h2_p = dram("h2_s", [NS, D]), dram("h2_p", [NP_, D])

        xs = t["x_sample"].rearrange("b n d -> (b n) d")
        xp = t["x_prompt"].rearrange("b n d -> (b n) d")
        ys = o["y_sample"].rearrange("b n d -> (b n) d")
        yp = o["y_prompt"].rearrange("b n d -> (b n) d")
        st_k = o["state_k"].rearrange("b l n h d -> (b l n) (h d)")
        st_v = o["state_v"].rearrange("b l n h d -> (b l n) (h d)")
        ck = t["cache_k"].rearrange("b l n h d -> (b l n) (h d)")
        cv = t["cache_v"].rearrange("b l n h d -> (b l n) (h d)")
        w_ada = t["w_ada"].rearrange("l k n -> (l k) n")
        w_in = t["w_in"].rearrange("l k n -> (l k) n")
        w_out = t["w_out"].rearrange("l k n -> (l k) n")
        w_gate = t["w_gate"].rearrange("l e k n -> (l e) k n")
        w_up = t["w_up"].rearrange("l e k n -> (l e) k n")
        w_down = t["w_down"].rearrange("l e k n -> (l e) k n")

        def rows(a_s, a_p, i):
            return a_s[i * P:(i + 1) * P, :] if i < ST else a_p[(i - ST) * P:(i - ST + 1) * P, :]

        def piece(w, kg, c0):
            return w[kg * KG * P:(kg + 1) * KG * P, c0:c0 + CC].rearrange("(r p) n -> p r n", p=P)

        pieces = [piece(w_ada, kg, a * CC) for a in range(ADA_A) for kg in range(4)]
        for kd, n, cc in B_UNITS:
            pieces += [piece(*((w_in, kg, cc * CC) if kd == "w" else (w_ada, kg, n * CC))) for kg in range(4)]
        D0 = len(pieces)
        for tc in range(3):
            for cc in range(4):
                pieces += [piece(w_out, kg, cc * CC) for kg in range(4)]

        PS = ctx.enter_context(nc.psum_tensor("PS", [P, 8, 512], F32))

        def keep(name, shape, dt=F32):
            return ctx.enter_context(nc.sbuf_tensor(name, shape, dt))

        ident = keep("ident", [P, P])
        maskL = keep("maskL", [P, P])
        maskR = keep("maskR", [P, P])
        sel = keep("sel", [5, 2])
        sinks = keep("sinks", [P, 2, NH])
        pscale = keep("pscale", [P, PW // P])
        wr = keep("wr", [P, KT, NE])
        ss = keep("ss", [P, 2 * TT])
        st = keep("st", [P, 8])
        sm = keep("sm", [P, 2, 8])
        aff = keep("aff", [P, TT, NE])
        ss2 = keep("ss2", [P, TT, 4])
        rs2 = keep("rs2", [P, 6, TT])
        gate_s, gate_p = keep("gate_s", [P, NE]), keep("gate_p", [CAP_P, NE])
        idx_s, idx_p = keep("idx_s", [P, NE + 1], U32), keep("idx_p", [CAP_P, NE + 1], U32)
        ig_s, ig_p = keep("ig_s", [P, 1], U32), keep("ig_p", [CAP_P, 1], U32)
        ic_s, ic_p = keep("ic_s", [P, 1], U32), keep("ic_p", [CAP_P, 1], U32)

        mix = ExitStack()

        def mixt(name, shape, dt):
            return mix.enter_context(nc.sbuf_tensor(name, shape, dt))

        raw = mixt("raw", [P, NRAW, KG, CC], F32)
        whi = mixt("whi", [P, NSPLIT, KG, CC], F32R)
        wlo = mixt("wlo", [P, NSPLIT, KG, CC], F32R)
        ahi = mixt("ahi", [P, KT, 512], F32R)
        alo = mixt("alo", [P, KT, 512], F32R)
        off = [0]
        arena = [None]

        def carve(*shape):
            n = int(np.prod(shape))
            v = arena[0][:, off[0]:off[0] + n]
            off[0] += n
            assert off[0] <= arena[0].shape[1], off[0]
            if len(shape) == 2:
                v = v.rearrange("p (a b) -> p a b", a=shape[0])
            if len(shape) == 3:
                v = v.rearrange("p (a b c) -> p a b c", a=shape[0], b=shape[1])
            return v

        early = ExitStack()
        arena[0] = early.enter_context(nc.sbuf_tensor("arena_ab", [P, 58 * 256], F32))
        cond_s = early.enter_context(nc.sbuf_tensor("cond_s", [P, KT, P], F32R))
        xb = carve(2, D)
        tabA, tabS = carve(D), carve(D)
        stg = carve(4, 512)
        rtab = carve(2, 256)
        rt0 = off[0]
        rt = carve(4, 256)
        junk = carve(D // 2).bitcast(BF16)
        nmix = arena[0][:, rt0:rt0 + D]
        arow = carve(2, 512)
        mrow = carve(2, 512)
        cond_r = stg[:, 0, 0:P]
        cond_f = stg[:, 1, 0:32]
        early.close()
        arena[0] = mixt("arena_cd", [P, 66 * 256], F32)
        off[0] = 0
        vv = carve(9, KW)
        qq = carve(AW)
        pt0 = off[0]
        pp = carve(2, 7 * P)
        pT = carve(2, 7, P)
        ktm = arena[0][:, pt0:pt0 + 9 * KW].rearrange("p (a b) -> p a b", a=9)
        assert pt0 + 9 * KW <= 3 * D
        kT = carve(2 * 9 * P)
        qT = carve(NH, P)
        pin = carve(2, 512 + 2 * HALO)
        pa = carve(2, 512 + 2 * HALO)
        pb = carve(2, 512 + 2 * HALO)
        mixT = carve(2, 512)
        rcnt = carve(512)
        pw = carve(2, PG)
        off[0] = 0
        tabG, tabA2, tabS2 = carve(D), carve(D), carve(D)
        x1 = carve(4, D)
        h2T = carve(4, 4, P)
        nffn = h2T.rearrange("p a b c -> p (a b c)")
        junk2 = carve(CC // 2).bitcast(BF16)
        assert CH[-1][1] == 2
        cols = x1[:, 2:4, :].rearrange("p a b -> p (a b)")
        affT = cols[0:NE, 0:NS + NP_]
        top, topf = cols[0:NE, 2048:2048 + CAP], cols[0:NE, 2304:2304 + CAP]
        topi = cols[0:NE, 2560:2560 + CAP].bitcast(U32)
        mix.close()

        ring = keep("ring", [P, NRING, KG, CC])
        xT = keep("xT", [P, KT, CAP])
        hid = keep("hid", [P, FE // P, CAP])
        hg = keep("hg", [P, 2, KG * CAP])
        yT = keep("yT", [P, 2, KG * CAP])
        g_s, g_p = keep("g_s", [P, D]), keep("g_p", [CAP_P, D])
        y_s, y_p = keep("y_s", [P, D]), keep("y_p", [CAP_P, D])
        g2_s, g2_p = keep("g2_s", [P, D]), keep("g2_p", [CAP_P, D])

        raw_in = [sem(f"raw_in{i}") for i in range(NRAW)]
        hi_ok, lo_ok, used = sem("hi_ok"), sem("lo_ok"), sem("used")
        consts_in, cond_in, zero_ok = sem("consts_in"), sem("cond_in"), sem("zero_ok")
        cond_tr, cond_f_ok, cond_hi, cond_lo = sem("cond_tr"), sem("cond_f_ok"), sem("cond_hi"), sem("cond_lo")
        arow_ok, sel_ok, mrow_ok = sem("arow_ok"), sem("sel_ok"), sem("mrow_ok")
        brow_in = [sem(f"brow_in{i}") for i in range(2)]
        mod_out = [sem(f"mod_out{i}") for i in range(2)]
        nmix_in, tab_in, tab_ok = sem("nmix_in"), sem("tab_in"), sem("tab_ok")
        x_in = [sem(f"x_in{i}") for i in range(2)]
        sq_ok, root_ok, h_ok = sem("sq_ok"), sem("root_ok"), sem("h_ok")
        ms_ok = sem("ms_ok")
        h_tr, h_hi, h_lo = sem("h_tr"), sem("h_hi"), sem("h_lo")
        stg_ok, stg_out = sem("stg_ok"), sem("stg_out")
        rtab_in = sem("rtab_in")
        dve_step, pool_step = sem("dve_step"), sem("pool_step")
        kv_in, q_in, unit_pe = sem("kv_in"), sem("q_in"), sem("unit_pe")
        copied, m_hi, masked, exped, sank = sem("copied"), sem("m_hi"), sem("masked"), sem("exped"), sem("sank")
        p_ok, p_tr, pt_a, pt_v, pv_ok, o_hi, o_lo = (sem(n) for n in ("p_ok", "p_tr", "pt_a", "pt_v", "pv_ok", "o_hi", "o_lo"))
        pin_in, mixed = sem("pin_in"), sem("mixed")
        dtab_in, x1_in, dtab_ok = sem("dtab_in"), sem("x1_in"), sem("dtab_ok")
        x1_ok, x1_out, h2_ok, h2_out = (sem(n) for n in ("x1_ok", "x1_out", "h2_ok", "h2_out"))
        h2_tr, h2T_ok, lmax_ok, lexp_ok, aff_ok = (
            sem(n) for n in ("h2_tr", "h2T_ok", "lmax_ok", "lexp_ok", "aff_ok"))
        h2T_used, sq2_ok, ms2_ok, root2_ok = (sem(n) for n in ("h2T_used", "sq2_ok", "ms2_ok", "root2_ok"))
        aff_tr, affT_ok, top_ok, top_tr, gate_ok = (sem(n) for n in ("aff_tr", "affT_ok", "top_ok", "top_tr", "gate_ok"))
        ring_in = [sem(f"ring_in{i}") for i in range(NRING)]
        ring_free, silu_ok, hid_ok = sem("ring_free"), sem("silu_ok"), sem("hid_ok")
        yT_ok, x_tr, xs_ok, xp_ok, y_tr, ys_ok, yp_ok = (
            sem(n) for n in ("yT_ok", "x_tr", "xs_ok", "xp_ok", "y_tr", "ys_ok", "yp_ok"))
        gs_in, gp_in, ig_ok, ic_ok, y_free, s_out, p_out = (
            sem(n) for n in ("gs_in", "gp_in", "ig_ok", "ic_ok", "y_free", "s_out", "p_out"))
        g2_in, turn = sem("g2_in"), sem("turn")
        NF = 4
        f_in = [sem(f"f_in{i}") for i in range(NF)]
        f_out = [sem(f"f_out{i}") for i in range(NF)]
        nf_in, f_sq, f_ms, f_root, f_ok = sem("nf_in"), sem("f_sq"), sem("f_ms"), sem("f_root"), sem("f_ok")

        N_CONST = 11
        n_units = len(UNITS)
        n_heads = HEADS_BEFORE[-1] + (UNITS[-1][1] == "H")
        n_copies = COPIES_BEFORE[-1] + (UNITS[-1][1] != "H")
        unit_end = [max(k for k in range(n_units) if UNITS[k][0] == tc) + 1 for tc in range(3)]
        unit_start = [0, unit_end[0], unit_end[1]]

        def heads_by(k):
            return HEADS_BEFORE[k] if k < n_units else n_heads

        def copies_by(k):
            return COPIES_BEFORE[k] if k < n_units else n_copies

        def m_by(k):
            return sum(1 for u in UNITS[:k] if u[1] == "M")

        def kind(k):
            return UNITS[k][1] if 0 <= k < n_units else None

        def in_chunk(k, tc):
            return unit_start[tc] <= k < unit_end[tc]

        def keys(tc, b):
            loc, ml, mr = local_blocks(tc, b)
            ctx_n = 0 if CH[tc][2] else PAST // P
            return ctx_n, [ctx_n + k for k in loc], ml, mr

        def ada_pieces(a):
            return 4 * (a + 1) if a < ADA_A else 4 * (ADA_A + B_UNITS.index(("a", a, 0)) + 1)

        def win_pieces(tc, cc):
            return 4 * (ADA_A + B_UNITS.index(("w", tc, cc)) + 1)

        def m_unit(n):
            return [k for k in range(n_units) if UNITS[k][1] == "M"][n]

        def staged_by(n):
            return sum((CH[c // 5][1] if c % 5 < 3 else 4) for c in range(n))

        def x1_by(tc, cc):
            return sum(4 * CH[c][1] for c in range(tc)) + (cc + 1) * CH[tc][1]

        def x_loads(i):
            n = i // 2 + 1
            if i % 2 == 0 and i >= ST:
                n += 1
            return n

        def p_place(cn, z):
            return z if cn else 4 * z

        kv_by = [64, 128, 160]

        stores_by = [0]
        for tc, (t0, nt, cond) in enumerate(CH):
            for cc in range(5):
                if cc < 3:
                    n = nt + (2 * nt if cond and cc == 2 else 0)
                else:
                    n = 4
                stores_by.append(stores_by[-1] + n)

        block = ctx.enter_context(nc.Block())

        @block.sync
        def _(sp):
            for g, src in enumerate(pieces):
                if g >= NRAW:
                    sp.wait_ge(lo_ok, g - NRAW + 1)
                sp.dma_start(raw[:, g % NRAW], src).then_inc(raw_in[g % NRAW], 16)
            with sp.Fori(0, NE) as e:
                n = 0
                for w, nkg, ncc in ((w_gate, 4, 1), (w_up, 4, 1), (w_gate, 4, 2), (w_up, 4, 2), (w_down, 2, 0)):
                    for c in (range(D // CC) if ncc == 0 else [ncc - 1]):
                        for kg in range(nkg):
                            sp.wait_ge(ring_free, e * PIECES_E + n + 1)
                            src = w[bass.ds(e, 1), kg * KG * P:(kg + 1) * KG * P, c * CC:(c + 1) * CC]
                            sp.dma_start(ring[:, n % NRING],
                                         src.rearrange("e (r p) n -> p (e r) n", p=P)).then_inc(ring_in[n % NRING], 16)
                            n += 1

        @block.tensor
        def _(pe):
            g = [0]

            def next_piece():
                n = g[0]
                g[0] += 1
                pe.wait_ge(lo_ok, n + 1)
                return whi[:, n % NSPLIT], wlo[:, n % NSPLIT]

            def ada(a):
                if a:
                    pe.wait_ge(arow_ok, a)
                for kg in range(4):
                    hi, lo = next_piece()
                    for r in range(KG):
                        kt = kg * KG + r
                        nc.tensor.matmul(PS[:, 7, :], cond_s[:, kt, :], hi[:, r, :], start=(kt == 0), stop=False)
                        last = nc.tensor.matmul(PS[:, 7, :], cond_s[:, kt, :], lo[:, r, :],
                                                start=False, stop=(kt == KT - 1))
                    last.then_inc(used, 1)

            def select(a):
                pe.wait_ge(arow_ok, a + 1)
                pe.wait_ge(brow_in[a % 2], 16 * (a // 2 + 1))
                if a:
                    pe.wait_ge(mrow_ok, a)
                nc.tensor.matmul(PS[0:2, 6, :], sel[0:5, :], arow[0:5, a % 2, :], start=True, stop=True).then_inc(sel_ok, 1)

            pe.wait_ge(consts_in, 16 * N_CONST)
            pe.wait_ge(cond_in, 32)
            nc.tensor.transpose(PS[:, 0, 0:32], cond_r[0:32, :], ident[0:32, 0:32]).then_inc(cond_tr, 1)
            pe.wait_ge(cond_lo, 1)
            for a in range(ADA_A):
                ada(a)
                if a:
                    select(a - 1)
            select(ADA_A - 1)

            def turn_h(tc):
                t0, nt, cond = CH[tc]
                for i in range(t0, t0 + nt):
                    pe.wait_ge(h_ok, i + 1)
                    for q in range(4):
                        n = 4 * i + q
                        if n >= 2:
                            pe.wait_ge(h_lo, n - 1)
                        for r in range(4):
                            kt = 4 * q + r
                            last = nc.tensor.transpose(PS[:, 4 + n % 2, r * P:(r + 1) * P],
                                                       xb[:, i % 2, kt * P:(kt + 1) * P], ident[:])
                        last.then_inc(h_tr, 1)
                pe.wait_ge(h_lo, 4 * (t0 + nt))

            def project(tc, cc):
                nt = CH[tc][1]
                T = nt * P
                pe.wait_ge(stg_ok, staged_by(5 * tc + cc)) if tc or cc else None
                for kg in range(4):
                    hi, lo = next_piece()
                    for r in range(KG):
                        kt = kg * KG + r
                        for m in range(nt if cc < 3 else 4):
                            s = slice(m * P, (m + 1) * P)
                            if cc < 3:
                                ops = ((ahi[:, kt, s], hi[:, r, :]), (alo[:, kt, s], hi[:, r, :]),
                                       (ahi[:, kt, s], lo[:, r, :]))
                                out = PS[:, m, :]
                            else:
                                ops = ((hi[:, r, s], ahi[:, kt, 0:T]), (hi[:, r, s], alo[:, kt, 0:T]),
                                       (lo[:, r, s], ahi[:, kt, 0:T]))
                                out = PS[:, m, 0:T]
                            for z, (w, x) in enumerate(ops):
                                last = nc.tensor.matmul(out, w, x, start=(kt == 0 and z == 0),
                                                        stop=(kt == KT - 1 and z == 2))
                    last.then_inc(used, 1)

            for u, (kd, n, cc) in enumerate(B_UNITS):
                if kd == "w":
                    if cc == 0:
                        turn_h(n)
                    project(n, cc)
                else:
                    ada(n)
                if u and B_UNITS[u - 1][0] == "a":
                    select(B_UNITS[u - 1][1])

            for tc, (t0, nt, cond) in enumerate(CH):
                if tc == 0:
                    pe.wait_ge(stg_ok, staged_by(15))
                    pe.wait_ge(mrow_ok, NADA)
                else:
                    pe.wait_ge(x1_ok, 16 * tc)
                    pe.wait_ge(h2T_ok, 4 * t0)
                nk = 9 if cond == 0 else 2
                for k in range(unit_start[tc], unit_end[tc] + 2):
                    if k < unit_end[tc]:
                        _, kd, b, h = UNITS[k]
                        pair = 2 * (k % 2)
                        if k - 2 >= unit_start[tc]:
                            if kind(k - 2) == "H":
                                pe.wait_ge(exped, heads_by(k - 1))
                            else:
                                pe.wait_ge(copied, copies_by(k - 1))
                        flat = PS[:, pair:pair + 2, :].rearrange("p a b -> p (a b)")
                        if kd == "K":
                            pe.wait_ge(kv_in, kv_by[tc])
                            for z in range(h * 8, min(h * 8 + 8, 2 * nk)):
                                kv, kb = z // nk, z % nk
                                last = nc.tensor.transpose(flat[:, (z % 8) * P:(z % 8 + 1) * P],
                                                           ktm[:, kb, kv * P:(kv + 1) * P], ident[:])
                        elif kd == "Q":
                            pe.wait_ge(q_in, 16 * (t0 + b + 1))
                            for z in range(NH):
                                last = nc.tensor.transpose(flat[:, z * P:(z + 1) * P], qq[:, z * P:(z + 1) * P], ident[:])
                        elif kd == "H":
                            if h == 0:
                                pe.wait_ge(copied, copies_by(k))
                            cn, loc, _, _ = keys(tc, b)
                            kv = h // (NH // NKV)
                            base = kv * nk * P
                            if cn:
                                nc.tensor.matmul(flat[:, 0:cn * P], qT[:, h, :], kT[:, base:base + cn * P],
                                                 start=True, stop=True)
                            l0 = base + loc[0] * P
                            last = nc.tensor.matmul(flat[:, cn * P:(cn + len(loc)) * P], qT[:, h, :],
                                                    kT[:, l0:l0 + len(loc) * P], start=True, stop=True)
                        else:
                            gi = 4 * tc + h
                            pe.wait_ge(mixed, gi + 1)
                            for m in range(2):
                                for z in range(2):
                                    last = nc.tensor.matmul(PS[:, pair + m, 0:nt * P], pw[:, z, m * P:(m + 1) * P],
                                                            mixT[:, z, 0:nt * P], start=(z == 0), stop=(z == 1))
                        last.then_inc(unit_pe, 1)
                    if in_chunk(k - 2, tc) and kind(k - 2) == "H":
                        _, _, b, h = UNITS[k - 2]
                        hc = heads_by(k - 2)
                        cn, loc, _, _ = keys(tc, b)
                        places = list(range(cn)) + loc
                        pe.wait_ge(pt_a, hc + 1)
                        pe.wait_ge(pt_v, hc + 1)
                        if tc and k - 2 < unit_start[tc] + 12:
                            pe.wait_ge(lexp_ok, t0)
                        if h % 4 == 0 and hc >= 8:
                            pe.wait_ge(o_lo, hc // 4 - 1)
                        for z, kb in enumerate(places):
                            last = nc.tensor.matmul(PS[:, 6 + h // 4, (h % 4) * P:(h % 4 + 1) * P],
                                                    vv[:, kb, (h // 4) * P:(h // 4 + 1) * P], pT[:, hc % 2, z, :],
                                                    start=(z == 0), stop=(z == len(places) - 1))
                        last.then_inc(pv_ok, 1)
                    if in_chunk(k - 1, tc) and kind(k - 1) == "H":
                        _, _, b, h = UNITS[k - 1]
                        hc = heads_by(k - 1)
                        cn, loc, _, _ = keys(tc, b)
                        pe.wait_ge(p_ok, hc + 1)
                        if hc:
                            pe.wait_ge(pt_a, hc)
                            pe.wait_ge(pt_v, hc)
                        flat = PS[:, 4:6, :].rearrange("p a b -> p (a b)")
                        for z in range(cn + len(loc)):
                            c0 = p_place(cn, z) * P
                            last = nc.tensor.transpose(flat[:, c0:c0 + P], pp[:, hc % 2, z * P:(z + 1) * P], ident[:])
                        last.then_inc(p_tr, 1)

                pe.wait_ge(exped, heads_by(unit_end[tc]))
                pe.wait_ge(copied, copies_by(unit_end[tc]))
                pe.wait_ge(o_lo, heads_by(unit_end[tc]) // 4)
                pe.wait_ge(pt_a, heads_by(unit_end[tc]))
                pe.wait_ge(pt_v, heads_by(unit_end[tc]))
                if tc == 2:
                    pe.wait_ge(aff_ok, ST)
                    for i in range(ST):
                        last = nc.tensor.transpose(PS[0:NE, 2 + i // 4, (i % 4) * P:(i % 4 + 1) * P], aff[:, i, :], ident[:])
                    last.then_inc(aff_tr, 1)
                for cc in range(4):
                    n = 4 * tc + cc
                    if cc >= 2:
                        pe.wait_ge(x1_ok, x1_by(tc, cc - 2))
                    for kg in range(4):
                        hi, lo = next_piece()
                        for r in range(KG):
                            kt = kg * KG + r
                            for m in range(nt):
                                s = slice(m * P, (m + 1) * P)
                                for z, (w, x) in enumerate(((ahi[:, kt, s], hi[:, r, :]), (alo[:, kt, s], hi[:, r, :]),
                                                            (ahi[:, kt, s], lo[:, r, :]))):
                                    last = nc.tensor.matmul(PS[:, 4 * (cc % 2) + m, :], w, x,
                                                            start=(kt == 0 and z == 0), stop=(kt == KT - 1 and z == 2))
                        last.then_inc(used, 1)
                pe.wait_ge(x1_ok, x1_by(tc, 3))
                if tc == 2:
                    pe.wait_ge(affT_ok, 1)
                for n in range(4 * t0, 4 * (t0 + nt) + 1):
                    if n < 4 * (t0 + nt):
                        pe.wait_ge(h2_ok, n // 4 + 1)
                        if n >= 4:
                            pe.wait_ge(h2T_ok, n - 3)
                        for r in range(4):
                            kt = 4 * (n % 4) + r
                            last = nc.tensor.transpose(PS[:, n % 4, r * P:(r + 1) * P],
                                                       x1[:, n // 4 - t0, kt * P:(kt + 1) * P], ident[:])
                        last.then_inc(h2_tr, 1)
                    if n > 4 * t0:
                        i, q = (n - 1) // 4, (n - 1) % 4
                        pe.wait_ge(h2T_ok, n)
                        if q == 0 and i >= 2:
                            pe.wait_ge(lexp_ok, i - 1)
                        for r in range(4):
                            kt = 4 * q + r
                            last = nc.tensor.matmul(PS[:, 6 + i % 2, 0:NE], h2T[:, q, r, :], wr[:, kt, :],
                                                    start=(kt == 0), stop=(kt == KT - 1))
                        last.then_inc(h2T_used, 1)

            pe.wait_ge(aff_ok, TT)
            for i in range(ST, TT):
                last = nc.tensor.transpose(PS[0:NE, 4, (i - ST) * P:(i - ST + 1) * P], aff[:, i, :], ident[:])
            last.then_inc(aff_tr, 1)
            nc.tensor.nop().then_inc(ring_free, NRING)
            pe.wait_ge(top_ok, 1)
            nc.tensor.transpose(PS[:, 0, 0:NE], top[:, 0:CAP_S], ident[0:NE, 0:NE])
            nc.tensor.transpose(PS[:, 0, NE:2 * NE], topf[:, 0:CAP_S], ident[0:NE, 0:NE])
            nc.tensor.transpose(PS[0:CAP_P, 1, 0:NE], top[:, CAP_S:CAP], ident[0:NE, 0:NE])
            nc.tensor.transpose(PS[0:CAP_P, 1, NE:2 * NE], topf[:, CAP_S:CAP], ident[0:NE, 0:NE]).then_inc(top_tr, 1)
            pe.wait_ge(gate_ok, 1)

            def turn_tokens(j):
                for r in range(4):
                    kt = 4 * j + r
                    nc.tensor.transpose(PS[:, 4, r * P:(r + 1) * P], g_s[:, kt * P:(kt + 1) * P], ident[:])
                    last = nc.tensor.transpose(PS[:, 5, r * CAP_P:(r + 1) * CAP_P], g_p[:, kt * P:(kt + 1) * P],
                                               ident[0:CAP_P, 0:CAP_P])
                last.then_inc(x_tr, 1)

            pe.wait_ge(affT_ok, 2)
            pe.wait_ge(gs_in, 16)
            pe.wait_ge(gp_in, 16)
            for j in range(4):
                if j:
                    pe.wait_ge(xs_ok, j)
                    pe.wait_ge(xp_ok, j)
                turn_tokens(j)

            with pe.Fori(0, NE) as e:
                def banks(b, w, x, kt, last_kt):
                    for m in range(4):
                        out = PS[:, b + m // 2, (m % 2) * CAP:(m % 2 + 1) * CAP]
                        ins = nc.tensor.matmul(out, w[:, m * P:(m + 1) * P], x, start=(kt == 0 and m % 2 == 0),
                                               stop=(kt == last_kt), skip_group_check=True)
                    return ins

                n = 0

                def take(n):
                    pe.wait_ge(ring_in[n % NRING], e * (16 * PIECES_E // NRING) + 16 * (n // NRING + 1))
                    return ring[:, n % NRING]

                for half in range(2):
                    for up in range(2):
                        if half == 1 and up == 0:
                            pe.wait_ge(silu_ok, e * 2 + 1)
                        if half == 1 and up == 1:
                            pe.wait_ge(hid_ok, e * 2 + 1)
                        for kg in range(4):
                            if half == 0 and up == 0:
                                pe.wait_ge(xs_ok, e * 4 + kg + 1)
                                pe.wait_ge(xp_ok, e * 4 + kg + 1)
                            w = take(n)
                            for r in range(KG):
                                kt = kg * KG + r
                                last = banks(2 * up, w[:, r, :], xT[:, kt, :], kt, KT - 1)
                            last.then_inc(ring_free, 1)
                            n += 1
                for cc in range(4):
                    if cc == 0:
                        pe.wait_ge(silu_ok, e * 2 + 2)
                        pe.wait_ge(hid_ok, e * 2 + 1)
                    if cc == 1:
                        pe.wait_ge(hid_ok, e * 2 + 2)
                    if cc >= 2:
                        pe.wait_ge(yT_ok, e * 4 + cc - 1)
                    for kg in range(2):
                        if cc == 0 and kg == 1:
                            pe.wait_ge(hid_ok, e * 2 + 2)
                        w = take(n)
                        for r in range(KG):
                            kt = kg * KG + r
                            last = banks(2 * (cc % 2), w[:, r, :], hid[:, kt, :], kt, FE // P - 1)
                        last.then_inc(ring_free, 1)
                        n += 1
                    if cc == 0:
                        pe.wait_ge(gs_in, e * 16 + 32)
                        pe.wait_ge(gp_in, e * 16 + 32)
                    pe.wait_ge(xs_ok, e * 4 + 4 + cc)
                    pe.wait_ge(xp_ok, e * 4 + 4 + cc)
                    turn_tokens(cc)
                    for c in ([cc - 1] if cc < 3 else [2, 3]):
                        if c < 0:
                            continue
                        pe.wait_ge(yT_ok, e * 4 + c + 1)
                        if c:
                            pe.wait_ge(ys_ok, e * 4 + c)
                            pe.wait_ge(yp_ok, e * 4 + c)
                        for m in range(4):
                            y = yT[:, c % 2, m * CAP:(m + 1) * CAP]
                            nc.tensor.transpose(PS[:, 6, m * P:(m + 1) * P], y[:, 0:CAP_S], ident[:])
                            last = nc.tensor.transpose(PS[0:CAP_P, 7, m * P:(m + 1) * P], y[:, CAP_S:CAP], ident[:])
                        last.then_inc(y_tr, 1)

        @block.scalar
        def _(act):
            g = [0]
            steps = [0]

            def split_hi():
                n = g[0]
                g[0] += 1
                act.wait_ge(raw_in[n % NRAW], 16 * (n // NRAW + 1))
                if n >= NSPLIT:
                    act.wait_ge(used, n - NSPLIT + 1)
                nc.scalar.activation(whi[:, n % NSPLIT], raw[:, n % NRAW], ACT.Copy).then_inc(hi_ok, 1)

            def ada_rows(a):
                act.wait_ge(used, ada_pieces(a))
                if a >= 2:
                    act.wait_ge(sel_ok, a - 1)
                nc.scalar.activation(arow[0:4, a % 2, :], PS[0:4, 7, :], ACT.Copy).then_inc(arow_ok, 1)

            def mod_rows(a):
                act.wait_ge(sel_ok, a + 1)
                if a >= 2:
                    act.wait_ge(mod_out[a % 2], 16 * (a // 2))
                nc.scalar.activation(mrow[0:2, a % 2, :], PS[0:2, 6, :], ACT.Copy).then_inc(mrow_ok, 1)

            act.wait_ge(cond_tr, 1)
            nc.scalar.activation(cond_f, PS[:, 0, 0:32], ACT.Silu).then_inc(cond_f_ok, 1)
            act.wait_ge(cond_f_ok, 1)
            act.wait_ge(zero_ok, 1)
            cf = cond_f.rearrange("p (c t) -> p t c", c=2)
            nc.scalar.activation(cond_s[:, :, 0:2], cf, ACT.Copy).then_inc(cond_hi, 1)
            for a in range(ADA_A):
                for kg in range(4):
                    split_hi()
                    if kg == 1 and a:
                        ada_rows(a - 1)
                        if a > 1:
                            mod_rows(a - 2)
            ada_rows(ADA_A - 1)
            mod_rows(ADA_A - 2)
            mod_rows(ADA_A - 1)

            def stage(tc, cc):
                nt = CH[tc][1]
                act.wait_ge(used, win_pieces(tc, cc))
                if tc or cc:
                    act.wait_ge(stg_out, 16 * stores_by[5 * tc + cc])
                for m in range(nt if cc < 3 else 4):
                    w = 512 if cc < 3 else nt * P
                    nc.scalar.activation(stg[:, m, 0:w], PS[:, m, 0:w], ACT.Copy).then_inc(stg_ok, 1)

            def square(i):
                act.wait_ge(x_in[i % 2], 16 * x_loads(i))
                if i:
                    act.wait_ge(sq_ok, i)
                if i == 0:
                    act.wait_ge(tab_ok, 1)
                nc.scalar.activation(junk, xb[:, i % 2, :], ACT.Square, accum_out=ss[:, i:i + 1]).then_inc(sq_ok, 1)
                act.wait_ge(ms_ok, i + 1)
                nc.scalar.activation(st[:, 1:2], st[:, 0:1], ACT.Sqrt).then_inc(root_ok, 1)

            def turned_hi(i, t0):
                for q in range(4):
                    n = 4 * i + q
                    act.wait_ge(h_tr, n + 1)
                    nc.scalar.activation(ahi[:, 4 * q:4 * q + 4, (i - t0) * P:(i - t0 + 1) * P],
                                         PS[:, 4 + n % 2, :].rearrange("p (a b) -> p a b", a=4), ACT.Copy).then_inc(h_hi, 1)

            def finish(u):
                kd, n, cc = B_UNITS[u]
                if kd == "w":
                    stage(n, cc)
                else:
                    ada_rows(n)
                if u and B_UNITS[u - 1][0] == "a":
                    mod_rows(B_UNITS[u - 1][1])

            square(0)
            square(1)
            for u, (kd, n, cc) in enumerate(B_UNITS):
                if kd == "w" and cc == 0:
                    t0, nt, cond = CH[n]
                    for j in range(nt):
                        turned_hi(t0 + j, t0)
                        if j + 2 < nt:
                            square(t0 + j + 2)
                for kg in range(4):
                    split_hi()
                    if kg == 1 and u:
                        finish(u - 1)
                if kd == "w" and cc == 3 and n < 2:
                    square(CH[n + 1][0])
                    square(CH[n + 1][0] + 1)
            finish(len(B_UNITS) - 1)

            for tc, (t0, nt, cond) in enumerate(CH):
                for k in range(unit_start[tc], unit_end[tc] + 2):
                    if k < unit_end[tc] and kind(k) == "H":
                        _, _, b, h = UNITS[k]
                        hc = heads_by(k)
                        cn, loc, _, _ = keys(tc, b)
                        w = (cn + len(loc)) * P
                        pair = 2 * (k % 2)
                        act.wait_ge(masked, hc + 1)
                        if hc >= 2:
                            act.wait_ge(p_tr, hc - 1)
                        nc.scalar.activation(pp[:, hc % 2, 0:w], PS[:, pair:pair + 2, :].rearrange("p a b -> p (a b)")[:, 0:w],
                                             ACT.Exp, bias=sm[:, hc % 2, 1:2], scale=SCALE,
                                             accum_out=sm[:, hc % 2, 2:3]).then_inc(exped, 1)
                        nc.scalar.activation(sm[:, hc % 2, 3:4], sinks[:, 0, h:h + 1], ACT.Exp,
                                             bias=sm[:, hc % 2, 1:2]).then_inc(sank, 1)
                    if k < unit_end[tc] and kind(k) == "M":
                        gi = UNITS[k][3]
                        pair = 2 * (k % 2)
                        act.wait_ge(unit_pe, k + 1)
                        for m in range(2):
                            ct = 2 * gi + m
                            nc.scalar.activation(ahi[:, NH + ct, 0:nt * P], PS[:, pair + m, 0:nt * P], ACT.Copy,
                                                 scale=pscale[:, ct:ct + 1]).then_inc(m_hi, 1)
                    if in_chunk(k - 1, tc) and kind(k - 1) == "H":
                        hc = heads_by(k - 1)
                        cn, loc, _, _ = keys(tc, UNITS[k - 1][2])
                        act.wait_ge(p_tr, hc + 1)
                        if hc >= 2:
                            act.wait_ge(pv_ok, hc - 1)
                        w = min(4, cn + len(loc))
                        if cn == 0:
                            w = 1
                        nc.scalar.activation(pT[:, hc % 2, 0:w, :], PS[:, 4, 0:w * P].rearrange("p (a b) -> p a b", a=w),
                                             ACT.Copy).then_inc(pt_a, 1)
                    if in_chunk(k - 2, tc) and kind(k - 2) == "H" and UNITS[k - 2][3] % 4 == 3:
                        _, _, b, h = UNITS[k - 2]
                        act.wait_ge(pv_ok, heads_by(k - 2) + 1)
                        nc.scalar.activation(ahi[:, h - 3:h + 1, b * P:(b + 1) * P],
                                             PS[:, 6 + h // 4, :].rearrange("p (a b) -> p a b", a=4), ACT.Copy).then_inc(o_hi, 1)
                if tc == 2:
                    act.wait_ge(aff_tr, 1)
                    act.wait_ge(h2_out, 16 * ST)
                    act.wait_ge(x1_out, 16 * 8)
                    nc.scalar.activation(affT[:, 0:NS], PS[0:NE, 2:4, :].rearrange("p a b -> p (a b)"), ACT.Copy).then_inc(affT_ok, 1)

                def squares(cc):
                    for m in range(nt):
                        act.wait_ge(x1_ok, x1_by(tc, cc) - nt + m + 1)
                        n = 4 * (4 * tc + cc) + m if tc < 2 else 32 + 2 * cc + m
                        if n:
                            act.wait_ge(sq2_ok, n)
                        nc.scalar.activation(junk2, x1[:, m, cc * CC:(cc + 1) * CC], ACT.Square,
                                             accum_out=ss2[:, t0 + m, cc:cc + 1]).then_inc(sq2_ok, 1)

                for cc in range(4):
                    for kg in range(4):
                        split_hi()
                        if kg == 2 and cc:
                            squares(cc - 1)
                squares(3)
                act.wait_ge(ms2_ok, tc + 1)
                nc.scalar.activation(rs2[:, 1, t0:t0 + nt], rs2[:, 0, t0:t0 + nt], ACT.Sqrt).then_inc(root2_ok, 1)

                def router_exp(i):
                    act.wait_ge(lmax_ok, i + 1)
                    nc.scalar.activation(aff[:, i, :], PS[:, 6 + i % 2, 0:NE], ACT.Exp, bias=rs2[:, 4, i:i + 1],
                                         accum_out=rs2[:, 5, i:i + 1]).then_inc(lexp_ok, 1)

                for i in range(t0, t0 + nt):
                    for q in range(4):
                        n = 4 * i + q
                        act.wait_ge(h2_tr, n + 1)
                        if n >= 4:
                            act.wait_ge(h2T_used, n - 3)
                        nc.scalar.activation(h2T[:, q], PS[:, q, :].rearrange("p (a b) -> p a b", a=4), ACT.Copy).then_inc(h2T_ok, 1)
                    if i > t0:
                        router_exp(i - 1)
                router_exp(t0 + nt - 1)

            act.wait_ge(aff_tr, 2)
            nc.scalar.activation(affT[:, NS:NS + NP_], PS[0:NE, 4, 0:NP_], ACT.Copy).then_inc(affT_ok, 1)

            def take_tokens(j):
                nc.scalar.activation(xT[:, 4 * j:4 * j + 4, 0:CAP_S], PS[:, 4, :].rearrange("p (a b) -> p a b", a=4),
                                     ACT.Copy).then_inc(xs_ok, 1)

            for j in range(4):
                act.wait_ge(x_tr, j + 1)
                take_tokens(j)

            with act.Fori(0, NE) as e:
                for half in range(2):
                    act.wait_ge(ring_free, e * PIECES_E + NRING + 8 * half + 4)
                    nc.scalar.activation(hg[:, half, :].rearrange("p (a b) -> p a b", a=2), PS[:, 0:2, 0:2 * CAP],
                                         ACT.Silu).then_inc(silu_ok, 1)
                for cc in range(4):
                    b = 2 * (cc % 2)
                    act.wait_ge(ring_free, e * PIECES_E + NRING + 18 + 2 * cc)
                    nc.scalar.activation(yT[:, cc % 2, :].rearrange("p (a b) -> p a b", a=2), PS[:, b:b + 2, 0:2 * CAP],
                                         ACT.Copy).then_inc(yT_ok, 1)
                    act.wait_ge(x_tr, e * 4 + 5 + cc)
                    take_tokens(cc)

            for i in range(TT):
                act.wait_ge(f_in[i % NF], 16 * (i // NF + 1))
                if i >= NF:
                    act.wait_ge(f_out[i % NF], 16 * (i // NF))
                nc.scalar.activation(ring[:, NF + i % NF].rearrange("p a b -> p (a b)"),
                                     ring[:, i % NF].rearrange("p a b -> p (a b)"), ACT.Square,
                                     accum_out=ss[:, TT + i:TT + i + 1]).then_inc(f_sq, 1)
                act.wait_ge(f_ms, i + 1)
                nc.scalar.activation(st[:, 1:2], st[:, 0:1], ACT.Sqrt).then_inc(f_root, 1)

        @block.vector
        def _(dve):
            g = [0]
            steps = [0]

            def link(ins):
                steps[0] += 1
                ins.then_inc(dve_step, 1)
                dve.wait_ge(dve_step, steps[0])

            def split_lo():
                n = g[0]
                g[0] += 1
                dve.wait_ge(hi_ok, n + 1)
                nc.vector.tensor_tensor(wlo[:, n % NSPLIT], raw[:, n % NRAW], whi[:, n % NSPLIT].bitcast(F32),
                                        ALU.subtract).then_inc(lo_ok, 1)

            def rstd(col, n, sq, ms, root):
                dve.wait_ge(sq, n)
                nc.vector.tensor_scalar(st[:, 0:1], ss[:, col:col + 1], 1.0 / D, EPS, ALU.mult, ALU.add).then_inc(ms, 1)
                dve.wait_ge(root, n)
                link(nc.vector.reciprocal(st[:, 2:3], st[:, 1:2]))
                link(nc.vector.scalar_tensor_tensor(out=st[:, 3:4], in0=st[:, 2:3], scalar=st[:, 2:3], in1=st[:, 0:1],
                                                    op0=ALU.mult, op1=ALU.mult))
                link(nc.vector.tensor_scalar(st[:, 3:4], st[:, 3:4], -0.5, 1.5, ALU.mult, ALU.add))
                link(nc.vector.tensor_tensor(st[:, 4:5], st[:, 2:3], st[:, 3:4], ALU.mult))

            nc.vector.memset(cond_s[:].bitcast(F32), 0.0).then_inc(zero_ok, 1)
            dve.wait_ge(cond_hi, 1)
            cf = cond_f.rearrange("p (c t) -> p t c", c=2)
            nc.vector.tensor_tensor(cond_s[:, :, 2:4], cf, cond_s[:, :, 0:2].bitcast(F32), ALU.subtract).then_inc(cond_lo, 1)
            for _ in range(4 * ADA_A):
                split_lo()

            def scale_table(n):
                dve.wait_ge(tab_in, 16 * (2 * n + 2))
                if n:
                    dve.wait_ge(x_in[0], 16 * (x_loads(ST) - 1))
                else:
                    dve.wait_ge(nmix_in, 16)
                w = xb[:, 0, :] if n else nmix
                nc.vector.scalar_tensor_tensor(out=tabA, in0=tabA, scalar=1.0, in1=w,
                                               op0=ALU.add, op1=ALU.mult).then_inc(tab_ok, 1)
                dve.wait_ge(tab_ok, n + 1)

            def modulated(i):
                rstd(i, i + 1, sq_ok, ms_ok, root_ok)
                x = xb[:, i % 2, :]
                link(nc.vector.scalar_tensor_tensor(out=x, in0=x, scalar=st[:, 4:5], in1=tabA,
                                                    op0=ALU.mult, op1=ALU.mult))
                nc.vector.tensor_tensor(x, x, tabS, ALU.add).then_inc(h_ok, 1)

            def turned_lo(i, t0):
                for q in range(4):
                    n = 4 * i + q
                    dve.wait_ge(h_hi, n + 1)
                    s = (slice(None), slice(4 * q, 4 * q + 4), slice((i - t0) * P, (i - t0 + 1) * P))
                    nc.vector.tensor_tensor(alo[s], PS[:, 4 + n % 2, :].rearrange("p (a b) -> p a b", a=4),
                                            ahi[s].bitcast(F32), ALU.subtract).then_inc(h_lo, 1)

            scale_table(0)
            modulated(0)
            modulated(1)
            for u, (kd, n, cc) in enumerate(B_UNITS):
                if kd == "w" and cc == 0:
                    t0, nt, cond = CH[n]
                    for j in range(nt):
                        turned_lo(t0 + j, t0)
                        if j + 2 < nt:
                            modulated(t0 + j + 2)
                for _ in range(4):
                    split_lo()
                if kd == "w" and cc == 3 and n < 2:
                    if CH[n + 1][2]:
                        scale_table(1)
                    modulated(CH[n + 1][0])
                    modulated(CH[n + 1][0] + 1)

            for tc, (t0, nt, cond) in enumerate(CH):
                for k in range(unit_start[tc], unit_end[tc] + 2):
                    if in_chunk(k - 1, tc) and kind(k - 1) == "H":
                        hc = heads_by(k - 1)
                        cn, loc, _, _ = keys(tc, UNITS[k - 1][2])
                        w = (cn + len(loc)) * P
                        s = sm[:, hc % 2, :]
                        dve.wait_ge(sank, hc + 1)
                        link(nc.vector.tensor_tensor(s[:, 4:5], s[:, 2:3], s[:, 3:4], ALU.add))
                        link(nc.vector.reciprocal(s[:, 5:6], s[:, 4:5]))
                        nc.vector.tensor_scalar(pp[:, hc % 2, 0:w], pp[:, hc % 2, 0:w], s[:, 5:6], None,
                                                ALU.mult).then_inc(p_ok, 1)
                    if k < unit_end[tc]:
                        _, kd, b, h = UNITS[k]
                        pair = 2 * (k % 2)
                        flat = PS[:, pair:pair + 2, :].rearrange("p a b -> p (a b)")
                        dve.wait_ge(unit_pe, k + 1)
                        if kd == "H":
                            hc = heads_by(k)
                            cn, loc, ml, mr = keys(tc, b)
                            w = (cn + len(loc)) * P
                            s = sm[:, hc % 2, :]
                            if ml:
                                v = flat[:, cn * P:(cn + 1) * P]
                                link(nc.vector.tensor_tensor(v, v, maskL[:], ALU.add))
                            if mr:
                                v = flat[:, w - P:w]
                                link(nc.vector.tensor_tensor(v, v, maskR[:], ALU.add))
                            link(nc.vector.reduce_max(s[:, 0:1], flat[:, 0:w], AXX))
                            nc.vector.tensor_scalar(s[:, 1:2], s[:, 0:1], -SCALE, sinks[:, 1, h:h + 1],
                                                    ALU.mult, ALU.min).then_inc(masked, 1)
                        elif kd == "K":
                            nk = 9 if cond == 0 else 2
                            if tc:
                                dve.wait_ge(h2_out, 16 * t0)
                            z0, z1 = h * 8, min(h * 8 + 8, 2 * nk)
                            nc.vector.tensor_copy(kT[:, z0 * P:z1 * P], flat[:, 0:(z1 - z0) * P]).then_inc(copied, 1)
                        elif kd == "Q":
                            nc.vector.tensor_copy(qT.rearrange("p a b -> p (a b)"), flat).then_inc(copied, 1)
                        else:
                            dve.wait_ge(m_hi, 2 * (m_by(k) + 1))
                            for m in range(2):
                                ct = 2 * h + m
                                ins = nc.vector.scalar_tensor_tensor(
                                    out=alo[:, NH + ct, 0:nt * P], in0=PS[:, pair + m, 0:nt * P],
                                    scalar=pscale[:, ct:ct + 1], in1=ahi[:, NH + ct, 0:nt * P].bitcast(F32),
                                    op0=ALU.mult, op1=ALU.subtract)
                            ins.then_inc(copied, 1)
                    if in_chunk(k - 1, tc) and kind(k - 1) == "H":
                        hc = heads_by(k - 1)
                        cn, loc, _, _ = keys(tc, UNITS[k - 1][2])
                        dve.wait_ge(p_tr, hc + 1)
                        if hc >= 2:
                            dve.wait_ge(pv_ok, hc - 1)
                        z0 = 4 if cn else 1
                        z1 = cn + len(loc)
                        flat = PS[:, 4:6, :].rearrange("p a b -> p (a b)")
                        c0 = p_place(cn, z0) * P
                        nc.vector.tensor_copy(pT[:, hc % 2, z0:z1, :],
                                              flat[:, c0:c0 + (z1 - z0) * P].rearrange("p (a b) -> p a b", b=P)).then_inc(pt_v, 1)
                    if in_chunk(k - 2, tc) and kind(k - 2) == "H" and UNITS[k - 2][3] % 4 == 3:
                        _, _, b, h = UNITS[k - 2]
                        dve.wait_ge(o_hi, (heads_by(k - 2) + 1) // 4)
                        s = (slice(None), slice(h - 3, h + 1), slice(b * P, (b + 1) * P))
                        nc.vector.tensor_tensor(alo[s], PS[:, 6 + h // 4, :].rearrange("p (a b) -> p a b", a=4),
                                                ahi[s].bitcast(F32), ALU.subtract).then_inc(o_lo, 1)

                def residual(cc):
                    dve.wait_ge(used, D0 + 4 * (4 * tc + cc + 1))
                    s = slice(cc * CC, (cc + 1) * CC)
                    for m in range(nt):
                        v = PS[:, 4 * (cc % 2) + m, :]
                        link(nc.vector.tensor_tensor(v, v, tabG[:, s], ALU.mult))
                        nc.vector.tensor_tensor(x1[:, m, s], x1[:, m, s], v, ALU.add).then_inc(x1_ok, 1)

                def top_round(c0, c1, k):
                    v, s = affT[:, c0:c1], slice(k, k + 8)
                    link(nc.vector.max(top[:, s], v))
                    link(nc.vector.max_index(topi[:, s], top[:, s], v))
                    link(nc.vector.match_replace(v, top[:, s], v, -1.0))

                for cc in range(4):
                    for kg in range(4):
                        split_lo()
                        if kg == 1 and cc:
                            if cc == 1:
                                dve.wait_ge(dtab_in, 16 * (4 * tc + 4))
                                dve.wait_ge(x1_in, 16 * (t0 + nt))
                            residual(cc - 1)
                        if tc == 2:
                            if cc == 0 and kg == 0:
                                dve.wait_ge(affT_ok, 1)
                            top_round(0, NS, 8 * (4 * cc + kg))
                nc.vector.scalar_tensor_tensor(out=tabA2, in0=tabA2, scalar=1.0, in1=nffn, op0=ALU.add,
                                               op1=ALU.mult).then_inc(dtab_ok, 1)
                residual(3)
                cs = slice(t0, t0 + nt)
                dve.wait_ge(sq2_ok, x1_by(tc, 3))
                link(nc.vector.reduce_sum(rs2[:, 0, cs], ss2[:, cs, :], AXX))
                nc.vector.tensor_scalar(rs2[:, 0, cs], rs2[:, 0, cs], 1.0 / D, EPS, ALU.mult, ALU.add).then_inc(ms2_ok, 1)
                dve.wait_ge(root2_ok, tc + 1)
                link(nc.vector.reciprocal(rs2[:, 2, cs], rs2[:, 1, cs]))
                link(nc.vector.tensor_tensor(rs2[:, 3, cs], rs2[:, 2, cs], rs2[:, 2, cs], ALU.mult))
                link(nc.vector.tensor_tensor(rs2[:, 3, cs], rs2[:, 3, cs], rs2[:, 0, cs], ALU.mult))
                link(nc.vector.tensor_scalar(rs2[:, 3, cs], rs2[:, 3, cs], -0.5, 1.5, ALU.mult, ALU.add))
                link(nc.vector.tensor_tensor(rs2[:, 2, cs], rs2[:, 2, cs], rs2[:, 3, cs], ALU.mult))
                dve.wait_ge(x1_out, 16 * 4 * (tc + 1))
                dve.wait_ge(dtab_ok, tc + 1)

                def router_max(i):
                    dve.wait_ge(h2T_used, 4 * i + 4)
                    nc.vector.tensor_reduce(rs2[:, 4, i:i + 1], PS[:, 6 + i % 2, 0:NE], AXX, ALU.max,
                                            negate=True).then_inc(lmax_ok, 1)

                for i in range(t0, t0 + nt):
                    x = x1[:, i - t0, :]
                    link(nc.vector.scalar_tensor_tensor(out=x, in0=x, scalar=rs2[:, 2, i:i + 1], in1=tabA2,
                                                        op0=ALU.mult, op1=ALU.mult))
                    nc.vector.tensor_tensor(x, x, tabS2, ALU.add).then_inc(h2_ok, 1)
                    if i > t0:
                        router_max(i - 1)
                router_max(t0 + nt - 1)
                dve.wait_ge(lexp_ok, t0 + nt)
                link(nc.vector.reciprocal(rs2[:, 3, cs], rs2[:, 5, cs]))
                for i in range(t0, t0 + nt):
                    nc.vector.tensor_scalar(aff[:, i, :], aff[:, i, :], rs2[:, 3, i:i + 1], None, ALU.mult).then_inc(aff_ok, 1)

            link(nc.vector.memset(idx_s[:], 0))
            link(nc.vector.memset(idx_p[:], 0))
            dve.wait_ge(affT_ok, 2)
            for r in range(CAP_P // 8):
                top_round(NS, NS + NP_, CAP_S + 8 * r)
            nc.vector.tensor_copy(topf, topi).then_inc(top_ok, 1)
            dve.wait_ge(top_tr, 1)
            link(nc.vector.tensor_copy(gate_s[:], PS[:, 0, 0:NE]))
            link(nc.vector.tensor_copy(gate_p[:], PS[0:CAP_P, 1, 0:NE]))
            link(nc.vector.tensor_copy(idx_s[:, 0:NE], PS[:, 0, NE:2 * NE]))
            link(nc.vector.tensor_copy(idx_p[:, 0:NE], PS[0:CAP_P, 1, NE:2 * NE]))
            nc.vector.tensor_copy(ig_s[:], idx_s[:, 0:1])
            nc.vector.tensor_copy(ig_p[:], idx_p[:, 0:1]).then_inc(gate_ok, 1)

            def take_prompt(j):
                nc.vector.tensor_copy(xT[:, 4 * j:4 * j + 4, CAP_S:CAP],
                                      PS[:, 5, 0:4 * CAP_P].rearrange("p (a b) -> p a b", a=4)).then_inc(xp_ok, 1)

            for j in range(4):
                dve.wait_ge(x_tr, j + 1)
                take_prompt(j)
            dve.wait_ge(g2_in, 32)

            with dve.Fori(0, NE) as e:
                dve.wait_ge(gs_in, e * 16 + 16)
                dve.wait_ge(gp_in, e * 16 + 16)
                nc.vector.tensor_copy(ig_s[:], idx_s[:, bass.ds(e + 1, 1)])
                nc.vector.tensor_copy(ig_p[:], idx_p[:, bass.ds(e + 1, 1)]).then_inc(ig_ok, 1)
                dve.wait_ge(y_free, e + 1)
                nc.vector.tensor_copy(ic_s[:], idx_s[:, bass.ds(e, 1)])
                nc.vector.tensor_copy(ic_p[:], idx_p[:, bass.ds(e, 1)]).then_inc(ic_ok, 1)
                for half in range(2):
                    dve.wait_ge(silu_ok, e * 2 + half + 1)
                    dve.wait_ge(ring_free, e * PIECES_E + NRING + 8 * half + 8)
                    h = hid[:, 4 * half:4 * half + 4, :].rearrange("p (a c) b -> p a (c b)", a=2)
                    nc.vector.tensor_tensor(h, hg[:, half, :].rearrange("p (a b) -> p a b", a=2), PS[:, 2:4, 0:2 * CAP],
                                            ALU.mult).then_inc(hid_ok, 1)

                def scale_rows(c):
                    s = slice(c * CC, (c + 1) * CC)
                    dve.wait_ge(y_tr, e * 4 + c + 1)
                    nc.vector.scalar_tensor_tensor(out=y_s[:, s], in0=PS[:, 6, :], scalar=gate_s[:, bass.ds(e, 1)],
                                                   in1=g2_s[:, s], op0=ALU.mult, op1=ALU.mult).then_inc(ys_ok, 1)
                    nc.vector.scalar_tensor_tensor(out=y_p[:, s], in0=PS[0:CAP_P, 7, :], scalar=gate_p[:, bass.ds(e, 1)],
                                                   in1=g2_p[:, s], op0=ALU.mult, op1=ALU.mult).then_inc(yp_ok, 1)

                for cc in range(4):
                    dve.wait_ge(x_tr, e * 4 + 5 + cc)
                    take_prompt(cc)
                    if cc:
                        scale_rows(cc - 1)
                scale_rows(3)

            dve.wait_ge(nf_in, 16)
            for i in range(TT):
                rstd(TT + i, i + 1, f_sq, f_ms, f_root)
                nc.vector.scalar_tensor_tensor(out=ring[:, NF + i % NF].rearrange("p a b -> p (a b)"),
                                               in0=ring[:, i % NF].rearrange("p a b -> p (a b)"), scalar=st[:, 4:5],
                                               in1=ring[:, 2 * NF].rearrange("p a b -> p (a b)"),
                                               op0=ALU.mult, op1=ALU.mult).then_inc(f_ok, 1)

        @block.gpsimd
        def _(pool):
            steps = [0]
            dma = nc.gpsimd.dma_start

            def link(ins):
                steps[0] += 1
                ins.then_inc(pool_step, 1)
                pool.wait_ge(pool_step, steps[0])

            dma(cond_r[0:16, :], t["c"].rearrange("b (t p) -> (b t) p", p=P)).then_inc(cond_in, 16)
            dma(cond_r[16:32, :], t["c_ctx"].rearrange("(t p) -> t p", p=P)).then_inc(cond_in, 16)
            dma(ident[:], t["k_ident"]).then_inc(consts_in, 16)
            dma(sel[:], t["k_sel"]).then_inc(consts_in, 16)
            dma(maskL[:], t["k_mask"][0]).then_inc(consts_in, 16)
            dma(maskR[:], t["k_mask"][1]).then_inc(consts_in, 16)
            dma(sinks[:, 0, :], t["sink_logits"][0].partition_broadcast(P)).then_inc(consts_in, 16)
            dma(sinks[:, 1, :], t["sink_logits"][0].partition_broadcast(P)).then_inc(consts_in, 16)
            dma(pscale[:], t["pool_scale"]).then_inc(consts_in, 16)
            for z in range(4):
                dma(wr[:, 4 * z:4 * z + 4, :],
                    t["w_router"][0, z * 512:(z + 1) * 512].rearrange("(t p) e -> p t e", p=P)).then_inc(consts_in, 16)

            def bias_row(a):
                if a >= 2:
                    pool.wait_ge(sel_ok, a - 1)
                dma(arow[4:5, a % 2, :], t["b_ada"][:, a * CC:(a + 1) * CC]).then_inc(brow_in[a % 2], 16)

            def store_mod(a):
                pool.wait_ge(mrow_ok, a + 1)
                dma(mod_d[:, a * CC:(a + 1) * CC], mrow[0:2, a % 2, :]).then_inc(mod_out[a % 2], 16)

            def mods_stored(n):
                pool.wait_ge(mod_out[0], 16 * ((n + 1) // 2))
                pool.wait_ge(mod_out[1], 16 * (n // 2))

            def table(dst, cond, m, n=P):
                return dma(dst, mod_d[cond, m * D:(m + 1) * D].partition_broadcast(n))

            def load_x(i):
                if i >= 2:
                    pool.wait_ge(h_tr, 4 * (i - 1))
                dma(xb[:, i % 2, :], rows(xs, xp, i)).then_inc(x_in[i % 2], 16)

            bias_row(0)
            bias_row(1)
            pool.wait_ge(consts_in, 16 * N_CONST)
            link(nc.gpsimd.tensor_scalar(sinks[:, 1, :], sinks[:, 1, :], -1.0, None, ALU.mult))
            dma(nmix, t["norm_mix"][0].partition_broadcast(P)).then_inc(nmix_in, 16)
            pool.wait_ge(nmix_in, 16)
            dma(xb[:, 0, :], rows(xs, xp, 0)).then_inc(x_in[0], 16)
            load_x(1)
            for a in range(ADA_A):
                store_mod(a)
                bias_row(a + 2)
                if a == ADA_A // 2 - 1:
                    mods_stored(ADA_A // 2)
                    table(tabS, 0, 0).then_inc(tab_in, 16)
            mods_stored(ADA_A)
            table(tabA, 0, 1).then_inc(tab_in, 16)

            def store_projection(tc, cc):
                t0, nt, cond = CH[tc]
                for m in range(nt if cc < 3 else 4):
                    pool.wait_ge(stg_ok, staged_by(5 * tc + cc) + m + 1)
                    i = t0 + m
                    if cc == 3 or cc == 4:
                        ct = (cc - 3) * 4 + m
                        dma(pool_d[ct * P:(ct + 1) * P, t0 * P:(t0 + nt) * P], stg[:, m, 0:nt * P]).then_inc(stg_out, 16)
                        continue
                    if cond == 0:
                        nr = 8 if cc < 2 else 4
                        dma(rtab, t["k_rope"][i]).then_inc(rtab_in, 16)
                        s = stg[:, m, 0:nr * 64].rearrange("p (a h f) -> p a h f", h=2, f=32)
                        a1, a2 = s[:, :, 0, :], s[:, :, 1, :]
                        cs, sn = (rtab[:, z, 0:nr * 32].rearrange("p (a f) -> p a f", f=32) for z in range(2))
                        r = [rt[:, z, 0:nr * 32].rearrange("p (a f) -> p a f", f=32) for z in range(4)]
                        pool.wait_ge(rtab_in, 16 * (3 * 4 * tc + 4 * cc + m + 1))
                        nc.gpsimd.tensor_tensor(r[0], a1, cs, ALU.mult)
                        nc.gpsimd.tensor_tensor(r[1], a2, sn, ALU.mult)
                        nc.gpsimd.tensor_tensor(r[2], a1, sn, ALU.mult)
                        link(nc.gpsimd.tensor_tensor(r[3], a2, cs, ALU.mult))
                        nc.gpsimd.tensor_tensor(a1, r[0], r[1], ALU.subtract)
                        link(nc.gpsimd.tensor_tensor(a2, r[2], r[3], ALU.add))
                    dma(qkv_d[i * P:(i + 1) * P, cc * CC:(cc + 1) * CC], stg[:, m, :]).then_inc(stg_out, 16)
                    if cond and cc == 2:
                        dma(st_k[m * P:(m + 1) * P, :], stg[:, m, 0:KW]).then_inc(stg_out, 16)
                        dma(st_v[m * P:(m + 1) * P, :], stg[:, m, KW:2 * KW]).then_inc(stg_out, 16)

            def load_rest(tc):
                for j in range(2, CH[tc][1]):
                    load_x(CH[tc][0] + j)

            def load_first(i):
                dma(xb[:, 0, :], rows(xs, xp, i)).then_inc(x_in[0], 16)
                dma(xb[:, 1, :], rows(xs, xp, i + 1)).then_inc(x_in[1], 16)

            load_rest(0)
            for u, (kd, n, cc) in enumerate(B_UNITS):
                if kd == "a":
                    if u + 1 < len(B_UNITS) and B_UNITS[u + 1][0] == "w" and B_UNITS[u + 1][2] == 0:
                        load_rest(B_UNITS[u + 1][1])
                    if B_UNITS[u + 1:u + 2] == [("w", 1, 3)]:
                        pool.wait_ge(tab_ok, 2)
                        load_first(ST)
                    store_mod(n)
                    if n + 2 < NADA:
                        bias_row(n + 2)
                    continue
                t0, nt, cond = CH[n]
                store_projection(n, cc)
                if cc == 1 and n < 2:
                    nxt = CH[n + 1][0]
                    pool.wait_ge(h_tr, 4 * nxt)
                    if CH[n + 1][2] == cond:
                        load_first(nxt)
                    else:
                        pool.wait_ge(h_ok, nxt)
                        table(tabS, 1, 0).then_inc(tab_in, 16)
                        table(tabA, 1, 1).then_inc(tab_in, 16)
                        dma(xb[:, 0, :], t["norm_mix"][0].partition_broadcast(P)).then_inc(x_in[0], 16)
            mods_stored(NADA)
            pool.wait_ge(stg_out, 16 * stores_by[-1])
            pool.wait_ge(used, D0)
            pool.wait_ge(lo_ok, D0)

            def load_q(i):
                if i:
                    k = max(z for z in range(n_units) if UNITS[z][1] == "Q" and CH[UNITS[z][0]][0] + UNITS[z][2] == i - 1)
                    pool.wait_ge(unit_pe, k + 1)
                dma(qq, qkv_d[i * P:(i + 1) * P, 0:AW]).then_inc(q_in, 16)

            def mixer(tc, gi):
                t0, nt, cond = CH[tc]
                T = nt * P
                w, L = POOLS[gi], T + 2 * HALO
                n = 4 * tc + gi
                first = t0 in (0, ST)
                final = t0 + nt in (ST, TT)
                c0, c1 = (HALO if first else 0), T + 2 * HALO - (HALO if final else 0)
                if n:
                    pool.wait_ge(mixed, n)
                    pool.wait_ge(unit_pe, m_unit(n - 1) + 1)
                if first:
                    link(nc.gpsimd.memset(pin[:, :, 0:HALO], 0.0))
                if final:
                    link(nc.gpsimd.memset(pin[:, :, HALO + T:L], 0.0))
                dma(pw, t["pool_w"][0, gi].rearrange("(z p) n -> p z n", p=P)).then_inc(pin_in, 16)
                dma(rcnt[:, 0:T], t["k_rcnt"][gi, t0 * P:t0 * P + T].partition_broadcast(P)).then_inc(pin_in, 16)
                for z in range(2):
                    ct = 2 * gi + z
                    dma(pin[:, z, c0:c1], pool_d[ct * P:(ct + 1) * P, t0 * P - HALO + c0:t0 * P - HALO + c1]).then_inc(pin_in, 16)
                pool.wait_ge(pin_in, 64 * (n + 1))
                link(nc.gpsimd.tensor_tensor(pa[:, :, 1:L], pin[:, :, 0:L - 1], pin[:, :, 1:L], ALU.add))
                src, dst, lo, hi, half = pa, pb, 1, L, 1
                while 2 * half < w:
                    link(nc.gpsimd.tensor_tensor(dst[:, :, lo + half:hi - half], src[:, :, lo:hi - 2 * half],
                                                 src[:, :, lo + 2 * half:hi], ALU.add))
                    lo, hi = lo + half, hi - half
                    src, dst, half = dst, src, 2 * half
                for z in range(2):
                    link(nc.gpsimd.tensor_tensor(src[:, z, HALO:HALO + T], src[:, z, HALO:HALO + T], rcnt[:, 0:T], ALU.mult))
                nc.gpsimd.tensor_tensor(mixT[:, :, 0:T], src[:, :, HALO:HALO + T], pin[:, :, HALO:HALO + T],
                                        ALU.subtract).then_inc(mixed, 1)

            for tc, (t0, nt, cond) in enumerate(CH):
                if tc:
                    pool.wait_ge(h2_ok, t0)
                if cond == 0:
                    k0 = max(0, t0 - 1)
                    for dst, cache, col in ((ktm, ck, AW), (vv, cv, AW + KW)):
                        dma(dst[:, 0:4, :], cache.rearrange("(b p) d -> p b d", p=P)).then_inc(kv_in, 16)
                        dma(dst[:, 4:9, :], qkv_d[k0 * P:(k0 + 5) * P, col:col + KW].rearrange("(b p) d -> p b d", p=P)).then_inc(kv_in, 16)
                else:
                    for dst, col in ((ktm, AW), (vv, AW + KW)):
                        dma(dst[:, 0:2, :], qkv_d[NS:NS + NP_, col:col + KW].rearrange("(b p) d -> p b d", p=P)).then_inc(kv_in, 16)
                load_q(t0)
                if tc:
                    pool.wait_ge(h2_out, 16 * t0)
                    pool.wait_ge(h2T_used, 4 * t0)
                per = 4 // nt
                for b in range(nt):
                    if b + 1 < nt:
                        pool_next = t0 + b + 1
                    for gi in range(b * per, b * per + per):
                        mixer(tc, gi)
                    if b + 1 < nt:
                        load_q(pool_next)

                pool.wait_ge(pv_ok, heads_by(unit_end[tc]))
                pool.wait_ge(unit_pe, unit_end[tc])
                pool.wait_ge(o_lo, heads_by(unit_end[tc]) // 4)
                pool.wait_ge(copied, copies_by(unit_end[tc]))
                pool.wait_ge(pt_a, heads_by(unit_end[tc]))
                table(tabG, cond, 2).then_inc(dtab_in, 16)
                table(tabA2, cond, 4).then_inc(dtab_in, 16)
                table(tabS2, cond, 3).then_inc(dtab_in, 16)
                dma(nffn, t["norm_ffn"][0].partition_broadcast(P)).then_inc(dtab_in, 16)
                for j in range(nt):
                    dma(x1[:, j, :], rows(xs, xp, t0 + j)).then_inc(x1_in, 16)
                for cc in range(4):
                    pool.wait_ge(x1_ok, x1_by(tc, cc))
                    a = res_p if cond else res_s[t0 * P:(t0 + nt) * P, :]
                    dma(a[:, cc * CC:(cc + 1) * CC].rearrange("(j p) n -> p j n", p=P),
                        x1[:, 0:nt, cc * CC:(cc + 1) * CC]).then_inc(x1_out, 16)
                for j in range(nt):
                    pool.wait_ge(h2_ok, t0 + j + 1)
                    dma(rows(h2_s, h2_p, t0 + j), x1[:, j, :]).then_inc(h2_out, 16)
            pool.wait_ge(x1_out, 16 * 12)
            pool.wait_ge(h2_out, 16 * TT)

            pool.wait_ge(gate_ok, 1)
            table(g2_s[:], 0, 5).then_inc(g2_in, 16)
            table(g2_p[:], 1, 5, CAP_P).then_inc(g2_in, 16)

            def gather():
                nc.gpsimd.indirect_dma_start(out=g_s[:], out_offset=None, in_=h2_s,
                                             in_offset=bass.IndirectOffsetOnAxis(ap=ig_s[:, 0:1], axis=0)).then_inc(gs_in, 16)
                nc.gpsimd.indirect_dma_start(out=g_p[:], out_offset=None, in_=h2_p,
                                             in_offset=bass.IndirectOffsetOnAxis(ap=ig_p[:, 0:1], axis=0)).then_inc(gp_in, 16)

            gather()
            nc.gpsimd.nop().then_inc(y_free, 1)
            with pool.Fori(0, NE) as e:
                pool.wait_ge(ig_ok, e + 1)
                pool.wait_ge(x_tr, e * 4 + 4)
                nc.gpsimd.nop().then_inc(turn, 1)
                gather()
                pool.wait_ge(ic_ok, e + 1)
                pool.wait_ge(ys_ok, e * 4 + 4)
                pool.wait_ge(yp_ok, e * 4 + 4)
                nc.gpsimd.nop().then_inc(turn, 1)
                nc.gpsimd.indirect_dma_start(out=res_s, out_offset=bass.IndirectOffsetOnAxis(ap=ic_s[:, 0:1], axis=0),
                                             in_=y_s[:], in_offset=None, compute_op=ALU.add).then_inc(s_out, 16)
                nc.gpsimd.indirect_dma_start(out=res_p, out_offset=bass.IndirectOffsetOnAxis(ap=ic_p[:, 0:1], axis=0),
                                             in_=y_p[:], in_offset=None, compute_op=ALU.add).then_inc(p_out, 16)
                pool.wait_ge(s_out, e * 16 + 16)
                pool.wait_ge(p_out, e * 16 + 16)
                nc.gpsimd.nop().then_inc(y_free, 1)

            pool.wait_ge(ring_free, NRING + NE * PIECES_E)
            pool.wait_ge(gs_in, 16 * (NE + 1))
            pool.wait_ge(gp_in, 16 * (NE + 1))
            flat = [ring[:, z].rearrange("p a b -> p (a b)") for z in range(2 * NF + 1)]
            dma(flat[2 * NF], t["norm_final"].partition_broadcast(P)).then_inc(nf_in, 16)
            for i in range(NF):
                dma(flat[i], rows(res_s, res_p, i)).then_inc(f_in[i], 16)
            for i in range(TT):
                pool.wait_ge(f_ok, i + 1)
                dma(rows(ys, yp, i), flat[NF + i % NF]).then_inc(f_out[i % NF], 16)
                if i + NF < TT:
                    dma(flat[i % NF], rows(res_s, res_p, i + NF)).then_inc(f_in[i % NF], 16)
            for z in range(NF):
                pool.wait_ge(f_out[z], 16 * ((TT - z + NF - 1) // NF))


def shape_constants():
    i = np.arange(P)
    mask = np.zeros((2, P, P), np.float32)
    mask[0][i[None, :] < i[:, None]] = NEG
    mask[1][i[None, :] > i[:, None]] = NEG
    grid, nf = 64, HD // 4
    pos = np.arange(NS)
    inv = (np.float32(10000.0) ** (-np.arange(nf, dtype=np.float32) / np.float32(nf))).astype(np.float32)
    ang = np.stack([(pos // grid).astype(np.float32)[:, None] * inv,
                    (pos % grid).astype(np.float32)[:, None] * inv], axis=1).reshape(NS, 2 * nf)
    rope = np.stack([np.tile(np.cos(ang), (1, 4)), np.tile(np.sin(ang), (1, 4))], axis=1).astype(np.float32)
    rcnt = np.zeros((4, NS + NP_), np.float32)
    for gi, w in enumerate(POOLS):
        for base, n in ((0, NS), (NS, NP_)):
            tok = np.arange(n)
            cnt = np.clip(tok + w - w // 2, 0, n) - np.clip(tok - w // 2, 0, n)
            rcnt[gi, base:base + n] = 1.0 / cnt
    sel = np.zeros((5, 2), np.float32)
    sel[[0, 2], 0] = 1.0
    sel[[1, 3], 1] = 1.0
    sel[4] = 1.0
    return {"k_ident": np.eye(P, dtype=np.float32), "k_mask": mask,
            "k_rope": rope.reshape(ST, P, 2, 256), "k_rcnt": rcnt, "k_sel": sel}


_INS = ["x_prompt", "x_sample", "c", "cache_k", "cache_v", "c_ctx", "w_ada", "b_ada", "norm_mix", "w_in",
        "sink_logits", "pool_w", "pool_scale", "w_out", "norm_ffn", "w_router", "w_gate", "w_up", "w_down",
        "norm_final"]
_OUTS = [("y_prompt", (1, NP_, D)), ("y_sample", (1, NS, D)), ("state_k", (1, 1, NP_, NKV, HD)),
         ("state_v", (1, 1, NP_, NKV, HD))]


def kernel(**inputs):
    import concourse.bacc as _bacc
    from concourse.bass_utils import run_bass_kernel_spmd as _run

    nc = _bacc.Bacc("TRN2", target_bir_lowering=False, num_devices=1)
    arrays = {n: np.ascontiguousarray(inputs[n]) for n in _INS}
    arrays["pool_scale"] = np.ascontiguousarray(arrays["pool_scale"].reshape(PW // P, P).T)
    arrays.update(shape_constants())
    t = {n: nc.dram_tensor(n, a.shape, F32, kind="ExternalInput").ap() for n, a in arrays.items()}
    o = {n: nc.dram_tensor(n, s, F32, kind="ExternalOutput").ap() for n, s in _OUTS}
    hybrid_backbone_step(nc, t, o)
    r = _run(nc, [arrays], core_ids=[0])
    return tuple(r.results[0][n] for n, _ in _OUTS)
```

```python
from contextlib import ExitStack

import numpy as np

import concourse.bass as bass
from concourse import mybir

F32 = mybir.dt.float32
F32R = mybir.dt.float32r
BF16 = mybir.dt.bfloat16
U32 = mybir.dt.uint32
ACT = mybir.ActivationFunctionType
ALU = mybir.AluOpType
AXX = mybir.AxisListType.X

P = 128
D = 2048
KT = D // P
NS = 1024
NP_ = 256
ST = NS // P
TT = (NS + NP_) // P
CH = [(0, 4, 0), (4, 4, 0), (8, 2, 1)]
PAST = 512
NH, NKV, HD = 8, 2, 128
AW = NH * HD
KW = NKV * HD
PW = D - AW
INW = AW + 2 * KW + PW
POOLS = (2, 4, 8, 16)
PG = PW // 4
HALO = 8
NE = 16
FE = 1024
CAP_S, CAP_P = 2 * NS // NE, 2 * NP_ // NE
CAP = CAP_S + CAP_P
Q = P // CAP_P
DQ = D // Q
EPS = 1e-6
NEG = -1e30
SCALE = HD ** -0.5
CC = 512
KG = 4
NRAW = 3
NSPLIT = 3
NRAW_F = 4
NSPL_F = 4
KF, CF = 8, 256
NADA = 6 * D // CC
ADA_A = 2 * D // CC
PIECES_E = 2 * (D // P // KF) * (FE // CF) + (FE // P // KF) * (D // CF)


def stream_units():
    units, a = [], ADA_A
    for tc, ada_after in enumerate(((2, 2, 2, 1, 1), (2, 2, 2, 1, 1), (0, 0, 0, 0, 0))):
        for cc in range(5):
            units.append(("w", tc, cc))
            for _ in range(ada_after[cc]):
                units.append(("a", a, 0))
                a += 1
    assert a == NADA
    return units


B_UNITS = stream_units()


def build_units():
    units = []
    for tc, (t0, nt, cond) in enumerate(CH):
        nk = 9 if cond == 0 else 2
        nu = (2 * nk + 7) // 8
        for u in range(nu):
            units.append((tc, "K", 0, u))
        per = 4 // nt
        for b in range(nt):
            units.append((tc, "Q", b, 0))
            for h in range(NH):
                units.append((tc, "H", b, h))
            for g in range(b * per, b * per + per):
                units.append((tc, "M", b, g))
    heads, copies, nh, ncp = [], [], 0, 0
    for u in units:
        heads.append(nh)
        copies.append(ncp)
        if u[1] == "H":
            nh += 1
        else:
            ncp += 1
    return units, heads, copies


UNITS, HEADS_BEFORE, COPIES_BEFORE = build_units()


def local_blocks(tc, b):
    t0, nt, cond = CH[tc]
    if cond:
        return [0, 1], False, False
    q = t0 + b
    first = max(0, t0 - 1)
    ks = [k for k in (q - 1, q, q + 1) if 0 <= k < ST]
    return [k - first for k in ks], q - 1 >= 0, q + 1 < ST


def hybrid_backbone_step(nc, t, o):
    ctx = ExitStack()
    with ctx:
        def sem(name):
            return ctx.enter_context(nc.semaphore(name))

        def dram(name, shape):
            return nc.dram_tensor(name, shape, F32, kind="Internal").ap()

        mod_d = dram("mod_rows", [2, 6 * D])
        qkv_d = dram("qkv_rows", [NS + NP_, AW + 2 * KW])
        pool_d = dram("pool_cols", [PW, NS + NP_])
        res_s, res_p = dram("resid_s", [NS, D]), dram("resid_p", [NP_, D])
        h2_s, h2_p = dram("h2_s", [NS, D]), dram("h2_p", [NP_, D])
        res_q, h2_q = (a.rearrange("t (m d) -> (t m) d", m=Q) for a in (res_p, h2_p))

        xs = t["x_sample"].rearrange("b n d -> (b n) d")
        xp = t["x_prompt"].rearrange("b n d -> (b n) d")
        ys = o["y_sample"].rearrange("b n d -> (b n) d")
        yp = o["y_prompt"].rearrange("b n d -> (b n) d")
        st_k = o["state_k"].rearrange("b l n h d -> (b l n) (h d)")
        st_v = o["state_v"].rearrange("b l n h d -> (b l n) (h d)")
        ck = t["cache_k"].rearrange("b l n h d -> (b l n) (h d)")
        cv = t["cache_v"].rearrange("b l n h d -> (b l n) (h d)")
        w_ada = t["w_ada"].rearrange("l k n -> (l k) n")
        w_in = t["w_in"].rearrange("l k n -> (l k) n")
        w_out = t["w_out"].rearrange("l k n -> (l k) n")
        w_gate = t["w_gate"].rearrange("l e k n -> (l e) k n")
        w_up = t["w_up"].rearrange("l e k n -> (l e) k n")
        w_down = t["w_down"].rearrange("l e k n -> (l e) k n")

        def rows(a_s, a_p, i):
            return a_s[i * P:(i + 1) * P, :] if i < ST else a_p[(i - ST) * P:(i - ST + 1) * P, :]

        def piece(w, kg, c0):
            return w[kg * KG * P:(kg + 1) * KG * P, c0:c0 + CC].rearrange("(r p) n -> p r n", p=P)

        pieces = [piece(w_ada, kg, a * CC) for a in range(ADA_A) for kg in range(4)]
        for kd, n, cc in B_UNITS:
            pieces += [piece(*((w_in, kg, cc * CC) if kd == "w" else (w_ada, kg, n * CC))) for kg in range(4)]
        D0 = len(pieces)
        for tc in range(3):
            for cc in range(4):
                pieces += [piece(w_out, kg, cc * CC) for kg in range(4)]

        PS = ctx.enter_context(nc.psum_tensor("PS", [P, 8, 512], F32))

        def keep(name, shape, dt=F32):
            return ctx.enter_context(nc.sbuf_tensor(name, shape, dt))

        ident = keep("ident", [P, P])
        maskL = keep("maskL", [P, P])
        maskR = keep("maskR", [P, P])
        sel = keep("sel", [5, 2])
        sinks = keep("sinks", [P, 2, NH])
        pscale = keep("pscale", [P, PW // P])
        wr = keep("wr", [P, KT, NE])
        ss = keep("ss", [P, 2 * TT])
        st = keep("st", [P, 8])
        sm = keep("sm", [P, 2, 8])
        aff = keep("aff", [P, TT, NE])
        ss2 = keep("ss2", [P, TT, 4])
        rs2 = keep("rs2", [P, 6, TT])
        gate_s, gate_p = keep("gate_s", [P, NE]), keep("gate_p", [P, NE])
        idx_s, idx_p = keep("idx_s", [P, NE + 1], U32), keep("idx_p", [P, NE + 1], U32)
        ig_s, ig_p = keep("ig_s", [P, 1], U32), keep("ig_p", [P, 1], U32)
        ic_s, ic_p = keep("ic_s", [P, 1], U32), keep("ic_p", [P, 1], U32)

        mix = ExitStack()

        def mixt(name, shape, dt):
            return mix.enter_context(nc.sbuf_tensor(name, shape, dt))

        raw = mixt("raw", [P, NRAW, KG, CC], F32)
        whi = mixt("whi", [P, NSPLIT, KG, CC], F32R)
        wlo = mixt("wlo", [P, NSPLIT, KG, CC], F32R)
        ahi = mixt("ahi", [P, KT, 512], F32R)
        alo = mixt("alo", [P, KT, 512], F32R)
        off = [0]
        arena = [None]

        def carve(*shape):
            n = int(np.prod(shape))
            v = arena[0][:, off[0]:off[0] + n]
            off[0] += n
            assert off[0] <= arena[0].shape[1], off[0]
            if len(shape) == 2:
                v = v.rearrange("p (a b) -> p a b", a=shape[0])
            if len(shape) == 3:
                v = v.rearrange("p (a b c) -> p a b c", a=shape[0], b=shape[1])
            return v

        early = ExitStack()
        arena[0] = early.enter_context(nc.sbuf_tensor("arena_ab", [P, 58 * 256], F32))
        cond_s = early.enter_context(nc.sbuf_tensor("cond_s", [P, KT, P], F32R))
        xb = carve(2, D)
        tabA, tabS = carve(D), carve(D)
        stg = carve(4, 512)
        rtab = carve(2, 256)
        rt0 = off[0]
        rt = carve(4, 256)
        junk = carve(D // 2).bitcast(BF16)
        nmix = arena[0][:, rt0:rt0 + D]
        arow = carve(2, 512)
        mrow = carve(2, 512)
        cond_r = stg[:, 0, 0:P]
        cond_f = stg[:, 1, 0:32]
        early.close()
        arena[0] = mixt("arena_cd", [P, 66 * 256], F32)
        off[0] = 0
        vv = carve(9, KW)
        qq = carve(AW)
        pt0 = off[0]
        pp = carve(2, 7 * P)
        pT = carve(2, 7, P)
        ktm = arena[0][:, pt0:pt0 + 9 * KW].rearrange("p (a b) -> p a b", a=9)
        assert pt0 + 9 * KW <= 3 * D
        kT = carve(2 * 9 * P)
        qT = carve(NH, P)
        pin = carve(2, 512 + 2 * HALO)
        pa = carve(2, 512 + 2 * HALO)
        pb = carve(2, 512 + 2 * HALO)
        mixT = carve(2, 512)
        rcnt = carve(512)
        pw = carve(2, PG)
        off[0] = 0
        tabG, tabA2, tabS2 = carve(D), carve(D), carve(D)
        x1 = carve(4, D)
        h2T = carve(4, 4, P)
        nffn = h2T.rearrange("p a b c -> p (a b c)")
        junk2 = carve(CC // 2).bitcast(BF16)
        assert CH[-1][1] == 2
        cols = x1[:, 2:4, :].rearrange("p a b -> p (a b)")
        affT = cols[0:NE, 0:NS + NP_]
        top, topf = cols[0:NE, 2048:2048 + CAP], cols[0:NE, 2304:2304 + CAP]
        topi = cols[0:NE, 2560:2560 + CAP].bitcast(U32)
        top_q = cols[0:NE, 2816:2816 + P].rearrange("p (a b) -> p a b", a=Q)
        topf_q = cols[0:NE, 3072:3072 + P].rearrange("p (a b) -> p a b", a=Q)
        mix.close()

        fmem = ExitStack()

        def expt(name, shape, dt=F32):
            return fmem.enter_context(nc.sbuf_tensor(name, shape, dt))

        raw_f = expt("raw_f", [P, NRAW_F, KF, CF])
        hi_f, lo_f = expt("hi_f", [P, NSPL_F, KF, CF], F32R), expt("lo_f", [P, NSPL_F, KF, CF], F32R)
        xT = expt("xT", [P, KT, 2 * CAP], F32R)
        hid = expt("hid", [P, FE // P, 2 * CAP], F32R)
        part = expt("part", [P, 2, 2 * CAP])
        gsum, usum = expt("gsum", [P, 2 * CAP]), expt("usum", [P, 2 * CAP])
        hg, hraw = expt("hg", [P, 2 * CAP]), expt("hraw", [P, 2 * CAP])
        yT = expt("yT", [P, 2, KG, CAP_S])
        yTp = expt("yTp", [P, DQ // P, Q, CAP_P])
        g_s, g_p = expt("g_s", [P, D]), expt("g_p", [P, DQ])
        y_s, y_p = expt("y_s", [P, D]), expt("y_p", [P, DQ])
        g2_s, g2_p = expt("g2_s", [P, D]), expt("g2_p", [P, DQ])
        fmem.close()
        NF = 4
        fin = keep("fin", [P, 2 * NF + 1, D])

        raw_in = [sem(f"raw_in{i}") for i in range(NRAW)]
        hi_ok, lo_ok, used = sem("hi_ok"), sem("lo_ok"), sem("used")
        consts_in, cond_in, zero_ok = sem("consts_in"), sem("cond_in"), sem("zero_ok")
        cond_tr, cond_f_ok, cond_hi, cond_lo = sem("cond_tr"), sem("cond_f_ok"), sem("cond_hi"), sem("cond_lo")
        arow_ok, sel_ok, mrow_ok = sem("arow_ok"), sem("sel_ok"), sem("mrow_ok")
        brow_in = [sem(f"brow_in{i}") for i in range(2)]
        mod_out = [sem(f"mod_out{i}") for i in range(2)]
        nmix_in, tab_in, tab_ok = sem("nmix_in"), sem("tab_in"), sem("tab_ok")
        x_in = [sem(f"x_in{i}") for i in range(2)]
        sq_ok, root_ok, h_ok = sem("sq_ok"), sem("root_ok"), sem("h_ok")
        ms_ok = sem("ms_ok")
        h_tr, h_hi, h_lo = sem("h_tr"), sem("h_hi"), sem("h_lo")
        stg_ok, stg_out = sem("stg_ok"), sem("stg_out")
        rtab_in = sem("rtab_in")
        dve_step, pool_step = sem("dve_step"), sem("pool_step")
        kv_in, q_in, unit_pe = sem("kv_in"), sem("q_in"), sem("unit_pe")
        copied, m_hi, masked, exped, sank = sem("copied"), sem("m_hi"), sem("masked"), sem("exped"), sem("sank")
        p_ok, p_tr, pt_a, pt_v, pv_ok, o_hi, o_lo = (sem(n) for n in ("p_ok", "p_tr", "pt_a", "pt_v", "pv_ok", "o_hi", "o_lo"))
        pin_in, mixed = sem("pin_in"), sem("mixed")
        dtab_in, x1_in, dtab_ok = sem("dtab_in"), sem("x1_in"), sem("dtab_ok")
        x1_ok, x1_out, h2_ok, h2_out = (sem(n) for n in ("x1_ok", "x1_out", "h2_ok", "h2_out"))
        h2_tr, h2T_ok, lmax_ok, lexp_ok, aff_ok = (
            sem(n) for n in ("h2_tr", "h2T_ok", "lmax_ok", "lexp_ok", "aff_ok"))
        h2T_used, sq2_ok, ms2_ok, root2_ok = (sem(n) for n in ("h2T_used", "sq2_ok", "ms2_ok", "root2_ok"))
        aff_tr, affT_ok, top_ok, top_tr, gate_ok = (sem(n) for n in ("aff_tr", "affT_ok", "top_ok", "top_tr", "gate_ok"))
        raw_f_in = [sem(f"raw_f_in{i}") for i in range(NRAW_F)]
        f_hi_ok, f_lo_ok, f_used = sem("f_hi_ok"), sem("f_lo_ok"), sem("f_used")
        part_ok, gsum_ok, usum_ok, silu_ok, hid_ok, hid_hi, hid_lo = (
            sem(n) for n in ("part_ok", "gsum_ok", "usum_ok", "silu_ok", "hid_ok", "hid_hi", "hid_lo"))
        yT_ok, x_tr, x_hi, x_lo, y_tr, ys_ok, yp_ok = (
            sem(n) for n in ("yT_ok", "x_tr", "x_hi", "x_lo", "y_tr", "ys_ok", "yp_ok"))
        gs_in, gp_in, ig_ok, ic_ok, y_free, s_out, p_out = (
            sem(n) for n in ("gs_in", "gp_in", "ig_ok", "ic_ok", "y_free", "s_out", "p_out"))
        g2_in, turn = sem("g2_in"), sem("turn")
        f_in = [sem(f"f_in{i}") for i in range(NF)]
        f_out = [sem(f"f_out{i}") for i in range(NF)]
        nf_in, f_sq, f_ms, f_root, f_ok = sem("nf_in"), sem("f_sq"), sem("f_ms"), sem("f_root"), sem("f_ok")

        N_CONST = 11
        n_units = len(UNITS)
        n_heads = HEADS_BEFORE[-1] + (UNITS[-1][1] == "H")
        n_copies = COPIES_BEFORE[-1] + (UNITS[-1][1] != "H")
        unit_end = [max(k for k in range(n_units) if UNITS[k][0] == tc) + 1 for tc in range(3)]
        unit_start = [0, unit_end[0], unit_end[1]]

        def heads_by(k):
            return HEADS_BEFORE[k] if k < n_units else n_heads

        def copies_by(k):
            return COPIES_BEFORE[k] if k < n_units else n_copies

        def m_by(k):
            return sum(1 for u in UNITS[:k] if u[1] == "M")

        def kind(k):
            return UNITS[k][1] if 0 <= k < n_units else None

        def in_chunk(k, tc):
            return unit_start[tc] <= k < unit_end[tc]

        def keys(tc, b):
            loc, ml, mr = local_blocks(tc, b)
            ctx_n = 0 if CH[tc][2] else PAST // P
            return ctx_n, [ctx_n + k for k in loc], ml, mr

        def ada_pieces(a):
            return 4 * (a + 1) if a < ADA_A else 4 * (ADA_A + B_UNITS.index(("a", a, 0)) + 1)

        def win_pieces(tc, cc):
            return 4 * (ADA_A + B_UNITS.index(("w", tc, cc)) + 1)

        def m_unit(n):
            return [k for k in range(n_units) if UNITS[k][1] == "M"][n]

        def staged_by(n):
            return sum((CH[c // 5][1] if c % 5 < 3 else 4) for c in range(n))

        def x1_by(tc, cc):
            return sum(4 * CH[c][1] for c in range(tc)) + (cc + 1) * CH[tc][1]

        def x_loads(i):
            n = i // 2 + 1
            if i % 2 == 0 and i >= ST:
                n += 1
            return n

        def p_place(cn, z):
            return z if cn else 4 * z

        kv_by = [64, 128, 160]

        stores_by = [0]
        for tc, (t0, nt, cond) in enumerate(CH):
            for cc in range(5):
                if cc < 3:
                    n = nt + (2 * nt if cond and cc == 2 else 0)
                else:
                    n = 4
                stores_by.append(stores_by[-1] + n)

        block = ctx.enter_context(nc.Block())

        @block.sync
        def _(sp):
            for g, src in enumerate(pieces):
                if g >= NRAW:
                    sp.wait_ge(lo_ok, g - NRAW + 1)
                sp.dma_start(raw[:, g % NRAW], src).then_inc(raw_in[g % NRAW], 16)
            with sp.Fori(0, NE) as e:
                n = 0
                units = [(w, c, kg) for c in range(FE // CF) for w in (w_gate, w_up) for kg in range(KT // KF)]
                units += [(w_down, c, 0) for c in range(D // CF)]
                for w, c, kg in units:
                    sp.wait_ge(f_lo_ok, e * PIECES_E + n + 1)
                    src = w[bass.ds(e, 1), kg * KF * P:(kg + 1) * KF * P, c * CF:(c + 1) * CF]
                    sp.dma_start(raw_f[:, n % NRAW_F],
                                 src.rearrange("e (r p) n -> p (e r) n", p=P)).then_inc(raw_f_in[n % NRAW_F], 16)
                    n += 1

        @block.tensor
        def _(pe):
            g = [0]

            def next_piece():
                n = g[0]
                g[0] += 1
                pe.wait_ge(lo_ok, n + 1)
                return whi[:, n % NSPLIT], wlo[:, n % NSPLIT]

            def ada(a):
                if a:
                    pe.wait_ge(arow_ok, a)
                for kg in range(4):
                    hi, lo = next_piece()
                    for r in range(KG):
                        kt = kg * KG + r
                        nc.tensor.matmul(PS[:, 7, :], cond_s[:, kt, :], hi[:, r, :], start=(kt == 0), stop=False)
                        last = nc.tensor.matmul(PS[:, 7, :], cond_s[:, kt, :], lo[:, r, :],
                                                start=False, stop=(kt == KT - 1))
                    last.then_inc(used, 1)

            def select(a):
                pe.wait_ge(arow_ok, a + 1)
                pe.wait_ge(brow_in[a % 2], 16 * (a // 2 + 1))
                if a:
                    pe.wait_ge(mrow_ok, a)
                nc.tensor.matmul(PS[0:2, 6, :], sel[0:5, :], arow[0:5, a % 2, :], start=True, stop=True).then_inc(sel_ok, 1)

            pe.wait_ge(consts_in, 16 * N_CONST)
            pe.wait_ge(cond_in, 32)
            nc.tensor.transpose(PS[:, 0, 0:32], cond_r[0:32, :], ident[0:32, 0:32]).then_inc(cond_tr, 1)
            pe.wait_ge(cond_lo, 1)
            for a in range(ADA_A):
                ada(a)
                if a:
                    select(a - 1)
            select(ADA_A - 1)

            def turn_h(tc):
                t0, nt, cond = CH[tc]
                for i in range(t0, t0 + nt):
                    pe.wait_ge(h_ok, i + 1)
                    for q in range(4):
                        n = 4 * i + q
                        if n >= 2:
                            pe.wait_ge(h_lo, n - 1)
                        for r in range(4):
                            kt = 4 * q + r
                            last = nc.tensor.transpose(PS[:, 4 + n % 2, r * P:(r + 1) * P],
                                                       xb[:, i % 2, kt * P:(kt + 1) * P], ident[:])
                        last.then_inc(h_tr, 1)
                pe.wait_ge(h_lo, 4 * (t0 + nt))

            def project(tc, cc):
                nt = CH[tc][1]
                T = nt * P
                pe.wait_ge(stg_ok, staged_by(5 * tc + cc)) if tc or cc else None
                for kg in range(4):
                    hi, lo = next_piece()
                    for r in range(KG):
                        kt = kg * KG + r
                        for m in range(nt if cc < 3 else 4):
                            s = slice(m * P, (m + 1) * P)
                            if cc < 3:
                                ops = ((ahi[:, kt, s], hi[:, r, :]), (alo[:, kt, s], hi[:, r, :]),
                                       (ahi[:, kt, s], lo[:, r, :]))
                                out = PS[:, m, :]
                            else:
                                ops = ((hi[:, r, s], ahi[:, kt, 0:T]), (hi[:, r, s], alo[:, kt, 0:T]),
                                       (lo[:, r, s], ahi[:, kt, 0:T]))
                                out = PS[:, m, 0:T]
                            for z, (w, x) in enumerate(ops):
                                last = nc.tensor.matmul(out, w, x, start=(kt == 0 and z == 0),
                                                        stop=(kt == KT - 1 and z == 2))
                    last.then_inc(used, 1)

            for u, (kd, n, cc) in enumerate(B_UNITS):
                if kd == "w":
                    if cc == 0:
                        turn_h(n)
                    project(n, cc)
                else:
                    ada(n)
                if u and B_UNITS[u - 1][0] == "a":
                    select(B_UNITS[u - 1][1])

            for tc, (t0, nt, cond) in enumerate(CH):
                if tc == 0:
                    pe.wait_ge(stg_ok, staged_by(15))
                    pe.wait_ge(mrow_ok, NADA)
                else:
                    pe.wait_ge(x1_ok, 16 * tc)
                    pe.wait_ge(h2T_ok, 4 * t0)
                nk = 9 if cond == 0 else 2
                for k in range(unit_start[tc], unit_end[tc] + 2):
                    if k < unit_end[tc]:
                        _, kd, b, h = UNITS[k]
                        pair = 2 * (k % 2)
                        if k - 2 >= unit_start[tc]:
                            if kind(k - 2) == "H":
                                pe.wait_ge(exped, heads_by(k - 1))
                            else:
                                pe.wait_ge(copied, copies_by(k - 1))
                        flat = PS[:, pair:pair + 2, :].rearrange("p a b -> p (a b)")
                        if kd == "K":
                            pe.wait_ge(kv_in, kv_by[tc])
                            for z in range(h * 8, min(h * 8 + 8, 2 * nk)):
                                kv, kb = z // nk, z % nk
                                last = nc.tensor.transpose(flat[:, (z % 8) * P:(z % 8 + 1) * P],
                                                           ktm[:, kb, kv * P:(kv + 1) * P], ident[:])
                        elif kd == "Q":
                            pe.wait_ge(q_in, 16 * (t0 + b + 1))
                            for z in range(NH):
                                last = nc.tensor.transpose(flat[:, z * P:(z + 1) * P], qq[:, z * P:(z + 1) * P], ident[:])
                        elif kd == "H":
                            if h == 0:
                                pe.wait_ge(copied, copies_by(k))
                            cn, loc, _, _ = keys(tc, b)
                            kv = h // (NH // NKV)
                            base = kv * nk * P
                            if cn:
                                nc.tensor.matmul(flat[:, 0:cn * P], qT[:, h, :], kT[:, base:base + cn * P],
                                                 start=True, stop=True)
                            l0 = base + loc[0] * P
                            last = nc.tensor.matmul(flat[:, cn * P:(cn + len(loc)) * P], qT[:, h, :],
                                                    kT[:, l0:l0 + len(loc) * P], start=True, stop=True)
                        else:
                            gi = 4 * tc + h
                            pe.wait_ge(mixed, gi + 1)
                            for m in range(2):
                                for z in range(2):
                                    last = nc.tensor.matmul(PS[:, pair + m, 0:nt * P], pw[:, z, m * P:(m + 1) * P],
                                                            mixT[:, z, 0:nt * P], start=(z == 0), stop=(z == 1))
                        last.then_inc(unit_pe, 1)
                    if in_chunk(k - 2, tc) and kind(k - 2) == "H":
                        _, _, b, h = UNITS[k - 2]
                        hc = heads_by(k - 2)
                        cn, loc, _, _ = keys(tc, b)
                        places = list(range(cn)) + loc
                        pe.wait_ge(pt_a, hc + 1)
                        pe.wait_ge(pt_v, hc + 1)
                        if tc and k - 2 < unit_start[tc] + 12:
                            pe.wait_ge(lexp_ok, t0)
                        if h % 4 == 0 and hc >= 8:
                            pe.wait_ge(o_lo, hc // 4 - 1)
                        for z, kb in enumerate(places):
                            last = nc.tensor.matmul(PS[:, 6 + h // 4, (h % 4) * P:(h % 4 + 1) * P],
                                                    vv[:, kb, (h // 4) * P:(h // 4 + 1) * P], pT[:, hc % 2, z, :],
                                                    start=(z == 0), stop=(z == len(places) - 1))
                        last.then_inc(pv_ok, 1)
                    if in_chunk(k - 1, tc) and kind(k - 1) == "H":
                        _, _, b, h = UNITS[k - 1]
                        hc = heads_by(k - 1)
                        cn, loc, _, _ = keys(tc, b)
                        pe.wait_ge(p_ok, hc + 1)
                        if hc:
                            pe.wait_ge(pt_a, hc)
                            pe.wait_ge(pt_v, hc)
                        flat = PS[:, 4:6, :].rearrange("p a b -> p (a b)")
                        for z in range(cn + len(loc)):
                            c0 = p_place(cn, z) * P
                            last = nc.tensor.transpose(flat[:, c0:c0 + P], pp[:, hc % 2, z * P:(z + 1) * P], ident[:])
                        last.then_inc(p_tr, 1)

                pe.wait_ge(exped, heads_by(unit_end[tc]))
                pe.wait_ge(copied, copies_by(unit_end[tc]))
                pe.wait_ge(o_lo, heads_by(unit_end[tc]) // 4)
                pe.wait_ge(pt_a, heads_by(unit_end[tc]))
                pe.wait_ge(pt_v, heads_by(unit_end[tc]))
                if tc == 2:
                    pe.wait_ge(aff_ok, ST)
                    for i in range(ST):
                        last = nc.tensor.transpose(PS[0:NE, 2 + i // 4, (i % 4) * P:(i % 4 + 1) * P], aff[:, i, :], ident[:])
                    last.then_inc(aff_tr, 1)
                for cc in range(4):
                    n = 4 * tc + cc
                    if cc >= 2:
                        pe.wait_ge(x1_ok, x1_by(tc, cc - 2))
                    for kg in range(4):
                        hi, lo = next_piece()
                        for r in range(KG):
                            kt = kg * KG + r
                            for m in range(nt):
                                s = slice(m * P, (m + 1) * P)
                                for z, (w, x) in enumerate(((ahi[:, kt, s], hi[:, r, :]), (alo[:, kt, s], hi[:, r, :]),
                                                            (ahi[:, kt, s], lo[:, r, :]))):
                                    last = nc.tensor.matmul(PS[:, 4 * (cc % 2) + m, :], w, x,
                                                            start=(kt == 0 and z == 0), stop=(kt == KT - 1 and z == 2))
                        last.then_inc(used, 1)
                pe.wait_ge(x1_ok, x1_by(tc, 3))
                if tc == 2:
                    pe.wait_ge(affT_ok, 1)
                for n in range(4 * t0, 4 * (t0 + nt) + 1):
                    if n < 4 * (t0 + nt):
                        pe.wait_ge(h2_ok, n // 4 + 1)
                        if n >= 4:
                            pe.wait_ge(h2T_ok, n - 3)
                        for r in range(4):
                            kt = 4 * (n % 4) + r
                            last = nc.tensor.transpose(PS[:, n % 4, r * P:(r + 1) * P],
                                                       x1[:, n // 4 - t0, kt * P:(kt + 1) * P], ident[:])
                        last.then_inc(h2_tr, 1)
                    if n > 4 * t0:
                        i, q = (n - 1) // 4, (n - 1) % 4
                        pe.wait_ge(h2T_ok, n)
                        if q == 0 and i >= 2:
                            pe.wait_ge(lexp_ok, i - 1)
                        for r in range(4):
                            kt = 4 * q + r
                            last = nc.tensor.matmul(PS[:, 6 + i % 2, 0:NE], h2T[:, q, r, :], wr[:, kt, :],
                                                    start=(kt == 0), stop=(kt == KT - 1))
                        last.then_inc(h2T_used, 1)

            pe.wait_ge(aff_ok, TT)
            for i in range(ST, TT):
                last = nc.tensor.transpose(PS[0:NE, 4, (i - ST) * P:(i - ST + 1) * P], aff[:, i, :], ident[:])
            last.then_inc(aff_tr, 1)
            pe.wait_ge(top_ok, 1)
            nc.tensor.transpose(PS[:, 0, 0:NE], top[:, 0:CAP_S], ident[0:NE, 0:NE])
            nc.tensor.transpose(PS[:, 0, NE:2 * NE], topf[:, 0:CAP_S], ident[0:NE, 0:NE])
            nc.tensor.transpose(PS[:, 1, 0:NE], top_q.rearrange("p a b -> p (a b)"), ident[0:NE, 0:NE])
            nc.tensor.transpose(PS[:, 1, NE:2 * NE], topf_q.rearrange("p a b -> p (a b)"),
                                ident[0:NE, 0:NE]).then_inc(top_tr, 1)
            pe.wait_ge(gate_ok, 1)

            def turn_tokens(j):
                for r in range(4):
                    kt = 4 * j + r
                    last = nc.tensor.transpose(PS[:, 4, r * P:(r + 1) * P], g_s[:, kt * P:(kt + 1) * P], ident[:])
                    if j == 0:
                        last = nc.tensor.transpose(PS[:, 5, r * P:(r + 1) * P], g_p[:, r * P:(r + 1) * P], ident[:])
                last.then_inc(x_tr, 1)

            pe.wait_ge(affT_ok, 2)
            pe.wait_ge(gs_in, 16)
            pe.wait_ge(gp_in, 16)
            for j in range(4):
                if j:
                    pe.wait_ge(x_lo, j)
                turn_tokens(j)

            with pe.Fori(0, NE) as e:
                def ktile(b, n, r, x, kt, last_kt):
                    for m in range(2):
                        w = slice(m * P, (m + 1) * P)
                        nc.tensor.matmul(PS[:, b + m, 0:2 * CAP], hi_f[:, n % NSPL_F, r, w], x, start=(kt == 0),
                                         stop=False, skip_group_check=True)
                        ins = nc.tensor.matmul(PS[:, b + m, 0:CAP], lo_f[:, n % NSPL_F, r, w], x[:, 0:CAP],
                                               start=False, stop=(kt == last_kt), skip_group_check=True)
                    return ins

                def turn_outputs(cc):
                    pe.wait_ge(yT_ok, e * 8 + 2 * cc + 2)
                    if cc:
                        pe.wait_ge(ys_ok, e * 4 + cc)
                    for m in range(4):
                        last = nc.tensor.transpose(PS[:, 6, m * P:(m + 1) * P], yT[:, cc % 2, m, :], ident[:])
                        if cc == 3:
                            last = nc.tensor.transpose(PS[:, 7, m * P:(m + 1) * P],
                                                       yTp[:, m].rearrange("p a b -> p (a b)"), ident[:])
                    last.then_inc(y_tr, 1)

                n = 0
                for q in range(FE // CF):
                    for up in range(2):
                        if q:
                            pe.wait_ge(hid_ok if up else gsum_ok, e * 4 + q)
                        for kg in range(KT // KF):
                            pe.wait_ge(f_lo_ok, e * PIECES_E + NRAW_F + n + 1)
                            for r in range(KF):
                                kt = kg * KF + r
                                if q == 0 and up == 0 and kt % 4 == 0:
                                    pe.wait_ge(x_lo, e * 4 + kt // 4 + 1)
                                last = ktile(2 * up, n, r, xT[:, kt, :], kt, KT - 1)
                            last.then_inc(f_used, 1)
                            n += 1
                for c in range(D // CF):
                    if c == 0:
                        pe.wait_ge(gsum_ok, e * 4 + 4)
                        pe.wait_ge(hid_lo, e * 4 + 3)
                    elif c == 1:
                        pe.wait_ge(hid_ok, e * 4 + 4)
                    else:
                        pe.wait_ge(yT_ok, e * 8 + c - 1)
                    pe.wait_ge(f_lo_ok, e * PIECES_E + NRAW_F + n + 1)
                    for r in range(KF):
                        if c == 0 and r == KF - 2:
                            pe.wait_ge(hid_lo, e * 4 + 4)
                        last = ktile(2 * (c % 2), n, r, hid[:, r, :], r, KF - 1)
                    last.then_inc(f_used, 1)
                    n += 1
                    if c % 2 == 0:
                        continue
                    cc = c // 2
                    if cc == 0:
                        pe.wait_ge(gs_in, e * 16 + 32)
                        pe.wait_ge(gp_in, e * 16 + 32)
                    if cc == 3:
                        turn_outputs(2)
                    pe.wait_ge(x_lo, e * 4 + 4 + cc)
                    turn_tokens(cc)
                    if cc in (1, 2):
                        turn_outputs(cc - 1)
                turn_outputs(3)

        @block.scalar
        def _(act):
            g = [0]
            steps = [0]

            def split_hi():
                n = g[0]
                g[0] += 1
                act.wait_ge(raw_in[n % NRAW], 16 * (n // NRAW + 1))
                if n >= NSPLIT:
                    act.wait_ge(used, n - NSPLIT + 1)
                nc.scalar.activation(whi[:, n % NSPLIT], raw[:, n % NRAW], ACT.Copy).then_inc(hi_ok, 1)

            def ada_rows(a):
                act.wait_ge(used, ada_pieces(a))
                if a >= 2:
                    act.wait_ge(sel_ok, a - 1)
                nc.scalar.activation(arow[0:4, a % 2, :], PS[0:4, 7, :], ACT.Copy).then_inc(arow_ok, 1)

            def mod_rows(a):
                act.wait_ge(sel_ok, a + 1)
                if a >= 2:
                    act.wait_ge(mod_out[a % 2], 16 * (a // 2))
                nc.scalar.activation(mrow[0:2, a % 2, :], PS[0:2, 6, :], ACT.Copy).then_inc(mrow_ok, 1)

            act.wait_ge(cond_tr, 1)
            nc.scalar.activation(cond_f, PS[:, 0, 0:32], ACT.Silu).then_inc(cond_f_ok, 1)
            act.wait_ge(cond_f_ok, 1)
            act.wait_ge(zero_ok, 1)
            cf = cond_f.rearrange("p (c t) -> p t c", c=2)
            nc.scalar.activation(cond_s[:, :, 0:2], cf, ACT.Copy).then_inc(cond_hi, 1)
            for a in range(ADA_A):
                for kg in range(4):
                    split_hi()
                    if kg == 1 and a:
                        ada_rows(a - 1)
                        if a > 1:
                            mod_rows(a - 2)
            ada_rows(ADA_A - 1)
            mod_rows(ADA_A - 2)
            mod_rows(ADA_A - 1)

            def stage(tc, cc):
                nt = CH[tc][1]
                act.wait_ge(used, win_pieces(tc, cc))
                if tc or cc:
                    act.wait_ge(stg_out, 16 * stores_by[5 * tc + cc])
                for m in range(nt if cc < 3 else 4):
                    w = 512 if cc < 3 else nt * P
                    nc.scalar.activation(stg[:, m, 0:w], PS[:, m, 0:w], ACT.Copy).then_inc(stg_ok, 1)

            def square(i):
                act.wait_ge(x_in[i % 2], 16 * x_loads(i))
                if i:
                    act.wait_ge(sq_ok, i)
                if i == 0:
                    act.wait_ge(tab_ok, 1)
                nc.scalar.activation(junk, xb[:, i % 2, :], ACT.Square, accum_out=ss[:, i:i + 1]).then_inc(sq_ok, 1)
                act.wait_ge(ms_ok, i + 1)
                nc.scalar.activation(st[:, 1:2], st[:, 0:1], ACT.Sqrt).then_inc(root_ok, 1)

            def turned_hi(i, t0):
                for q in range(4):
                    n = 4 * i + q
                    act.wait_ge(h_tr, n + 1)
                    nc.scalar.activation(ahi[:, 4 * q:4 * q + 4, (i - t0) * P:(i - t0 + 1) * P],
                                         PS[:, 4 + n % 2, :].rearrange("p (a b) -> p a b", a=4), ACT.Copy).then_inc(h_hi, 1)

            def finish(u):
                kd, n, cc = B_UNITS[u]
                if kd == "w":
                    stage(n, cc)
                else:
                    ada_rows(n)
                if u and B_UNITS[u - 1][0] == "a":
                    mod_rows(B_UNITS[u - 1][1])

            square(0)
            square(1)
            for u, (kd, n, cc) in enumerate(B_UNITS):
                if kd == "w" and cc == 0:
                    t0, nt, cond = CH[n]
                    for j in range(nt):
                        turned_hi(t0 + j, t0)
                        if j + 2 < nt:
                            square(t0 + j + 2)
                for kg in range(4):
                    split_hi()
                    if kg == 1 and u:
                        finish(u - 1)
                if kd == "w" and cc == 3 and n < 2:
                    square(CH[n + 1][0])
                    square(CH[n + 1][0] + 1)
            finish(len(B_UNITS) - 1)

            for tc, (t0, nt, cond) in enumerate(CH):
                for k in range(unit_start[tc], unit_end[tc] + 2):
                    if k < unit_end[tc] and kind(k) == "H":
                        _, _, b, h = UNITS[k]
                        hc = heads_by(k)
                        cn, loc, _, _ = keys(tc, b)
                        w = (cn + len(loc)) * P
                        pair = 2 * (k % 2)
                        act.wait_ge(masked, hc + 1)
                        if hc >= 2:
                            act.wait_ge(p_tr, hc - 1)
                        nc.scalar.activation(pp[:, hc % 2, 0:w], PS[:, pair:pair + 2, :].rearrange("p a b -> p (a b)")[:, 0:w],
                                             ACT.Exp, bias=sm[:, hc % 2, 1:2], scale=SCALE,
                                             accum_out=sm[:, hc % 2, 2:3]).then_inc(exped, 1)
                        nc.scalar.activation(sm[:, hc % 2, 3:4], sinks[:, 0, h:h + 1], ACT.Exp,
                                             bias=sm[:, hc % 2, 1:2]).then_inc(sank, 1)
                    if k < unit_end[tc] and kind(k) == "M":
                        gi = UNITS[k][3]
                        pair = 2 * (k % 2)
                        act.wait_ge(unit_pe, k + 1)
                        for m in range(2):
                            ct = 2 * gi + m
                            nc.scalar.activation(ahi[:, NH + ct, 0:nt * P], PS[:, pair + m, 0:nt * P], ACT.Copy,
                                                 scale=pscale[:, ct:ct + 1]).then_inc(m_hi, 1)
                    if in_chunk(k - 1, tc) and kind(k - 1) == "H":
                        hc = heads_by(k - 1)
                        cn, loc, _, _ = keys(tc, UNITS[k - 1][2])
                        act.wait_ge(p_tr, hc + 1)
                        if hc >= 2:
                            act.wait_ge(pv_ok, hc - 1)
                        w = min(4, cn + len(loc))
                        if cn == 0:
                            w = 1
                        nc.scalar.activation(pT[:, hc % 2, 0:w, :], PS[:, 4, 0:w * P].rearrange("p (a b) -> p a b", a=w),
                                             ACT.Copy).then_inc(pt_a, 1)
                    if in_chunk(k - 2, tc) and kind(k - 2) == "H" and UNITS[k - 2][3] % 4 == 3:
                        _, _, b, h = UNITS[k - 2]
                        act.wait_ge(pv_ok, heads_by(k - 2) + 1)
                        nc.scalar.activation(ahi[:, h - 3:h + 1, b * P:(b + 1) * P],
                                             PS[:, 6 + h // 4, :].rearrange("p (a b) -> p a b", a=4), ACT.Copy).then_inc(o_hi, 1)
                if tc == 2:
                    act.wait_ge(aff_tr, 1)
                    act.wait_ge(h2_out, 16 * ST)
                    act.wait_ge(x1_out, 16 * 8)
                    nc.scalar.activation(affT[:, 0:NS], PS[0:NE, 2:4, :].rearrange("p a b -> p (a b)"), ACT.Copy).then_inc(affT_ok, 1)

                def squares(cc):
                    for m in range(nt):
                        act.wait_ge(x1_ok, x1_by(tc, cc) - nt + m + 1)
                        n = 4 * (4 * tc + cc) + m if tc < 2 else 32 + 2 * cc + m
                        if n:
                            act.wait_ge(sq2_ok, n)
                        nc.scalar.activation(junk2, x1[:, m, cc * CC:(cc + 1) * CC], ACT.Square,
                                             accum_out=ss2[:, t0 + m, cc:cc + 1]).then_inc(sq2_ok, 1)

                for cc in range(4):
                    for kg in range(4):
                        split_hi()
                        if kg == 2 and cc:
                            squares(cc - 1)
                squares(3)
                act.wait_ge(ms2_ok, tc + 1)
                nc.scalar.activation(rs2[:, 1, t0:t0 + nt], rs2[:, 0, t0:t0 + nt], ACT.Sqrt).then_inc(root2_ok, 1)

                def router_exp(i):
                    act.wait_ge(lmax_ok, i + 1)
                    nc.scalar.activation(aff[:, i, :], PS[:, 6 + i % 2, 0:NE], ACT.Exp, bias=rs2[:, 4, i:i + 1],
                                         accum_out=rs2[:, 5, i:i + 1]).then_inc(lexp_ok, 1)

                for i in range(t0, t0 + nt):
                    for q in range(4):
                        n = 4 * i + q
                        act.wait_ge(h2_tr, n + 1)
                        if n >= 4:
                            act.wait_ge(h2T_used, n - 3)
                        nc.scalar.activation(h2T[:, q], PS[:, q, :].rearrange("p (a b) -> p a b", a=4), ACT.Copy).then_inc(h2T_ok, 1)
                    if i > t0:
                        router_exp(i - 1)
                router_exp(t0 + nt - 1)

            act.wait_ge(aff_tr, 2)
            nc.scalar.activation(affT[:, NS:NS + NP_], PS[0:NE, 4, 0:NP_], ACT.Copy).then_inc(affT_ok, 1)

            def take_hi(j):
                if j == 0:
                    nc.scalar.activation(xT[:, :, CAP_S:CAP].rearrange("p (m r) t -> p m r t", m=Q),
                                         PS[:, 5, :].rearrange("p (r m t) -> p m r t", m=Q, t=CAP_P), ACT.Copy)
                nc.scalar.activation(xT[:, 4 * j:4 * j + 4, 0:CAP_S], PS[:, 4, :].rearrange("p (a b) -> p a b", a=4),
                                     ACT.Copy).then_inc(x_hi, 1)

            def split_f(n, e):
                act.wait_ge(raw_f_in[n % NRAW_F], e * (16 * PIECES_E // NRAW_F) + 16 * (n // NRAW_F + 1))
                nc.scalar.activation(hi_f[:, n % NSPL_F], raw_f[:, n % NRAW_F], ACT.Copy).then_inc(f_hi_ok, 1)

            for n in range(NSPL_F):
                split_f(n, 0)
            for j in range(4):
                act.wait_ge(x_tr, j + 1)
                take_hi(j)

            def expert_hi(e, more):
                for n in range(PIECES_E):
                    act.wait_ge(f_used, e * PIECES_E + n + 1)
                    if n < 16 and n % 4 == 1:
                        nc.scalar.activation(part[:, 0, :].rearrange("p (a b) -> p a b", a=2), PS[:, 0:2, CAP:2 * CAP],
                                             ACT.Copy).then_inc(part_ok, 1)
                        act.wait_ge(gsum_ok, e * 4 + n // 4 + 1)
                        nc.scalar.activation(hg[:], gsum[:], ACT.Silu).then_inc(silu_ok, 1)
                    if n < 16 and n % 4 == 3:
                        nc.scalar.activation(part[:, 1, :].rearrange("p (a b) -> p a b", a=2), PS[:, 2:4, CAP:2 * CAP],
                                             ACT.Copy).then_inc(part_ok, 1)
                        act.wait_ge(hid_ok, e * 4 + n // 4 + 1)
                        nc.scalar.activation(hid[:, n // 4 * 2:n // 4 * 2 + 2, 0:CAP],
                                             hraw[:].rearrange("p (a b) -> p a b", a=2), ACT.Copy).then_inc(hid_hi, 1)
                    if n >= 16:
                        c = n - 16
                        b = 2 * (c % 2)
                        if c >= 2:
                            act.wait_ge(yT_ok, e * 8 + c - 1)
                        nc.scalar.activation(part[:, c % 2, :].rearrange("p (a b) -> p a b", a=2),
                                             PS[:, b:b + 2, CAP:2 * CAP], ACT.Copy).then_inc(part_ok, 1)
                        if c % 2:
                            act.wait_ge(x_tr, e * 4 + 5 + c // 2)
                            take_hi(c // 2)
                    if n + NSPL_F < PIECES_E:
                        split_f(n + NSPL_F, e)
                    elif more:
                        split_f(n + NSPL_F - PIECES_E, e + 1)
                act.wait_ge(yT_ok, e * 8 + 8)

            with act.Fori(0, NE - 1) as e:
                expert_hi(e, True)
            expert_hi(NE - 1, False)

            for i in range(TT):
                act.wait_ge(f_in[i % NF], 16 * (i // NF + 1))
                if i >= NF:
                    act.wait_ge(f_out[i % NF], 16 * (i // NF))
                nc.scalar.activation(fin[:, NF + i % NF],
                                     fin[:, i % NF], ACT.Square,
                                     accum_out=ss[:, TT + i:TT + i + 1]).then_inc(f_sq, 1)
                act.wait_ge(f_ms, i + 1)
                nc.scalar.activation(st[:, 1:2], st[:, 0:1], ACT.Sqrt).then_inc(f_root, 1)

        @block.vector
        def _(dve):
            g = [0]
            steps = [0]

            def link(ins):
                steps[0] += 1
                ins.then_inc(dve_step, 1)
                dve.wait_ge(dve_step, steps[0])

            def split_lo():
                n = g[0]
                g[0] += 1
                dve.wait_ge(hi_ok, n + 1)
                nc.vector.tensor_tensor(wlo[:, n % NSPLIT], raw[:, n % NRAW], whi[:, n % NSPLIT].bitcast(F32),
                                        ALU.subtract).then_inc(lo_ok, 1)

            def rstd(col, n, sq, ms, root):
                dve.wait_ge(sq, n)
                nc.vector.tensor_scalar(st[:, 0:1], ss[:, col:col + 1], 1.0 / D, EPS, ALU.mult, ALU.add).then_inc(ms, 1)
                dve.wait_ge(root, n)
                link(nc.vector.reciprocal(st[:, 2:3], st[:, 1:2]))
                link(nc.vector.scalar_tensor_tensor(out=st[:, 3:4], in0=st[:, 2:3], scalar=st[:, 2:3], in1=st[:, 0:1],
                                                    op0=ALU.mult, op1=ALU.mult))
                link(nc.vector.tensor_scalar(st[:, 3:4], st[:, 3:4], -0.5, 1.5, ALU.mult, ALU.add))
                link(nc.vector.tensor_tensor(st[:, 4:5], st[:, 2:3], st[:, 3:4], ALU.mult))

            nc.vector.memset(cond_s[:].bitcast(F32), 0.0).then_inc(zero_ok, 1)
            dve.wait_ge(cond_hi, 1)
            cf = cond_f.rearrange("p (c t) -> p t c", c=2)
            nc.vector.tensor_tensor(cond_s[:, :, 2:4], cf, cond_s[:, :, 0:2].bitcast(F32), ALU.subtract).then_inc(cond_lo, 1)
            for _ in range(4 * ADA_A):
                split_lo()

            def scale_table(n):
                dve.wait_ge(tab_in, 16 * (2 * n + 2))
                if n:
                    dve.wait_ge(x_in[0], 16 * (x_loads(ST) - 1))
                else:
                    dve.wait_ge(nmix_in, 16)
                w = xb[:, 0, :] if n else nmix
                nc.vector.scalar_tensor_tensor(out=tabA, in0=tabA, scalar=1.0, in1=w,
                                               op0=ALU.add, op1=ALU.mult).then_inc(tab_ok, 1)
                dve.wait_ge(tab_ok, n + 1)

            def modulated(i):
                rstd(i, i + 1, sq_ok, ms_ok, root_ok)
                x = xb[:, i % 2, :]
                link(nc.vector.scalar_tensor_tensor(out=x, in0=x, scalar=st[:, 4:5], in1=tabA,
                                                    op0=ALU.mult, op1=ALU.mult))
                nc.vector.tensor_tensor(x, x, tabS, ALU.add).then_inc(h_ok, 1)

            def turned_lo(i, t0):
                for q in range(4):
                    n = 4 * i + q
                    dve.wait_ge(h_hi, n + 1)
                    s = (slice(None), slice(4 * q, 4 * q + 4), slice((i - t0) * P, (i - t0 + 1) * P))
                    nc.vector.tensor_tensor(alo[s], PS[:, 4 + n % 2, :].rearrange("p (a b) -> p a b", a=4),
                                            ahi[s].bitcast(F32), ALU.subtract).then_inc(h_lo, 1)

            scale_table(0)
            modulated(0)
            modulated(1)
            for u, (kd, n, cc) in enumerate(B_UNITS):
                if kd == "w" and cc == 0:
                    t0, nt, cond = CH[n]
                    for j in range(nt):
                        turned_lo(t0 + j, t0)
                        if j + 2 < nt:
                            modulated(t0 + j + 2)
                for _ in range(4):
                    split_lo()
                if kd == "w" and cc == 3 and n < 2:
                    if CH[n + 1][2]:
                        scale_table(1)
                    modulated(CH[n + 1][0])
                    modulated(CH[n + 1][0] + 1)

            for tc, (t0, nt, cond) in enumerate(CH):
                for k in range(unit_start[tc], unit_end[tc] + 2):
                    if in_chunk(k - 1, tc) and kind(k - 1) == "H":
                        hc = heads_by(k - 1)
                        cn, loc, _, _ = keys(tc, UNITS[k - 1][2])
                        w = (cn + len(loc)) * P
                        s = sm[:, hc % 2, :]
                        dve.wait_ge(sank, hc + 1)
                        link(nc.vector.tensor_tensor(s[:, 4:5], s[:, 2:3], s[:, 3:4], ALU.add))
                        link(nc.vector.reciprocal(s[:, 5:6], s[:, 4:5]))
                        nc.vector.tensor_scalar(pp[:, hc % 2, 0:w], pp[:, hc % 2, 0:w], s[:, 5:6], None,
                                                ALU.mult).then_inc(p_ok, 1)
                    if k < unit_end[tc]:
                        _, kd, b, h = UNITS[k]
                        pair = 2 * (k % 2)
                        flat = PS[:, pair:pair + 2, :].rearrange("p a b -> p (a b)")
                        dve.wait_ge(unit_pe, k + 1)
                        if kd == "H":
                            hc = heads_by(k)
                            cn, loc, ml, mr = keys(tc, b)
                            w = (cn + len(loc)) * P
                            s = sm[:, hc % 2, :]
                            if ml:
                                v = flat[:, cn * P:(cn + 1) * P]
                                link(nc.vector.tensor_tensor(v, v, maskL[:], ALU.add))
                            if mr:
                                v = flat[:, w - P:w]
                                link(nc.vector.tensor_tensor(v, v, maskR[:], ALU.add))
                            link(nc.vector.reduce_max(s[:, 0:1], flat[:, 0:w], AXX))
                            nc.vector.tensor_scalar(s[:, 1:2], s[:, 0:1], -SCALE, sinks[:, 1, h:h + 1],
                                                    ALU.mult, ALU.min).then_inc(masked, 1)
                        elif kd == "K":
                            nk = 9 if cond == 0 else 2
                            if tc:
                                dve.wait_ge(h2_out, 16 * t0)
                            z0, z1 = h * 8, min(h * 8 + 8, 2 * nk)
                            nc.vector.tensor_copy(kT[:, z0 * P:z1 * P], flat[:, 0:(z1 - z0) * P]).then_inc(copied, 1)
                        elif kd == "Q":
                            nc.vector.tensor_copy(qT.rearrange("p a b -> p (a b)"), flat).then_inc(copied, 1)
                        else:
                            dve.wait_ge(m_hi, 2 * (m_by(k) + 1))
                            for m in range(2):
                                ct = 2 * h + m
                                ins = nc.vector.scalar_tensor_tensor(
                                    out=alo[:, NH + ct, 0:nt * P], in0=PS[:, pair + m, 0:nt * P],
                                    scalar=pscale[:, ct:ct + 1], in1=ahi[:, NH + ct, 0:nt * P].bitcast(F32),
                                    op0=ALU.mult, op1=ALU.subtract)
                            ins.then_inc(copied, 1)
                    if in_chunk(k - 1, tc) and kind(k - 1) == "H":
                        hc = heads_by(k - 1)
                        cn, loc, _, _ = keys(tc, UNITS[k - 1][2])
                        dve.wait_ge(p_tr, hc + 1)
                        if hc >= 2:
                            dve.wait_ge(pv_ok, hc - 1)
                        z0 = 4 if cn else 1
                        z1 = cn + len(loc)
                        flat = PS[:, 4:6, :].rearrange("p a b -> p (a b)")
                        c0 = p_place(cn, z0) * P
                        nc.vector.tensor_copy(pT[:, hc % 2, z0:z1, :],
                                              flat[:, c0:c0 + (z1 - z0) * P].rearrange("p (a b) -> p a b", b=P)).then_inc(pt_v, 1)
                    if in_chunk(k - 2, tc) and kind(k - 2) == "H" and UNITS[k - 2][3] % 4 == 3:
                        _, _, b, h = UNITS[k - 2]
                        dve.wait_ge(o_hi, (heads_by(k - 2) + 1) // 4)
                        s = (slice(None), slice(h - 3, h + 1), slice(b * P, (b + 1) * P))
                        nc.vector.tensor_tensor(alo[s], PS[:, 6 + h // 4, :].rearrange("p (a b) -> p a b", a=4),
                                                ahi[s].bitcast(F32), ALU.subtract).then_inc(o_lo, 1)

                def residual(cc):
                    dve.wait_ge(used, D0 + 4 * (4 * tc + cc + 1))
                    s = slice(cc * CC, (cc + 1) * CC)
                    for m in range(nt):
                        v = PS[:, 4 * (cc % 2) + m, :]
                        link(nc.vector.tensor_tensor(v, v, tabG[:, s], ALU.mult))
                        nc.vector.tensor_tensor(x1[:, m, s], x1[:, m, s], v, ALU.add).then_inc(x1_ok, 1)

                def top_round(c0, c1, k):
                    v, s = affT[:, c0:c1], slice(k, k + 8)
                    link(nc.vector.max(top[:, s], v))
                    link(nc.vector.max_index(topi[:, s], top[:, s], v))
                    link(nc.vector.match_replace(v, top[:, s], v, -1.0))

                for cc in range(4):
                    for kg in range(4):
                        split_lo()
                        if kg == 1 and cc:
                            if cc == 1:
                                dve.wait_ge(dtab_in, 16 * (4 * tc + 4))
                                dve.wait_ge(x1_in, 16 * (t0 + nt))
                            residual(cc - 1)
                        if tc == 2:
                            if cc == 0 and kg == 0:
                                dve.wait_ge(affT_ok, 1)
                            top_round(0, NS, 8 * (4 * cc + kg))
                nc.vector.scalar_tensor_tensor(out=tabA2, in0=tabA2, scalar=1.0, in1=nffn, op0=ALU.add,
                                               op1=ALU.mult).then_inc(dtab_ok, 1)
                residual(3)
                cs = slice(t0, t0 + nt)
                dve.wait_ge(sq2_ok, x1_by(tc, 3))
                link(nc.vector.reduce_sum(rs2[:, 0, cs], ss2[:, cs, :], AXX))
                nc.vector.tensor_scalar(rs2[:, 0, cs], rs2[:, 0, cs], 1.0 / D, EPS, ALU.mult, ALU.add).then_inc(ms2_ok, 1)
                dve.wait_ge(root2_ok, tc + 1)
                link(nc.vector.reciprocal(rs2[:, 2, cs], rs2[:, 1, cs]))
                link(nc.vector.tensor_tensor(rs2[:, 3, cs], rs2[:, 2, cs], rs2[:, 2, cs], ALU.mult))
                link(nc.vector.tensor_tensor(rs2[:, 3, cs], rs2[:, 3, cs], rs2[:, 0, cs], ALU.mult))
                link(nc.vector.tensor_scalar(rs2[:, 3, cs], rs2[:, 3, cs], -0.5, 1.5, ALU.mult, ALU.add))
                link(nc.vector.tensor_tensor(rs2[:, 2, cs], rs2[:, 2, cs], rs2[:, 3, cs], ALU.mult))
                dve.wait_ge(x1_out, 16 * 4 * (tc + 1))
                dve.wait_ge(dtab_ok, tc + 1)

                def router_max(i):
                    dve.wait_ge(h2T_used, 4 * i + 4)
                    nc.vector.tensor_reduce(rs2[:, 4, i:i + 1], PS[:, 6 + i % 2, 0:NE], AXX, ALU.max,
                                            negate=True).then_inc(lmax_ok, 1)

                for i in range(t0, t0 + nt):
                    x = x1[:, i - t0, :]
                    link(nc.vector.scalar_tensor_tensor(out=x, in0=x, scalar=rs2[:, 2, i:i + 1], in1=tabA2,
                                                        op0=ALU.mult, op1=ALU.mult))
                    nc.vector.tensor_tensor(x, x, tabS2, ALU.add).then_inc(h2_ok, 1)
                    if i > t0:
                        router_max(i - 1)
                router_max(t0 + nt - 1)
                dve.wait_ge(lexp_ok, t0 + nt)
                link(nc.vector.reciprocal(rs2[:, 3, cs], rs2[:, 5, cs]))
                for i in range(t0, t0 + nt):
                    nc.vector.tensor_scalar(aff[:, i, :], aff[:, i, :], rs2[:, 3, i:i + 1], None, ALU.mult).then_inc(aff_ok, 1)

            link(nc.vector.memset(idx_s[:], 0))
            link(nc.vector.memset(idx_p[:], 0))
            dve.wait_ge(affT_ok, 2)
            nc.vector.nop().then_inc(f_lo_ok, NRAW_F)
            for r in range(CAP_P // 8):
                top_round(NS, NS + NP_, CAP_S + 8 * r)
            link(nc.vector.tensor_copy(topf, topi))
            for m in range(Q):
                nc.vector.tensor_copy(top_q[:, m, :], top[:, CAP_S:CAP])
                ins = nc.vector.tensor_scalar(topf_q[:, m, :], topf[:, CAP_S:CAP], float(Q), float(m), ALU.mult, ALU.add)
            ins.then_inc(top_ok, 1)
            dve.wait_ge(top_tr, 1)
            link(nc.vector.tensor_copy(gate_s[:], PS[:, 0, 0:NE]))
            link(nc.vector.tensor_copy(gate_p[:], PS[:, 1, 0:NE]))
            link(nc.vector.tensor_copy(idx_s[:, 0:NE], PS[:, 0, NE:2 * NE]))
            link(nc.vector.tensor_copy(idx_p[:, 0:NE], PS[:, 1, NE:2 * NE]))
            nc.vector.tensor_copy(ig_s[:], idx_s[:, 0:1])
            nc.vector.tensor_copy(ig_p[:], idx_p[:, 0:1]).then_inc(gate_ok, 1)

            def take_lo(j):
                dve.wait_ge(x_hi, xh[0] + j + 1)
                if j == 0:
                    hi, lo = (xT[:, :, z + CAP_S:z + CAP].rearrange("p (m r) t -> p m r t", m=Q) for z in (0, CAP))
                    nc.vector.tensor_tensor(lo, PS[:, 5, :].rearrange("p (r m t) -> p m r t", m=Q, t=CAP_P),
                                            hi.bitcast(F32), ALU.subtract)
                nc.vector.tensor_tensor(xT[:, 4 * j:4 * j + 4, CAP:CAP + CAP_S],
                                        PS[:, 4, :].rearrange("p (a b) -> p a b", a=4),
                                        xT[:, 4 * j:4 * j + 4, 0:CAP_S].bitcast(F32), ALU.subtract).then_inc(x_lo, 1)

            def split_f(n, e):
                dve.wait_ge(f_hi_ok, e * PIECES_E + n + 1)
                nc.vector.tensor_tensor(lo_f[:, n % NSPL_F], raw_f[:, n % NRAW_F], hi_f[:, n % NSPL_F].bitcast(F32),
                                        ALU.subtract).then_inc(f_lo_ok, 1)

            xh = [0]
            for n in range(NSPL_F):
                split_f(n, 0)
            for j in range(4):
                take_lo(j)
            dve.wait_ge(g2_in, 16 * (1 + Q))

            def expert_lo(e, more):
                xh[0] = e * 4 + 4
                dve.wait_ge(gs_in, e * 16 + 16)
                dve.wait_ge(gp_in, e * 16 + 16)
                nc.vector.tensor_copy(ig_s[:], idx_s[:, bass.ds(e + 1, 1)])
                nc.vector.tensor_copy(ig_p[:], idx_p[:, bass.ds(e + 1, 1)]).then_inc(ig_ok, 1)

                def scale_rows(c):
                    s = slice(c * CC, (c + 1) * CC)
                    dve.wait_ge(y_tr, e * 4 + c + 1)
                    nc.vector.scalar_tensor_tensor(out=y_s[:, s], in0=PS[:, 6, :], scalar=gate_s[:, bass.ds(e, 1)],
                                                   in1=g2_s[:, s], op0=ALU.mult, op1=ALU.mult).then_inc(ys_ok, 1)
                    if c == 3:
                        nc.vector.scalar_tensor_tensor(out=y_p[:], in0=PS[:, 7, :], scalar=gate_p[:, bass.ds(e, 1)],
                                                       in1=g2_p[:], op0=ALU.mult, op1=ALU.mult).then_inc(yp_ok, 1)

                for n in range(PIECES_E):
                    if n < 16 and n % 4 == 1:
                        dve.wait_ge(part_ok, e * 16 + n // 2 + 1)
                        nc.vector.tensor_tensor(gsum[:].rearrange("p (a b) -> p a b", a=2), PS[:, 0:2, 0:CAP],
                                                part[:, 0, :].rearrange("p (a b) -> p a b", a=2),
                                                ALU.add).then_inc(gsum_ok, 1)
                    if n < 16 and n % 4 == 3:
                        dve.wait_ge(part_ok, e * 16 + n // 2 + 1)
                        nc.vector.tensor_tensor(usum[:].rearrange("p (a b) -> p a b", a=2), PS[:, 2:4, 0:CAP],
                                                part[:, 1, :].rearrange("p (a b) -> p a b", a=2),
                                                ALU.add).then_inc(usum_ok, 1)
                        dve.wait_ge(usum_ok, e * 4 + n // 4 + 1)
                        dve.wait_ge(silu_ok, e * 4 + n // 4 + 1)
                        nc.vector.tensor_tensor(hraw[:], hg[:], usum[:], ALU.mult).then_inc(hid_ok, 1)
                        dve.wait_ge(hid_hi, e * 4 + n // 4 + 1)
                        h = hid[:, n // 4 * 2:n // 4 * 2 + 2, :]
                        nc.vector.tensor_tensor(h[:, :, CAP:2 * CAP], hraw[:].rearrange("p (a b) -> p a b", a=2),
                                                h[:, :, 0:CAP].bitcast(F32), ALU.subtract).then_inc(hid_lo, 1)
                    if n >= 16:
                        c = n - 16
                        cc = c // 2
                        if c == 0:
                            dve.wait_ge(y_free, e + 1)
                            nc.vector.tensor_copy(ic_s[:], idx_s[:, bass.ds(e, 1)])
                            nc.vector.tensor_copy(ic_p[:], idx_p[:, bass.ds(e, 1)]).then_inc(ic_ok, 1)
                        dve.wait_ge(part_ok, e * 16 + 9 + c)
                        b = 2 * (c % 2)
                        lo = part[:, c % 2, :].rearrange("p (a b) -> p a b", a=2)
                        nc.vector.tensor_tensor(yTp[:, b:b + 2, cc, :], PS[:, b:b + 2, CAP_S:CAP], lo[:, :, CAP_S:CAP], ALU.add)
                        nc.vector.tensor_tensor(yT[:, cc % 2, b:b + 2, :], PS[:, b:b + 2, 0:CAP_S], lo[:, :, 0:CAP_S],
                                                ALU.add).then_inc(yT_ok, 1)
                        if c % 2:
                            if cc == 3:
                                scale_rows(2)
                            take_lo(cc)
                            if cc in (1, 2):
                                scale_rows(cc - 1)
                            if cc == 3:
                                scale_rows(3)
                    if n + NSPL_F < PIECES_E:
                        split_f(n + NSPL_F, e)
                    elif more:
                        split_f(n + NSPL_F - PIECES_E, e + 1)

            with dve.Fori(0, NE - 1) as e:
                expert_lo(e, True)
            expert_lo(NE - 1, False)

            dve.wait_ge(nf_in, 16)
            for i in range(TT):
                rstd(TT + i, i + 1, f_sq, f_ms, f_root)
                nc.vector.scalar_tensor_tensor(out=fin[:, NF + i % NF],
                                               in0=fin[:, i % NF], scalar=st[:, 4:5],
                                               in1=fin[:, 2 * NF],
                                               op0=ALU.mult, op1=ALU.mult).then_inc(f_ok, 1)

        @block.gpsimd
        def _(pool):
            steps = [0]
            dma = nc.gpsimd.dma_start

            def link(ins):
                steps[0] += 1
                ins.then_inc(pool_step, 1)
                pool.wait_ge(pool_step, steps[0])

            dma(cond_r[0:16, :], t["c"].rearrange("b (t p) -> (b t) p", p=P)).then_inc(cond_in, 16)
            dma(cond_r[16:32, :], t["c_ctx"].rearrange("(t p) -> t p", p=P)).then_inc(cond_in, 16)
            dma(ident[:], t["k_ident"]).then_inc(consts_in, 16)
            dma(sel[:], t["k_sel"]).then_inc(consts_in, 16)
            dma(maskL[:], t["k_mask"][0]).then_inc(consts_in, 16)
            dma(maskR[:], t["k_mask"][1]).then_inc(consts_in, 16)
            dma(sinks[:, 0, :], t["sink_logits"][0].partition_broadcast(P)).then_inc(consts_in, 16)
            dma(sinks[:, 1, :], t["sink_logits"][0].partition_broadcast(P)).then_inc(consts_in, 16)
            dma(pscale[:], t["pool_scale"]).then_inc(consts_in, 16)
            for z in range(4):
                dma(wr[:, 4 * z:4 * z + 4, :],
                    t["w_router"][0, z * 512:(z + 1) * 512].rearrange("(t p) e -> p t e", p=P)).then_inc(consts_in, 16)

            def bias_row(a):
                if a >= 2:
                    pool.wait_ge(sel_ok, a - 1)
                dma(arow[4:5, a % 2, :], t["b_ada"][:, a * CC:(a + 1) * CC]).then_inc(brow_in[a % 2], 16)

            def store_mod(a):
                pool.wait_ge(mrow_ok, a + 1)
                dma(mod_d[:, a * CC:(a + 1) * CC], mrow[0:2, a % 2, :]).then_inc(mod_out[a % 2], 16)

            def mods_stored(n):
                pool.wait_ge(mod_out[0], 16 * ((n + 1) // 2))
                pool.wait_ge(mod_out[1], 16 * (n // 2))

            def table(dst, cond, m, n=P):
                return dma(dst, mod_d[cond, m * D:(m + 1) * D].partition_broadcast(n))

            def load_x(i):
                if i >= 2:
                    pool.wait_ge(h_tr, 4 * (i - 1))
                dma(xb[:, i % 2, :], rows(xs, xp, i)).then_inc(x_in[i % 2], 16)

            bias_row(0)
            bias_row(1)
            pool.wait_ge(consts_in, 16 * N_CONST)
            link(nc.gpsimd.tensor_scalar(sinks[:, 1, :], sinks[:, 1, :], -1.0, None, ALU.mult))
            dma(nmix, t["norm_mix"][0].partition_broadcast(P)).then_inc(nmix_in, 16)
            pool.wait_ge(nmix_in, 16)
            dma(xb[:, 0, :], rows(xs, xp, 0)).then_inc(x_in[0], 16)
            load_x(1)
            for a in range(ADA_A):
                store_mod(a)
                bias_row(a + 2)
                if a == ADA_A // 2 - 1:
                    mods_stored(ADA_A // 2)
                    table(tabS, 0, 0).then_inc(tab_in, 16)
            mods_stored(ADA_A)
            table(tabA, 0, 1).then_inc(tab_in, 16)

            def store_projection(tc, cc):
                t0, nt, cond = CH[tc]
                for m in range(nt if cc < 3 else 4):
                    pool.wait_ge(stg_ok, staged_by(5 * tc + cc) + m + 1)
                    i = t0 + m
                    if cc == 3 or cc == 4:
                        ct = (cc - 3) * 4 + m
                        dma(pool_d[ct * P:(ct + 1) * P, t0 * P:(t0 + nt) * P], stg[:, m, 0:nt * P]).then_inc(stg_out, 16)
                        continue
                    if cond == 0:
                        nr = 8 if cc < 2 else 4
                        dma(rtab, t["k_rope"][i]).then_inc(rtab_in, 16)
                        s = stg[:, m, 0:nr * 64].rearrange("p (a h f) -> p a h f", h=2, f=32)
                        a1, a2 = s[:, :, 0, :], s[:, :, 1, :]
                        cs, sn = (rtab[:, z, 0:nr * 32].rearrange("p (a f) -> p a f", f=32) for z in range(2))
                        r = [rt[:, z, 0:nr * 32].rearrange("p (a f) -> p a f", f=32) for z in range(4)]
                        pool.wait_ge(rtab_in, 16 * (3 * 4 * tc + 4 * cc + m + 1))
                        nc.gpsimd.tensor_tensor(r[0], a1, cs, ALU.mult)
                        nc.gpsimd.tensor_tensor(r[1], a2, sn, ALU.mult)
                        nc.gpsimd.tensor_tensor(r[2], a1, sn, ALU.mult)
                        link(nc.gpsimd.tensor_tensor(r[3], a2, cs, ALU.mult))
                        nc.gpsimd.tensor_tensor(a1, r[0], r[1], ALU.subtract)
                        link(nc.gpsimd.tensor_tensor(a2, r[2], r[3], ALU.add))
                    dma(qkv_d[i * P:(i + 1) * P, cc * CC:(cc + 1) * CC], stg[:, m, :]).then_inc(stg_out, 16)
                    if cond and cc == 2:
                        dma(st_k[m * P:(m + 1) * P, :], stg[:, m, 0:KW]).then_inc(stg_out, 16)
                        dma(st_v[m * P:(m + 1) * P, :], stg[:, m, KW:2 * KW]).then_inc(stg_out, 16)

            def load_rest(tc):
                for j in range(2, CH[tc][1]):
                    load_x(CH[tc][0] + j)

            def load_first(i):
                dma(xb[:, 0, :], rows(xs, xp, i)).then_inc(x_in[0], 16)
                dma(xb[:, 1, :], rows(xs, xp, i + 1)).then_inc(x_in[1], 16)

            load_rest(0)
            for u, (kd, n, cc) in enumerate(B_UNITS):
                if kd == "a":
                    if u + 1 < len(B_UNITS) and B_UNITS[u + 1][0] == "w" and B_UNITS[u + 1][2] == 0:
                        load_rest(B_UNITS[u + 1][1])
                    if B_UNITS[u + 1:u + 2] == [("w", 1, 3)]:
                        pool.wait_ge(tab_ok, 2)
                        load_first(ST)
                    store_mod(n)
                    if n + 2 < NADA:
                        bias_row(n + 2)
                    continue
                t0, nt, cond = CH[n]
                store_projection(n, cc)
                if cc == 1 and n < 2:
                    nxt = CH[n + 1][0]
                    pool.wait_ge(h_tr, 4 * nxt)
                    if CH[n + 1][2] == cond:
                        load_first(nxt)
                    else:
                        pool.wait_ge(h_ok, nxt)
                        table(tabS, 1, 0).then_inc(tab_in, 16)
                        table(tabA, 1, 1).then_inc(tab_in, 16)
                        dma(xb[:, 0, :], t["norm_mix"][0].partition_broadcast(P)).then_inc(x_in[0], 16)
            mods_stored(NADA)
            pool.wait_ge(stg_out, 16 * stores_by[-1])
            pool.wait_ge(used, D0)
            pool.wait_ge(lo_ok, D0)

            def load_q(i):
                if i:
                    k = max(z for z in range(n_units) if UNITS[z][1] == "Q" and CH[UNITS[z][0]][0] + UNITS[z][2] == i - 1)
                    pool.wait_ge(unit_pe, k + 1)
                dma(qq, qkv_d[i * P:(i + 1) * P, 0:AW]).then_inc(q_in, 16)

            def mixer(tc, gi):
                t0, nt, cond = CH[tc]
                T = nt * P
                w, L = POOLS[gi], T + 2 * HALO
                n = 4 * tc + gi
                first = t0 in (0, ST)
                final = t0 + nt in (ST, TT)
                c0, c1 = (HALO if first else 0), T + 2 * HALO - (HALO if final else 0)
                if n:
                    pool.wait_ge(mixed, n)
                    pool.wait_ge(unit_pe, m_unit(n - 1) + 1)
                if first:
                    link(nc.gpsimd.memset(pin[:, :, 0:HALO], 0.0))
                if final:
                    link(nc.gpsimd.memset(pin[:, :, HALO + T:L], 0.0))
                dma(pw, t["pool_w"][0, gi].rearrange("(z p) n -> p z n", p=P)).then_inc(pin_in, 16)
                dma(rcnt[:, 0:T], t["k_rcnt"][gi, t0 * P:t0 * P + T].partition_broadcast(P)).then_inc(pin_in, 16)
                for z in range(2):
                    ct = 2 * gi + z
                    dma(pin[:, z, c0:c1], pool_d[ct * P:(ct + 1) * P, t0 * P - HALO + c0:t0 * P - HALO + c1]).then_inc(pin_in, 16)
                pool.wait_ge(pin_in, 64 * (n + 1))
                link(nc.gpsimd.tensor_tensor(pa[:, :, 1:L], pin[:, :, 0:L - 1], pin[:, :, 1:L], ALU.add))
                src, dst, lo, hi, half = pa, pb, 1, L, 1
                while 2 * half < w:
                    link(nc.gpsimd.tensor_tensor(dst[:, :, lo + half:hi - half], src[:, :, lo:hi - 2 * half],
                                                 src[:, :, lo + 2 * half:hi], ALU.add))
                    lo, hi = lo + half, hi - half
                    src, dst, half = dst, src, 2 * half
                for z in range(2):
                    link(nc.gpsimd.tensor_tensor(src[:, z, HALO:HALO + T], src[:, z, HALO:HALO + T], rcnt[:, 0:T], ALU.mult))
                nc.gpsimd.tensor_tensor(mixT[:, :, 0:T], src[:, :, HALO:HALO + T], pin[:, :, HALO:HALO + T],
                                        ALU.subtract).then_inc(mixed, 1)

            for tc, (t0, nt, cond) in enumerate(CH):
                if tc:
                    pool.wait_ge(h2_ok, t0)
                if cond == 0:
                    k0 = max(0, t0 - 1)
                    for dst, cache, col in ((ktm, ck, AW), (vv, cv, AW + KW)):
                        dma(dst[:, 0:4, :], cache.rearrange("(b p) d -> p b d", p=P)).then_inc(kv_in, 16)
                        dma(dst[:, 4:9, :], qkv_d[k0 * P:(k0 + 5) * P, col:col + KW].rearrange("(b p) d -> p b d", p=P)).then_inc(kv_in, 16)
                else:
                    for dst, col in ((ktm, AW), (vv, AW + KW)):
                        dma(dst[:, 0:2, :], qkv_d[NS:NS + NP_, col:col + KW].rearrange("(b p) d -> p b d", p=P)).then_inc(kv_in, 16)
                load_q(t0)
                if tc:
                    pool.wait_ge(h2_out, 16 * t0)
                    pool.wait_ge(h2T_used, 4 * t0)
                per = 4 // nt
                for b in range(nt):
                    if b + 1 < nt:
                        pool_next = t0 + b + 1
                    for gi in range(b * per, b * per + per):
                        mixer(tc, gi)
                    if b + 1 < nt:
                        load_q(pool_next)

                pool.wait_ge(pv_ok, heads_by(unit_end[tc]))
                pool.wait_ge(unit_pe, unit_end[tc])
                pool.wait_ge(o_lo, heads_by(unit_end[tc]) // 4)
                pool.wait_ge(copied, copies_by(unit_end[tc]))
                pool.wait_ge(pt_a, heads_by(unit_end[tc]))
                table(tabG, cond, 2).then_inc(dtab_in, 16)
                table(tabA2, cond, 4).then_inc(dtab_in, 16)
                table(tabS2, cond, 3).then_inc(dtab_in, 16)
                dma(nffn, t["norm_ffn"][0].partition_broadcast(P)).then_inc(dtab_in, 16)
                for j in range(nt):
                    dma(x1[:, j, :], rows(xs, xp, t0 + j)).then_inc(x1_in, 16)
                for cc in range(4):
                    pool.wait_ge(x1_ok, x1_by(tc, cc))
                    a = res_p if cond else res_s[t0 * P:(t0 + nt) * P, :]
                    dma(a[:, cc * CC:(cc + 1) * CC].rearrange("(j p) n -> p j n", p=P),
                        x1[:, 0:nt, cc * CC:(cc + 1) * CC]).then_inc(x1_out, 16)
                for j in range(nt):
                    pool.wait_ge(h2_ok, t0 + j + 1)
                    dma(rows(h2_s, h2_p, t0 + j), x1[:, j, :]).then_inc(h2_out, 16)
            pool.wait_ge(x1_out, 16 * 12)
            pool.wait_ge(h2_out, 16 * TT)

            pool.wait_ge(gate_ok, 1)
            table(g2_s[:], 0, 5).then_inc(g2_in, 16)
            for m in range(Q):
                dma(g2_p[m * CAP_P:(m + 1) * CAP_P, :],
                    mod_d[1, 5 * D + m * DQ:5 * D + (m + 1) * DQ].partition_broadcast(CAP_P)).then_inc(g2_in, 16)

            def gather():
                nc.gpsimd.indirect_dma_start(out=g_s[:], out_offset=None, in_=h2_s,
                                             in_offset=bass.IndirectOffsetOnAxis(ap=ig_s[:, 0:1], axis=0)).then_inc(gs_in, 16)
                nc.gpsimd.indirect_dma_start(out=g_p[:], out_offset=None, in_=h2_q,
                                             in_offset=bass.IndirectOffsetOnAxis(ap=ig_p[:, 0:1], axis=0)).then_inc(gp_in, 16)

            gather()
            nc.gpsimd.nop().then_inc(y_free, 1)
            with pool.Fori(0, NE) as e:
                pool.wait_ge(ig_ok, e + 1)
                pool.wait_ge(x_tr, e * 4 + 4)
                nc.gpsimd.nop().then_inc(turn, 1)
                gather()
                pool.wait_ge(ic_ok, e + 1)
                pool.wait_ge(ys_ok, e * 4 + 4)
                pool.wait_ge(yp_ok, e + 1)
                nc.gpsimd.nop().then_inc(turn, 1)
                nc.gpsimd.indirect_dma_start(out=res_s, out_offset=bass.IndirectOffsetOnAxis(ap=ic_s[:, 0:1], axis=0),
                                             in_=y_s[:], in_offset=None, compute_op=ALU.add).then_inc(s_out, 16)
                nc.gpsimd.indirect_dma_start(out=res_q, out_offset=bass.IndirectOffsetOnAxis(ap=ic_p[:, 0:1], axis=0),
                                             in_=y_p[:], in_offset=None, compute_op=ALU.add).then_inc(p_out, 16)
                pool.wait_ge(s_out, e * 16 + 16)
                pool.wait_ge(p_out, e * 16 + 16)
                nc.gpsimd.nop().then_inc(y_free, 1)

            pool.wait_ge(f_used, NE * PIECES_E)
            pool.wait_ge(gs_in, 16 * (NE + 1))
            pool.wait_ge(gp_in, 16 * (NE + 1))
            dma(fin[:, 2 * NF], t["norm_final"].partition_broadcast(P)).then_inc(nf_in, 16)
            for i in range(NF):
                dma(fin[:, i], rows(res_s, res_p, i)).then_inc(f_in[i], 16)
            for i in range(TT):
                pool.wait_ge(f_ok, i + 1)
                dma(rows(ys, yp, i), fin[:, NF + i % NF]).then_inc(f_out[i % NF], 16)
                if i + NF < TT:
                    dma(fin[:, i % NF], rows(res_s, res_p, i + NF)).then_inc(f_in[i % NF], 16)
            for z in range(NF):
                pool.wait_ge(f_out[z], 16 * ((TT - z + NF - 1) // NF))


def shape_constants():
    i = np.arange(P)
    mask = np.zeros((2, P, P), np.float32)
    mask[0][i[None, :] < i[:, None]] = NEG
    mask[1][i[None, :] > i[:, None]] = NEG
    grid, nf = 64, HD // 4
    pos = np.arange(NS)
    inv = (np.float32(10000.0) ** (-np.arange(nf, dtype=np.float32) / np.float32(nf))).astype(np.float32)
    ang = np.stack([(pos // grid).astype(np.float32)[:, None] * inv,
                    (pos % grid).astype(np.float32)[:, None] * inv], axis=1).reshape(NS, 2 * nf)
    rope = np.stack([np.tile(np.cos(ang), (1, 4)), np.tile(np.sin(ang), (1, 4))], axis=1).astype(np.float32)
    rcnt = np.zeros((4, NS + NP_), np.float32)
    for gi, w in enumerate(POOLS):
        for base, n in ((0, NS), (NS, NP_)):
            tok = np.arange(n)
            cnt = np.clip(tok + w - w // 2, 0, n) - np.clip(tok - w // 2, 0, n)
            rcnt[gi, base:base + n] = 1.0 / cnt
    sel = np.zeros((5, 2), np.float32)
    sel[[0, 2], 0] = 1.0
    sel[[1, 3], 1] = 1.0
    sel[4] = 1.0
    return {"k_ident": np.eye(P, dtype=np.float32), "k_mask": mask,
            "k_rope": rope.reshape(ST, P, 2, 256), "k_rcnt": rcnt, "k_sel": sel}


_INS = ["x_prompt", "x_sample", "c", "cache_k", "cache_v", "c_ctx", "w_ada", "b_ada", "norm_mix", "w_in",
        "sink_logits", "pool_w", "pool_scale", "w_out", "norm_ffn", "w_router", "w_gate", "w_up", "w_down",
        "norm_final"]
_OUTS = [("y_prompt", (1, NP_, D)), ("y_sample", (1, NS, D)), ("state_k", (1, 1, NP_, NKV, HD)),
         ("state_v", (1, 1, NP_, NKV, HD))]


def kernel(**inputs):
    import concourse.bacc as _bacc
    from concourse.bass_utils import run_bass_kernel_spmd as _run

    nc = _bacc.Bacc("TRN2", target_bir_lowering=False, num_devices=1)
    arrays = {n: np.ascontiguousarray(inputs[n]) for n in _INS}
    arrays["pool_scale"] = np.ascontiguousarray(arrays["pool_scale"].reshape(PW // P, P).T)
    arrays.update(shape_constants())
    t = {n: nc.dram_tensor(n, a.shape, F32, kind="ExternalInput").ap() for n, a in arrays.items()}
    o = {n: nc.dram_tensor(n, s, F32, kind="ExternalOutput").ap() for n, s in _OUTS}
    hybrid_backbone_step(nc, t, o)
    r = _run(nc, [arrays], core_ids=[0])
    return tuple(r.results[0][n] for n, _ in _OUTS)
```
